# Optimizing a Trainium2 kernel written in Bass

```python
import jax, jax.numpy as jnp
from jax import lax
import numpy as np
import math
import jax
import jax.numpy as jnp

D_MODEL = 1024
BATCH = 1
SEQ = 256
DEPTH = 2

POOL_WINDOWS = (2, 4, 8, 16)
POOL_WIDTH = 512
POOL_GROUP = POOL_WIDTH // len(POOL_WINDOWS)
N_HEADS = 8
HEAD_DIM = 64
ATTN_WIDTH = N_HEADS * HEAD_DIM
MOBA_BLOCK = 256
MOBA_TOP_K = 3
Q_CHUNK = 64
ROPE_THETA = 10000.0
N_BRANCH = 2
IN_WIDTH = POOL_WIDTH + 3 * ATTN_WIDTH + N_BRANCH * D_MODEL
D_FF = 2816
EPS = 1e-6
NEG = -1e30


def rms_norm(x, g):
    xf = x.astype(jnp.float32)
    y = xf * lax.rsqrt(jnp.mean(xf * xf, axis=-1, keepdims=True) + EPS)
    return (y * g.astype(jnp.float32)).astype(x.dtype)

def swiglu(h, w_gate_up, w_down):
    a, b = jnp.split(h @ w_gate_up, 2, axis=-1)
    return (jax.nn.silu(a) * b) @ w_down

def rope(x):
    S, Dh = x.shape[1], x.shape[-1]
    half = Dh // 2
    inv_freq = 1.0 / (ROPE_THETA ** (jnp.arange(half, dtype=jnp.float32) * (2.0 / Dh)))
    ang = jnp.arange(S, dtype=jnp.float32)[:, None] * inv_freq[None, :]
    cos = jnp.cos(ang)[None, :, None, :]
    sin = jnp.sin(ang)[None, :, None, :]
    xf = x.astype(jnp.float32)
    x1, x2 = xf[..., :half], xf[..., half:]
    out = jnp.concatenate([x1 * cos - x2 * sin, x2 * cos + x1 * sin], axis=-1)
    return out.astype(x.dtype)

def multiscale_pool(u, w_grp, scale):
    B, S, _ = u.shape
    G = len(POOL_WINDOWS)
    uf = u.astype(jnp.float32).reshape(B, S, G, POOL_GROUP)
    csum = jnp.concatenate([jnp.zeros((B, 1, G, POOL_GROUP), jnp.float32),
                            jnp.cumsum(uf, axis=1)], axis=1)
    t = jnp.arange(S)
    means = []
    for g, w in enumerate(POOL_WINDOWS):
        lo = jnp.maximum(t + 1 - w, 0)
        cnt = (t + 1 - lo).astype(jnp.float32)
        means.append((csum[:, 1:, g] - csum[:, lo, g]) / cnt[None, :, None])
    pooled = jnp.stack(means, axis=2)
    d = (pooled - uf).astype(u.dtype)
    y = jnp.einsum('bsgc,gcd->bsgd', d, w_grp).reshape(B, S, POOL_WIDTH)
    return y * scale

def moba_attention(q, k, v):
    B, S, H, Dh = q.shape
    nb = -(-S // MOBA_BLOCK)
    pad = nb * MOBA_BLOCK - S
    kp = jnp.pad(k, ((0, 0), (0, pad), (0, 0), (0, 0)))
    vp = jnp.pad(v, ((0, 0), (0, pad), (0, 0), (0, 0)))
    kb = kp.reshape(B, nb, MOBA_BLOCK, H, Dh).transpose(0, 3, 1, 2, 4)
    vb = vp.reshape(B, nb, MOBA_BLOCK, H, Dh).transpose(0, 3, 1, 2, 4)
    kbar = jnp.mean(kb.astype(jnp.float32), axis=3)
    nc = S // Q_CHUNK
    qc = q.reshape(B, nc, Q_CHUNK, H, Dh).transpose(1, 0, 3, 2, 4)
    k_eff = min(MOBA_TOP_K, nb)
    scale = Dh ** -0.5
    bi = jnp.arange(B)[:, None, None, None]
    hi = jnp.arange(H)[None, :, None, None]
    blk_ids = jnp.arange(nb)

    def one_chunk(args):
        qi, ci = args
        q0 = ci * Q_CHUNK
        qblk = q0 // MOBA_BLOCK
        qpos = q0 + jnp.arange(Q_CHUNK)
        gate = jnp.einsum('bhqd,bhnd->bhqn', qi.astype(jnp.float32), kbar)
        gate = jnp.where(blk_ids < qblk, gate, NEG)
        _, sel = lax.top_k(gate, k_eff)
        valid = sel < qblk
        ksel = kb[bi, hi, sel]
        vsel = vb[bi, hi, sel]
        kown = lax.dynamic_index_in_dim(kb, qblk, axis=2, keepdims=False)
        vown = lax.dynamic_index_in_dim(vb, qblk, axis=2, keepdims=False)
        s_sel = jnp.einsum('bhqd,bhqknd->bhqkn', qi, ksel).astype(jnp.float32) * scale
        s_sel = jnp.where(valid[..., None], s_sel, NEG).reshape(B, H, Q_CHUNK, k_eff * MOBA_BLOCK)
        kpos = qblk * MOBA_BLOCK + jnp.arange(MOBA_BLOCK)
        s_own = jnp.einsum('bhqd,bhnd->bhqn', qi, kown).astype(jnp.float32) * scale
        s_own = jnp.where(kpos[None, :] <= qpos[:, None], s_own, NEG)
        p = jax.nn.softmax(jnp.concatenate([s_sel, s_own], axis=-1), axis=-1).astype(v.dtype)
        p_sel = p[..., :k_eff * MOBA_BLOCK].reshape(B, H, Q_CHUNK, k_eff, MOBA_BLOCK)
        p_own = p[..., k_eff * MOBA_BLOCK:]
        return (jnp.einsum('bhqkn,bhqknd->bhqd', p_sel, vsel)
                + jnp.einsum('bhqn,bhnd->bhqd', p_own, vown))

    out = lax.map(one_chunk, (qc, jnp.arange(nc)))
    return out.transpose(1, 0, 3, 2, 4).reshape(B, S, H * Dh)

def hybrid_layer(x, ffn1_norm, ffn1_w_gate_up, ffn1_w_down, mix_norm, w_in, b_gate,
                 pool_w, pool_scale, q_norm, k_norm, w_branch_pool, w_branch_attn, w_out,
                 ffn2_norm, ffn2_w_gate_up, ffn2_w_down):
    B, S, D = x.shape
    x = x + 0.5 * swiglu(rms_norm(x, ffn1_norm), ffn1_w_gate_up, ffn1_w_down)
    h = rms_norm(x, mix_norm)
    z = h @ w_in
    o1 = POOL_WIDTH
    o2 = o1 + ATTN_WIDTH
    o3 = o2 + ATTN_WIDTH
    o4 = o3 + ATTN_WIDTH
    u, q, k, v, gl = z[..., :o1], z[..., o1:o2], z[..., o2:o3], z[..., o3:o4], z[..., o4:]
    y_pool = multiscale_pool(u, pool_w, pool_scale)
    q = rope(rms_norm(q.reshape(B, S, N_HEADS, HEAD_DIM), q_norm))
    k = rope(rms_norm(k.reshape(B, S, N_HEADS, HEAD_DIM), k_norm))
    v = v.reshape(B, S, N_HEADS, HEAD_DIM)
    y_attn = moba_attention(q, k, v)
    gates = jax.nn.sigmoid(gl + b_gate).reshape(B, S, N_BRANCH, D)
    merged = gates[:, :, 0] * (y_pool @ w_branch_pool) + gates[:, :, 1] * (y_attn @ w_branch_attn)
    x = x + merged @ w_out
    x = x + 0.5 * swiglu(rms_norm(x, ffn2_norm), ffn2_w_gate_up, ffn2_w_down)
    return x

def first_inputs(seed: int = 0) -> dict:
    key = jax.random.key(seed)
    ks = jax.random.split(key, 18)
    f32 = jnp.float32

    def w(k, shape, fan_in):
        return jax.random.normal(k, shape, f32) * (fan_in ** -0.5)

    def gain(k, shape):
        return 1.0 + 0.1 * jax.random.normal(k, shape, f32)

    L = DEPTH
    return {
        "x": jax.random.normal(ks[0], (BATCH, SEQ, D_MODEL), f32),
        "ffn1_norm": gain(ks[1], (L, D_MODEL)),
        "ffn1_w_gate_up": w(ks[2], (L, D_MODEL, 2 * D_FF), D_MODEL),
        "ffn1_w_down": w(ks[3], (L, D_FF, D_MODEL), D_FF),
        "mix_norm": gain(ks[4], (L, D_MODEL)),
        "w_in": w(ks[5], (L, D_MODEL, IN_WIDTH), D_MODEL),
        "b_gate": 0.1 * jax.random.normal(ks[6], (L, N_BRANCH * D_MODEL), f32),
        "pool_w": w(ks[7], (L, len(POOL_WINDOWS), POOL_GROUP, POOL_GROUP), POOL_GROUP),
        "pool_scale": gain(ks[8], (L, POOL_WIDTH)),
        "q_norm": gain(ks[9], (L, HEAD_DIM)),
        "k_norm": gain(ks[10], (L, HEAD_DIM)),
        "w_branch_pool": w(ks[11], (L, POOL_WIDTH, D_MODEL), POOL_WIDTH),
        "w_branch_attn": w(ks[12], (L, ATTN_WIDTH, D_MODEL), ATTN_WIDTH),
        "w_out": w(ks[13], (L, D_MODEL, D_MODEL), D_MODEL),
        "ffn2_norm": gain(ks[14], (L, D_MODEL)),
        "ffn2_w_gate_up": w(ks[15], (L, D_MODEL, 2 * D_FF), D_MODEL),
        "ffn2_w_down": w(ks[16], (L, D_FF, D_MODEL), D_FF),
    }

def first_block(x, ffn1_norm, ffn1_w_gate_up, ffn1_w_down, mix_norm, w_in, b_gate,
              pool_w, pool_scale, q_norm, k_norm, w_branch_pool, w_branch_attn, w_out,
              ffn2_norm, ffn2_w_gate_up, ffn2_w_down):
    for l in range(DEPTH):
        x = hybrid_layer(x, ffn1_norm[l], ffn1_w_gate_up[l], ffn1_w_down[l], mix_norm[l],
                         w_in[l], b_gate[l], pool_w[l], pool_scale[l], q_norm[l], k_norm[l],
                         w_branch_pool[l], w_branch_attn[l], w_out[l],
                         ffn2_norm[l], ffn2_w_gate_up[l], ffn2_w_down[l])
    return x


GDN_HEADS = 4
GDN_DK = 128
GDN_DV = 128
GDN_CONV = 4
GDN_CHUNK = 64
RET_HEADS = 4
RET_DK = 64
RET_DV = 128
RET_CHUNK = 64
DIL_HEADS = 4
DIL_DH = 128
DIL_PATTERNS = ((128, 1), (512, 4), (2048, 16))
DIFF_HEADS = 4
DIFF_DK = 64
DIFF_DV = 128
Q_BLOCK = 128

GDN_QK_W = GDN_HEADS * GDN_DK
GDN_V_W = GDN_HEADS * GDN_DV
GDN_CONV_W = 2 * GDN_QK_W + GDN_V_W
RET_QK_W = RET_HEADS * RET_DK
RET_V_W = RET_HEADS * RET_DV
IN0_SPLITS = (GDN_CONV_W, GDN_V_W, GDN_HEADS, GDN_HEADS, RET_QK_W, RET_QK_W, RET_V_W, RET_V_W)
IN0_W = sum(IN0_SPLITS)
MIX0_W = GDN_V_W + RET_V_W
DIL_W = DIL_HEADS * DIL_DH
DIFF_QK_W = DIFF_HEADS * 2 * DIFF_DK
DIFF_V_W = DIFF_HEADS * DIFF_DV
IN1_SPLITS = (DIL_W, DIL_W, DIL_W, DIFF_QK_W, DIFF_QK_W, DIFF_V_W)
IN1_W = sum(IN1_SPLITS)
MIX1_W = DIL_W + DIFF_V_W


def rmsnorm(x, w=None):
    xf = x.astype(jnp.float32)
    y = xf * lax.rsqrt(jnp.mean(xf * xf, axis=-1, keepdims=True) + EPS)
    if w is not None:
        y = y * w.astype(jnp.float32)
    return y.astype(x.dtype)

def l2norm(t):
    tf = t.astype(jnp.float32)
    return (tf * lax.rsqrt(jnp.sum(tf * tf, axis=-1, keepdims=True) + EPS)).astype(t.dtype)

def split_cols(t, sizes):
    offs = np.cumsum(sizes)[:-1].tolist()
    return jnp.split(t, offs, axis=-1)

def swiglu_2(h, w_up, w_down):
    gate, up = jnp.split(h @ w_up, 2, axis=-1)
    return (jax.nn.silu(gate) * up) @ w_down

def rope_tables(seq, dim):
    inv = ROPE_THETA ** (-jnp.arange(0, dim, 2, dtype=jnp.float32) / dim)
    ang = jnp.arange(seq, dtype=jnp.float32)[:, None] * inv[None, :]
    return jnp.cos(ang), jnp.sin(ang)

def apply_rope(x, cos, sin):
    x1, x2 = jnp.split(x, 2, axis=-1)
    c = cos[None, :, None, :].astype(x.dtype)
    s = sin[None, :, None, :].astype(x.dtype)
    return jnp.concatenate([x1 * c - x2 * s, x1 * s + x2 * c], axis=-1)

def causal_depthwise_conv(x, w):
    K, C = w.shape
    return lax.conv_general_dilated(x, w[:, None, :].astype(x.dtype), window_strides=(1,),
                                    padding=[(K - 1, 0)], dimension_numbers=('NWC', 'WIO', 'NWC'),
                                    feature_group_count=C)

def to_chunks(t, c):
    B, S = t.shape[:2]
    t = t.reshape(B, S // c, c, *t.shape[2:])
    return jnp.swapaxes(t, 2, 3)

def from_chunks(t):
    t = jnp.swapaxes(t, 2, 3)
    return t.reshape(t.shape[0], t.shape[1] * t.shape[2], *t.shape[3:])

def gated_delta_rule_chunked(q, k, v, g, beta):
    B, S, H, dk = q.shape
    dv = v.shape[-1]
    C = GDN_CHUNK
    f32 = jnp.float32
    qc, kc, vc = (to_chunks(t.astype(f32), C) for t in (q, k, v))
    gc, bc = (to_chunks(t.astype(f32), C) for t in (g, beta))
    gcum = jnp.cumsum(gc, axis=-1)
    idx = jnp.arange(C)
    causal = idx[:, None] >= idx[None, :]
    strict = idx[:, None] > idx[None, :]
    gdiff = gcum[..., :, None] - gcum[..., None, :]
    decay = jnp.where(causal, jnp.exp(jnp.where(causal, gdiff, 0.0)), 0.0)
    a_strict = jnp.where(strict, jnp.einsum('bnhid,bnhjd->bnhij', kc, kc) * decay * bc[..., :, None], 0.0)
    rhs = jnp.concatenate([vc * bc[..., None], kc * (bc * jnp.exp(gcum))[..., None]], axis=-1)
    sol = lax.linalg.triangular_solve(a_strict + jnp.eye(C, dtype=f32), rhs, left_side=True,
                                      lower=True, unit_diagonal=True)
    u, w = sol[..., :dv], sol[..., dv:]
    qk = jnp.einsum('bnhid,bnhjd->bnhij', qc, kc) * decay
    q_dec = qc * jnp.exp(gcum)[..., None]
    g_last = gcum[..., -1]
    k_dec = kc * jnp.exp(g_last[..., None] - gcum)[..., None]

    def step(state, xs):
        qk_n, q_n, w_n, u_n, k_n, gl_n = xs
        v_new = u_n - jnp.einsum('bhcd,bhde->bhce', w_n, state)
        o_n = jnp.einsum('bhcd,bhde->bhce', q_n, state) + jnp.einsum('bhij,bhje->bhie', qk_n, v_new)
        state = state * jnp.exp(gl_n)[..., None, None] + jnp.einsum('bhcd,bhce->bhde', k_n, v_new)
        return state, o_n

    xs = tuple(jnp.moveaxis(t, 1, 0) for t in (qk, q_dec, w, u, k_dec, g_last))
    _, o = lax.scan(step, jnp.zeros((B, H, dk, dv), f32), xs)
    return from_chunks(jnp.moveaxis(o, 0, 1)).astype(v.dtype)

def retention_chunked(q, k, v):
    B, S, H, dk = q.shape
    dv = v.shape[-1]
    C = RET_CHUNK
    f32 = jnp.float32
    log_gamma = jnp.log(1.0 - 2.0 ** (-5.0 - jnp.arange(H, dtype=f32)))
    qc, kc, vc = (to_chunks(t.astype(f32), C) for t in (q, k, v))
    idx = jnp.arange(C, dtype=f32)
    rel = idx[:, None] - idx[None, :]
    causal = rel >= 0
    dmask = jnp.where(causal, jnp.exp(jnp.where(causal, rel, 0.0)[None] * log_gamma[:, None, None]), 0.0)
    intra = jnp.einsum('bnhij,bnhje->bnhie', jnp.einsum('bnhid,bnhjd->bnhij', qc, kc) * dmask, vc)
    k_scale = jnp.exp((C - 1 - idx)[None, :] * log_gamma[:, None])
    q_scale = jnp.exp((idx + 1)[None, :] * log_gamma[:, None])
    chunk_decay = jnp.exp(C * log_gamma)
    kv = jnp.einsum('bnhcd,bnhce->bnhde', kc * k_scale[..., None], vc)

    def step(state, kv_n):
        return state * chunk_decay[:, None, None] + kv_n, state

    _, prev = lax.scan(step, jnp.zeros((B, H, dk, dv), f32), jnp.moveaxis(kv, 1, 0))
    prev = jnp.moveaxis(prev, 0, 1)
    inter = jnp.einsum('bnhcd,bnhde->bnhce', qc, prev) * q_scale[..., None]
    return from_chunks(intra + inter).astype(v.dtype)

def dilated_branch(q, k, v, window, dilation):
    B, S, H, d = q.shape
    L = S // dilation
    n_keys = window // dilation
    blk = min(n_keys, L)
    nb = -(-L // blk)
    Lp = nb * blk

    def strided(t):
        t = t.reshape(B, L, dilation, H, d).swapaxes(1, 2)
        t = jnp.pad(t, ((0, 0), (0, 0), (0, Lp - L), (0, 0), (0, 0)))
        return t.reshape(B, dilation, nb, blk, H, d)

    def with_prev(t):
        prev = jnp.pad(t, ((0, 0), (0, 0), (1, 0), (0, 0), (0, 0), (0, 0)))[:, :, :-1]
        return jnp.concatenate([prev, t], axis=3)

    qs = strided(q)
    kb, vb = with_prev(strided(k)), with_prev(strided(v))
    s = jnp.einsum('brnqhd,brnkhd->brnhqk', qs, kb).astype(jnp.float32)
    qi = jnp.arange(blk)[:, None] + blk
    kj = jnp.arange(2 * blk)[None, :]
    dist = qi - kj
    band = (dist >= 0) & (dist <= n_keys)
    has_prev = (jnp.arange(nb) > 0)[:, None, None] | (kj >= blk)[None]
    valid = band[None] & has_prev
    s = jnp.where(valid[:, None], s, -jnp.inf)
    m = jnp.max(s, axis=-1)
    p = jnp.exp(s - m[..., None])
    l = jnp.sum(p, axis=-1)
    o = jnp.einsum('brnhqk,brnkhd->brnqhd', p.astype(v.dtype), vb).astype(jnp.float32)

    def unstrided(t):
        t = t.reshape(B, dilation, Lp, *t.shape[4:])[:, :, :L]
        return t.swapaxes(1, 2).reshape(B, S, *t.shape[3:])

    return unstrided(o), unstrided(m.swapaxes(3, 4)), unstrided(l.swapaxes(3, 4))

def dilated_attention(q, k, v):
    outs = [dilated_branch(q, k, v, w, r) for (w, r) in DIL_PATTERNS]
    m_all = jnp.max(jnp.stack([o[1] for o in outs]), axis=0)
    num = jnp.zeros_like(outs[0][0])
    den = jnp.zeros_like(outs[0][2])
    for o_g, m_g, l_g in outs:
        scale = jnp.exp(m_g - m_all)
        num = num + o_g * scale[..., None]
        den = den + l_g * scale
    return (num / den[..., None]).astype(v.dtype)

def differential_attention(q1, q2, k1, k2, v, lam):
    B, S, H, dk = q1.shape
    nq = S // Q_BLOCK

    def blocks(t):
        return jnp.moveaxis(t.reshape(B, nq, Q_BLOCK, H, t.shape[-1]), 1, 0)

    key_pos = jnp.arange(S)

    def one_block(args):
        i, qa, qb = args
        q_pos = i * Q_BLOCK + jnp.arange(Q_BLOCK)
        causal = (q_pos[:, None] >= key_pos[None, :])[None, None]
        s1 = jnp.where(causal, jnp.einsum('bqhd,bkhd->bhqk', qa, k1).astype(jnp.float32), -jnp.inf)
        s2 = jnp.where(causal, jnp.einsum('bqhd,bkhd->bhqk', qb, k2).astype(jnp.float32), -jnp.inf)
        attn = jax.nn.softmax(s1, axis=-1) - lam * jax.nn.softmax(s2, axis=-1)
        return jnp.einsum('bhqk,bkhe->bqhe', attn.astype(v.dtype), v)

    o = lax.map(one_block, (jnp.arange(nq), blocks(q1), blocks(q2)))
    return jnp.moveaxis(o, 0, 1).reshape(B, S, H, v.shape[-1])

def mixer_delta_retention(h, w_in, conv_w, a_log, dt_bias, gdn_norm, w_out, cos, sin):
    B, S, _ = h.shape
    qkv, z, b, a, rq, rk, rv, rg = split_cols(h @ w_in, IN0_SPLITS)
    qkv = jax.nn.silu(causal_depthwise_conv(qkv, conv_w))
    q, k, v = split_cols(qkv, (GDN_QK_W, GDN_QK_W, GDN_V_W))
    q = l2norm(q.reshape(B, S, GDN_HEADS, GDN_DK)) * GDN_DK ** -0.5
    k = l2norm(k.reshape(B, S, GDN_HEADS, GDN_DK))
    v = v.reshape(B, S, GDN_HEADS, GDN_DV)
    beta = jax.nn.sigmoid(b)
    g = -jnp.exp(a_log) * jax.nn.softplus(a + dt_bias)
    o_a = gated_delta_rule_chunked(q, k, v, g, beta)
    o_a = rmsnorm(o_a, gdn_norm) * jax.nn.silu(z.reshape(B, S, GDN_HEADS, GDN_DV))
    rq = apply_rope(rq.reshape(B, S, RET_HEADS, RET_DK), cos, sin) * RET_DK ** -0.5
    rk = apply_rope(rk.reshape(B, S, RET_HEADS, RET_DK), cos, sin)
    o_b = retention_chunked(rq, rk, rv.reshape(B, S, RET_HEADS, RET_DV))
    o_b = rmsnorm(o_b) * jax.nn.silu(rg.reshape(B, S, RET_HEADS, RET_DV))
    o = jnp.concatenate([o_a.reshape(B, S, GDN_V_W), o_b.reshape(B, S, RET_V_W)], axis=-1)
    return o @ w_out

def mixer_dilated_differential(h, w_in, lambda_q1, lambda_k1, lambda_q2, lambda_k2, diff_norm, w_out,
                               cos128, sin128, cos64, sin64, lambda_init):
    B, S, _ = h.shape
    cq, ck, cv, dq, dk, dv = split_cols(h @ w_in, IN1_SPLITS)
    cq = apply_rope(cq.reshape(B, S, DIL_HEADS, DIL_DH), cos128, sin128) * DIL_DH ** -0.5
    ck = apply_rope(ck.reshape(B, S, DIL_HEADS, DIL_DH), cos128, sin128)
    o_c = dilated_attention(cq, ck, cv.reshape(B, S, DIL_HEADS, DIL_DH))
    dq = dq.reshape(B, S, DIFF_HEADS, 2, DIFF_DK)
    dk = dk.reshape(B, S, DIFF_HEADS, 2, DIFF_DK)
    q1 = apply_rope(dq[..., 0, :], cos64, sin64) * DIFF_DK ** -0.5
    q2 = apply_rope(dq[..., 1, :], cos64, sin64) * DIFF_DK ** -0.5
    k1 = apply_rope(dk[..., 0, :], cos64, sin64)
    k2 = apply_rope(dk[..., 1, :], cos64, sin64)
    lam = (jnp.exp(jnp.sum(lambda_q1 * lambda_k1).astype(jnp.float32))
           - jnp.exp(jnp.sum(lambda_q2 * lambda_k2).astype(jnp.float32)) + lambda_init)
    o_d = differential_attention(q1, q2, k1, k2, dv.reshape(B, S, DIFF_HEADS, DIFF_DV), lam)
    o_d = rmsnorm(o_d, diff_norm) * (1.0 - lambda_init)
    o = jnp.concatenate([o_c.reshape(B, S, DIL_W), o_d.reshape(B, S, DIFF_V_W)], axis=-1)
    return o @ w_out

def second_inputs(seed: int = 0) -> dict:
    key = jax.random.key(seed)
    ks = iter(jax.random.split(key, 64))

    def nrm(shape, scale):
        return jax.random.normal(next(ks), shape, jnp.float32) * scale

    def gain(n):
        return 1.0 + 0.02 * jax.random.normal(next(ks), (n,), jnp.float32)

    inp = {}
    inp['x'] = nrm((BATCH, SEQ, D_MODEL), 1.0)

    def ffn(prefix):
        inp[prefix + '_norm'] = gain(D_MODEL)
        inp[prefix + '_w_up'] = nrm((D_MODEL, 2 * D_FF), D_MODEL ** -0.5)
        inp[prefix + '_w_down'] = nrm((D_FF, D_MODEL), D_FF ** -0.5)

    ffn('l0_ffn1')
    inp['l0_mix_norm'] = gain(D_MODEL)
    inp['l0_w_in'] = nrm((D_MODEL, IN0_W), D_MODEL ** -0.5)
    inp['l0_conv_w'] = nrm((GDN_CONV, GDN_CONV_W), GDN_CONV ** -0.5)
    inp['l0_a_log'] = jnp.log(jax.random.uniform(next(ks), (GDN_HEADS,), jnp.float32, 1.0, 16.0))
    dt = jnp.exp(jax.random.uniform(next(ks), (GDN_HEADS,), jnp.float32, math.log(1e-3), math.log(1e-1)))
    inp['l0_dt_bias'] = dt + jnp.log(-jnp.expm1(-dt))
    inp['l0_gdn_norm'] = gain(GDN_DV)
    inp['l0_w_out'] = nrm((MIX0_W, D_MODEL), MIX0_W ** -0.5)
    ffn('l0_ffn2')
    ffn('l1_ffn1')
    inp['l1_mix_norm'] = gain(D_MODEL)
    inp['l1_w_in'] = nrm((D_MODEL, IN1_W), D_MODEL ** -0.5)
    inp['l1_lambda_q1'] = nrm((DIFF_DK,), 0.1)
    inp['l1_lambda_k1'] = nrm((DIFF_DK,), 0.1)
    inp['l1_lambda_q2'] = nrm((DIFF_DK,), 0.1)
    inp['l1_lambda_k2'] = nrm((DIFF_DK,), 0.1)
    inp['l1_diff_norm'] = gain(DIFF_DV)
    inp['l1_w_out'] = nrm((MIX1_W, D_MODEL), MIX1_W ** -0.5)
    ffn('l1_ffn2')
    inp['final_norm'] = gain(D_MODEL)
    return inp

def second_block(x, l0_ffn1_norm, l0_ffn1_w_up, l0_ffn1_w_down, l0_mix_norm, l0_w_in, l0_conv_w, l0_a_log,
              l0_dt_bias, l0_gdn_norm, l0_w_out, l0_ffn2_norm, l0_ffn2_w_up, l0_ffn2_w_down,
              l1_ffn1_norm, l1_ffn1_w_up, l1_ffn1_w_down, l1_mix_norm, l1_w_in, l1_lambda_q1, l1_lambda_k1,
              l1_lambda_q2, l1_lambda_k2, l1_diff_norm, l1_w_out, l1_ffn2_norm, l1_ffn2_w_up, l1_ffn2_w_down,
              final_norm):
    S = x.shape[1]
    cos64, sin64 = rope_tables(S, 64)
    cos128, sin128 = rope_tables(S, 128)
    ffn1 = ((l0_ffn1_norm, l0_ffn1_w_up, l0_ffn1_w_down), (l1_ffn1_norm, l1_ffn1_w_up, l1_ffn1_w_down))
    ffn2 = ((l0_ffn2_norm, l0_ffn2_w_up, l0_ffn2_w_down), (l1_ffn2_norm, l1_ffn2_w_up, l1_ffn2_w_down))
    mix_norm = (l0_mix_norm, l1_mix_norm)
    for i in range(DEPTH):
        n1, wu1, wd1 = ffn1[i]
        x = x + 0.5 * swiglu_2(rmsnorm(x, n1), wu1, wd1)
        h = rmsnorm(x, mix_norm[i])
        if i % 2 == 0:
            mix = mixer_delta_retention(h, l0_w_in, l0_conv_w, l0_a_log, l0_dt_bias, l0_gdn_norm, l0_w_out,
                                        cos64, sin64)
        else:
            lambda_init = 0.8 - 0.6 * math.exp(-0.3 * i)
            mix = mixer_dilated_differential(h, l1_w_in, l1_lambda_q1, l1_lambda_k1, l1_lambda_q2, l1_lambda_k2,
                                             l1_diff_norm, l1_w_out, cos128, sin128, cos64, sin64, lambda_init)
        x = x + mix
        n2, wu2, wd2 = ffn2[i]
        x = x + 0.5 * swiglu_2(rmsnorm(x, n2), wu2, wd2)
    return rmsnorm(x, final_norm)


def setup_inputs(seed=0):
    out = dict(first_inputs(seed))
    for name, value in second_inputs(seed + 1).items():
        if name != "x":
            out[name + "_2"] = value
    return out


def reference(
    x, ffn1_norm, ffn1_w_gate_up, ffn1_w_down, mix_norm, w_in, b_gate, pool_w, pool_scale,
    q_norm, k_norm, w_branch_pool, w_branch_attn, w_out, ffn2_norm, ffn2_w_gate_up, ffn2_w_down,
    l0_ffn1_norm_2, l0_ffn1_w_up_2, l0_ffn1_w_down_2, l0_mix_norm_2, l0_w_in_2, l0_conv_w_2,
    l0_a_log_2, l0_dt_bias_2, l0_gdn_norm_2, l0_w_out_2, l0_ffn2_norm_2, l0_ffn2_w_up_2,
    l0_ffn2_w_down_2, l1_ffn1_norm_2, l1_ffn1_w_up_2, l1_ffn1_w_down_2, l1_mix_norm_2,
    l1_w_in_2, l1_lambda_q1_2, l1_lambda_k1_2, l1_lambda_q2_2, l1_lambda_k2_2, l1_diff_norm_2,
    l1_w_out_2, l1_ffn2_norm_2, l1_ffn2_w_up_2, l1_ffn2_w_down_2, final_norm_2,
):
    x = first_block(
        x, ffn1_norm, ffn1_w_gate_up, ffn1_w_down, mix_norm, w_in, b_gate, pool_w, pool_scale,
        q_norm, k_norm, w_branch_pool, w_branch_attn, w_out, ffn2_norm, ffn2_w_gate_up,
        ffn2_w_down,
    )
    return second_block(
        x, l0_ffn1_norm_2, l0_ffn1_w_up_2, l0_ffn1_w_down_2, l0_mix_norm_2, l0_w_in_2,
        l0_conv_w_2, l0_a_log_2, l0_dt_bias_2, l0_gdn_norm_2, l0_w_out_2, l0_ffn2_norm_2,
        l0_ffn2_w_up_2, l0_ffn2_w_down_2, l1_ffn1_norm_2, l1_ffn1_w_up_2, l1_ffn1_w_down_2,
        l1_mix_norm_2, l1_w_in_2, l1_lambda_q1_2, l1_lambda_k1_2, l1_lambda_q2_2,
        l1_lambda_k2_2, l1_diff_norm_2, l1_w_out_2, l1_ffn2_norm_2, l1_ffn2_w_up_2,
        l1_ffn2_w_down_2, final_norm_2,
    )


_drawn_inputs = setup_inputs


def setup_inputs(seed=0):
    import zlib

    import numpy as np

    out = dict(_drawn_inputs(seed))
    spreads = {}
    factors = {'q_norm': 3.072,
     'k_norm': 2.902,
     'l0_ffn1_norm_2': 6.898,
     'l0_mix_norm_2': 3.474,
     'l0_gdn_norm_2': 8.0,
     'l0_ffn2_norm_2': 8.0,
     'l1_ffn1_norm_2': 8.0,
     'l1_mix_norm_2': 15.443,
     'l1_lambda_q1_2': 3.592,
     'l1_lambda_k1_2': 7.087,
     'l1_lambda_k2_2': 8.0,
     'l1_diff_norm_2': 200.0,
     'l1_ffn2_norm_2': 31.612,
     'final_norm_2': 24.286}
    for name, (base, spread) in spreads.items():
        noise = np.random.default_rng([zlib.crc32(name.encode()), seed]).standard_normal(out[name].shape)
        drawn = base * np.exp(spread * noise) if base else spread * noise
        out[name] = jnp.asarray(drawn.astype(out[name].dtype))
    for name, factor in factors.items():
        out[name] = (out[name] * factor).astype(out[name].dtype)
    return out
```

```python
from contextlib import ExitStack
import math

import concourse.bass as bass
from concourse import mybir

F32 = mybir.dt.float32
F32R = mybir.dt.float32r
ALU = mybir.AluOpType
ACT = mybir.ActivationFunctionType
AX_X = mybir.AxisListType.X

P = 128
SEQ = 256
TT = SEQ // P
D = 1024
KT = D // P
DFF = 2816
LAMBDA_INIT = 0.8 - 0.6 * math.exp(-0.3)
DIL_SCALE = 128 ** -0.5
MIX_FLOATS = 20960
CH = 256
NCH = DFF // CH
EPS = 1e-6
NEG = -1e30
PIECE = 2048
SLOTS = 3

def starts(program, per_phase):
    out = [0]
    for kind in program:
        out.append(out[-1] + per_phase[kind])
    return out


N_PARAMS = {"ffn": 0, "pool_attn": 8, "delta_ret": 14, "dil_diff": 6}
ROPES = {"ffn": 0, "pool_attn": 2, "delta_ret": 1, "dil_diff": 4}
QK_TURNS = {"ffn": 0, "pool_attn": 2, "delta_ret": 0, "dil_diff": 4}
O_TURNS = {"ffn": 0, "pool_attn": 1, "delta_ret": 2, "dil_diff": 2}
BT_SPLITS = {"ffn": 0, "pool_attn": 2, "delta_ret": 2, "dil_diff": 2}
TURNS = {"ffn": 1, "pool_attn": 2, "delta_ret": 1, "dil_diff": 1}
PRODUCTS = {"ffn": 1, "pool_attn": 3, "delta_ret": 1, "dil_diff": 1}
CHUNKS = {"ffn": 0, "pool_attn": 8, "delta_ret": 4, "dil_diff": 6}
ACT_EVACS = {"ffn": 0, "pool_attn": 8, "delta_ret": 8, "dil_diff": 12}
MAPS = {"ffn": 0, "pool_attn": 8, "delta_ret": 0, "dil_diff": 12}
ROUNDS = {"ffn": 0, "pool_attn": 2, "delta_ret": 0, "dil_diff": 6}
HEAD_NORMS = {"ffn": 0, "pool_attn": 2, "delta_ret": 4, "dil_diff": 1}
PROGRAM = ["ffn", "pool_attn", "ffn"] * 2 + ["ffn", "delta_ret", "ffn", "ffn", "dil_diff", "ffn"]
USE = None
PIECES = {"ffn": 3 * NCH, "pool_attn": 24, "delta_ret": 18, "dil_diff": 16}


def build(nc, program, t):
    n_pieces = sum(PIECES[kind] for kind in program)
    first_piece = starts(program, PIECES)
    turn0 = starts(program, TURNS)
    out0 = starts(program, PRODUCTS)
    chunk0 = starts(program, CHUNKS)
    evac0 = starts(program, ACT_EVACS)
    map0 = starts(program, MAPS)
    round0 = starts(program, ROUNDS)
    head_norm0 = starts(program, HEAD_NORMS)
    rope0 = starts(program, ROPES)
    turned0 = starts(program, QK_TURNS)
    o_turn0 = starts(program, O_TURNS)
    bt0 = starts(program, BT_SPLITS)

    with ExitStack() as ctx:
        def sb(name, shape, dt=F32):
            return ctx.enter_context(nc.sbuf_tensor(name, shape, dt))

        def sem(name):
            return ctx.enter_context(nc.semaphore(name))

        bank = [ctx.enter_context(nc.psum_tensor(f"bank{i}", [P, 512], F32)) for i in range(8)]

        w_raw = [sb(f"w_raw{s}", [P, PIECE]) for s in range(SLOTS)]
        w_hi = [sb(f"w_hi{s}", [P, PIECE], F32R) for s in range(SLOTS)]
        w_lo = [sb(f"w_lo{s}", [P, PIECE], F32R) for s in range(SLOTS)]
        x = sb("x", [P, TT, D])
        xn = sb("xn", [P, TT, D])
        gain = sb("gain", [P, D])
        ident = sb("ident", [P, P])
        minus_half = sb("minus_half", [P, 16])
        stat = sb("stat", [P, 3, TT])
        xt_hi = sb("xt_hi", [P, KT, SEQ], F32R)
        xt_lo = sb("xt_lo", [P, KT, SEQ], F32R)
        gate = sb("gate", [P, TT, CH])
        hid = sb("hid", [P, TT, CH])
        ht_hi = sb("ht_hi", [P, 2, SEQ], F32R)
        ht_lo = sb("ht_lo", [P, 2, SEQ], F32R)

        bt_hi = sb("bt_hi", [P, 4, SEQ], F32R)
        bt_lo = sb("bt_lo", [P, 4, SEQ], F32R)
        mix = sb("mix", [P, MIX_FLOATS])
        expsum = sb("expsum", [P, 2, TT, 8])
        negmax = sb("negmax", [P, 2, TT])
        hstat = sb("hstat", [P, 3, 16])

        def carve(sizes):
            parts, at = {}, 0
            for name, size in sizes.items():
                parts[name] = mix[:, at:at + size]
                at += size
            assert at <= MIX_FLOATS, at
            return parts

        landed = [sem(f"weights_landed{s}") for s in range(SLOTS)]
        hi_done = sem("hi_done")
        lo_done = sem("lo_done")
        used = sem("piece_used")
        x_in = sem("x_in")
        id_in = sem("ident_in")
        gain_in = sem("gain_in")
        x_ready = sem("x_ready")
        ss_done = sem("squares_summed")
        xn_ready = sem("xn_ready")
        xt_done = sem("xt_transposed")
        xt_hi_done = sem("xt_hi_done")
        xt_lo_done = sem("xt_lo_done")
        up_done = sem("up_done")
        gate_ready = sem("gate_ready")
        hid_ready = sem("hid_ready")
        ht_done = sem("ht_transposed")
        ht_hi_done = sem("ht_hi_done")
        ht_lo_done = sem("ht_lo_done")
        out_done = sem("out_product_done")
        dve_step = sem("dve_step")
        stored = sem("stored")
        params_in = sem("mixer_params_in")
        proj_done = sem("chunk_tile0_done")
        act_evac = sem("chunk_tile_taken_by_act")
        gate_added = sem("gate_bias_added")
        hsq_done = sem("head_squares_done")
        hmean_ready = sem("head_mean_ready")
        hrstd_ready = sem("head_rstd_ready")
        diff_done = sem("pool_difference_done")
        diff_ready = sem("pool_difference_ready")
        y_done = sem("pool_product_done")
        bt_hi_done = sem("bt_hi_done")
        bt_lo_done = sem("bt_lo_done")
        qk_ready = sem("qk_roped")
        qkt_done = sem("qk_transposed")
        qkt_ready = sem("qk_transpose_ready")
        s_done = sem("scores_done")
        s_masked = sem("scores_masked")
        max_ready = sem("max_ready")
        exp_done = sem("exp_done")
        pt_done = sem("probs_transposed")
        pt_ready = sem("probs_transpose_ready")
        pv_done = sem("pv_done")
        o_ready = sem("attention_round_ready")
        ot_done = sem("attention_transposed")
        gates_ready = sem("gates_ready")
        branch_ready = sem("branch_gated")
        M = {name: sem("m_" + name) for name in (
            "ba_hi", "ba_split", "ba_done", "abs_ready", "exps_ready", "softplus_ready", "g_ready", "ug_ready", "sums_done",
            "gcum_copied", "e4_ready", "diff_done", "diff_ready", "decay_ready", "pads_zero", "ct_ready", "conv_ready",
            "co_ready", "co_turned", "tm_ready", "normed", "kb_ready", "kt_turned", "kt_ready", "kbt_turned", "kbt_ready",
            "qt_turned", "qt_ready", "qd_ready", "qdt_turned", "qdt_ready", "at_done", "at_ready", "qk_done", "qk_masked",
            "xt0_ready", "x0_turned", "x0_ready", "level_masked", "t1_done", "t1_ready", "y_done", "x_updated",
            "vb_ready", "kbe_ready", "kd_ready", "u_done", "u_ready", "wt_done", "wt_ready", "rqk_turned", "rqk_ready",
            "rs_done", "rs_ready", "ro_done", "ro_ready", "oa_ready", "sq_ready", "half_normed", "vw_done", "vn_ready",
            "ds_done", "s_ready", "o_done", "gz_ready")}
        ba_hi = sb("ba_hi", [P, KT * 8], F32R)
        ba_lo = sb("ba_lo", [P, KT * 8], F32R)
        lam_sums = sem("lambda_sums")
        lam_exp = sem("lambda_exponentials")
        diff_squared = sem("diff_ready_to_square")
        diff_normed = sem("diff_normed")
        mean_ready = sem("mean_square_ready")
        rstd_ready = sem("rstd_ready")
        half_ready = sem("minus_half_ready")

        block = ctx.enter_context(nc.Block())
        norms = len(program) + 1

        def params_at(k):
            return 16 * sum(N_PARAMS[kind] for kind in program[:k + 1])

        last = len(program) - 1

        def up_view(w, k):
            return w[:, k * 512:(k + 1) * 512]

        def down_view(w, k, h):
            return w[:, k * 1024 + h * 512:k * 1024 + (h + 1) * 512]

        def retention_probs(h):
            buf = G["qt_pr"] if h < 2 else G["decay_oa"]
            return buf[:, (h % 2) * 384:(h % 2) * 384 + 384]

        def psum3(b, k):
            return bank[b][:, :].rearrange("p (k q) -> p k q", k=k)

        A = carve(dict(probs=768, probs_t=768, u=1024, q=1024, k=1024, v=1024, sq=1024, rot=1024, qt=1024,
                       kt=1024, gates=4096, pool_w=512, pool_scale=4, qk_norm=128, pool_mean=1536,
                       mask=384, rope=256, rope_g=512))
        B = carve(dict(probs=768, probs_t=768, cq=1024, ck=1024, cv=1024, dq=1024, dk=1024, dv=1024, rot=1024,
                       cqt=1024, ckt=1024, dqt=1024, dkt=1024, diff=1024, sq=1024, prod=256,
                       mask=384, mask_dil=384, rope=256, rope_wide=512, lambdas=256, diff_norm=128, lam=8))
        B_PARAMS = ("mask", "mask_dil", "rope", "rope_wide", "lambdas", "diff_norm")
        G = carve(dict(ct_co=4120, k_kd=1024, q_qd_u=1024, v_vb=1024, kb_kbe=1024, gz=1024, rqk_ob=1024, rv=1024,
                       rg=1024, decay_oa=1024, kt_rt=1024, qt_pr=1024, kbt_wt=1024, qdt=1024,
                       ones=128, before=128, after=128, sub=256, below=128, level=768, ret=1024, rope=256,
                       gdn_norm=128, conv=48, alog_dt=8, ba=64, ab=64, gates=64, e4=32, gc=8))
        G_PARAMS = ("ones", "before", "after", "sub", "below", "level", "ret", "rope", "gdn_norm", "conv", "alog_dt", "ba")
        ct = [G["ct_co"][:, i * 1036:(i + 1) * 1036].rearrange("p (c q) -> p c q", c=4) for i in range(2)]
        co = [G["ct_co"][:, 2072 + i * 1024:2072 + (i + 1) * 1024].rearrange("p (c q) -> p c q", c=4) for i in range(2)]
        mats = lambda v: v.rearrange("p (t h q) -> p t h q", t=TT, h=4)
        inv, inv_t, prod1, lev = (mats(G["ct_co"][:, i * 1024:(i + 1) * 1024]) for i in range(4))
        at_m = mats(xn[:, 0, :])
        qk_m = mats(xn[:, 1, :])
        state = gate[:, :, :].rearrange("p t c -> p (t c)").rearrange("p (h e) -> p h e", h=4)
        v_new = hid[:, :, :].rearrange("p t c -> p (t c)").rearrange("p (h e) -> p h e", h=4)
        A_PARAMS = ("pool_w", "pool_scale", "qk_norm", "pool_mean", "mask", "rope")
        tok = lambda v, d=512: v.rearrange("p (t d) -> p t d", t=TT)
        heads = lambda v, w=64: v.rearrange("p (t h d) -> p t h d", t=TT, d=w)

        def causal_map(g, q_t, k_t, off, width):
            return [(q_t[off:off + width, 0:P], k_t[off:off + width, 0:P]),
                    (q_t[off:off + width, P:SEQ], k_t[off:off + width, 0:SEQ])]

        @block.sync
        def _(sp):
            sp.dma_start(x[:, :, :], t["x"].rearrange("(t p) d -> p t d", p=P)).then_inc(x_in, 16)
            for s in range(SLOTS):
                sp.dma_start(w_raw[s][:, :], t["weights"][s]).then_inc(landed[s], 16)
            rounds = n_pieces // SLOTS
            with sp.Fori(1, rounds) as i:
                for s in range(SLOTS):
                    sp.wait_ge(lo_done, i * SLOTS + (s + 1 - SLOTS))
                    sp.dma_start(w_raw[s][:, :], t["weights"][i * SLOTS + s]).then_inc(landed[s], 16)
            for m in range(rounds * SLOTS, n_pieces):
                s = m % SLOTS
                sp.wait_ge(lo_done, m + 1 - SLOTS)
                sp.dma_start(w_raw[s][:, :], t["weights"][m]).then_inc(landed[s], 16)
            for tt in range(TT):
                sp.wait_ge(xn_ready, TT * turn0[-1] + tt + 1)
                sp.dma_start(t["out"][tt * P:(tt + 1) * P, :], xn[:, tt, :]).then_inc(stored, 16)
            sp.wait_ge(stored, 16 * TT)

        @block.gpsimd
        def _(pool):
            def rstd(k, tt):
                pool.wait_ge(mean_ready, TT * k + tt + 1)
                nc.gpsimd.tensor_tensor(stat[:, 2, tt:tt + 1], stat[:, 1, tt:tt + 1], minus_half[:, 0:1], ALU.pow).then_inc(rstd_ready, 1)

            pool.dma_start(ident[:, :], t["ident"]).then_inc(id_in, 16)
            pool.memset(minus_half[:, :], -0.5).then_inc(half_ready, 1)
            pool.wait_ge(half_ready, 1)
            def load_gain(k):
                if k < norms:
                    if k:
                        pool.wait_ge(xn_ready, TT * (turn0[k - 1] + 1))
                    pool.dma_start(gain[:, :], t["gains"][k:k + 1, :].to_broadcast([P, D])).then_inc(gain_in, 16)

            def head_rstd(i, n):
                pool.wait_ge(hmean_ready, i + 1)
                nc.gpsimd.tensor_tensor(hstat[:, 2, 0:n], hstat[:, 1, 0:n], minus_half[:, 0:n], ALU.pow).then_inc(hrstd_ready, 1)

            def load_pool_attn(i):
                for name in A_PARAMS:
                    src = t["a_" + name][i] if name in ("pool_w", "pool_scale", "qk_norm") else t["a_" + name]
                    pool.dma_start(A[name], src.to_broadcast([P, 128]) if name == "qk_norm" else src).then_inc(params_in, 16)
                for tt in range(TT):
                    pool.dma_start(tok(A["gates"])[:, tt, :], t["a_b_gate"][i].to_broadcast([P, 2048])).then_inc(params_in, 16)

            def load_dil_diff():
                for name in B_PARAMS:
                    src = t["b_" + name]
                    pool.dma_start(B[name], src.to_broadcast([P, src.shape[1]]) if src.shape[0] == 1 else src).then_inc(params_in, 16)

            def load_delta_ret():
                for name in G_PARAMS:
                    src = t["g_" + name]
                    pool.dma_start(G[name], src.to_broadcast([P, src.shape[1]]) if src.shape[0] == 1 else src).then_inc(params_in, 16)
                for _ in range(2):
                    pool.dma_start(ct[_][:, :, 0:3], t["g_zeros"].rearrange("p (c q) -> p c q", c=4)).then_inc(params_in, 16)

            def delta_ret(k):
                h0 = head_norm0[k]
                head_rstd(h0, 8)
                head_rstd(h0 + 1, 8)
                for l in range(1, 6):
                    if l == 1:
                        pool.wait_ge(M["x0_ready"], 1)
                    else:
                        pool.wait_ge(M["t1_done"], TT * (l - 1))
                    m = G["level"][:, l * P:(l + 1) * P].unsqueeze(1).broadcast_to([P, 8, P])
                    nc.gpsimd.tensor_tensor(lev.rearrange("p t h q -> p (t h) q"), at_m.rearrange("p t h q -> p (t h) q"),
                                            m, ALU.mult).then_inc(M["level_masked"], 1)
                head_rstd(h0 + 2, 8)
                head_rstd(h0 + 3, 8)

            load_gain(0)
            seen = {"pool_attn": 0, "delta_ret": 0, "dil_diff": 0}

            def load_params(k):
                kind = program[k] if k < len(program) else "ffn"
                if kind == "pool_attn":
                    load_pool_attn(seen[kind])
                if kind == "dil_diff":
                    load_dil_diff()
                if kind == "delta_ret":
                    load_delta_ret()
                if kind != "ffn":
                    seen[kind] += 1

            load_params(0)
            for k in range(norms):
                for tt in range(TT):
                    rstd(k, tt)
                if k == len(program):
                    break
                load_gain(k + 1)
                if program[k] == "ffn":
                    load_params(k + 1)
                if program[k] == "pool_attn":
                    head_rstd(head_norm0[k], 16)
                    head_rstd(head_norm0[k] + 1, 16)
                if program[k] == "dil_diff":
                    head_rstd(head_norm0[k], 8)
                if program[k] == "delta_ret":
                    delta_ret(k)

        @block.scalar
        def _(act):
            def split_hi(m, s, skip=False):
                act.wait_ge(landed[s], landed_count(m, s))
                if not skip:
                    act.wait_ge(used, m + (1 - SLOTS))
                nc.scalar.activation(w_hi[s][:, :], w_raw[s][:, :], ACT.Copy).then_inc(hi_done, 1)

            def landed_count(m, s):
                return 16 * (m // SLOTS + 1)

            def norm(k):
                for tt in range(TT):
                    act.wait_ge(x_ready, TT * (k - 1) + tt + 1) if k else act.wait_ge(x_in, 16)
                    nc.scalar.activation(xn[:, tt, :], x[:, tt, :], ACT.Square,
                                         accum_out=stat[:, 0, tt:tt + 1]).then_inc(ss_done, 1)

            def xt_high(k):
                for tt in range(TT):
                    for g in range(2):
                        b = 4 + 2 * tt + g
                        act.wait_ge(xt_done, 4 * k + 2 * tt + g + 1)
                        nc.scalar.activation(xt_hi[:, 4 * g:4 * g + 4, tt * P:(tt + 1) * P],
                                             bank[b][:, :].rearrange("p (k q) -> p k q", k=4),
                                             ACT.Copy).then_inc(xt_hi_done, 1)

            def ffn(f, n0):
                base = n0

                def hi(m, s):
                    split_hi(m, s)

                def gates(c):
                    for tt in range(TT):
                        if tt == 0:
                            act.wait_ge(up_done, c + (NCH * f + 1))
                        else:
                            act.wait_ge(used, base + 2 if isinstance(c, int) and c == 0 else c * SLOTS + (base + 1))
                        nc.scalar.activation(gate[:, tt, :], bank[4 + tt][:, 0:CH], ACT.Silu).then_inc(gate_ready, 1)

                def ht_high(c):
                    act.wait_ge(ht_done, c + (NCH * f + 1))
                    nc.scalar.activation(ht_hi[:, :, :], bank[6][:, :].rearrange("p (k q) -> p k q", k=2),
                                         ACT.Copy).then_inc(ht_hi_done, 1)

                def step(c, peeled=True):
                    m = base + 2 - SLOTS + c * SLOTS
                    ht_high(c - 1)
                    ahead(m, 2, c)
                    ahead(m, 3, c)
                    gates(c)
                    ahead(m, 4, c)

                def ahead(m, j, c):
                    s = (base + 2 + j) % SLOTS
                    if isinstance(c, int):
                        if m + j < n_pieces:
                            split_hi(m + j, s)
                        return
                    q = (base - 1 + j) // SLOTS
                    act.wait_ge(landed[s], c * 16 + 16 * (q + 1))
                    act.wait_ge(used, c * SLOTS + (base - 1 + j + 1 - SLOTS))
                    nc.scalar.activation(w_hi[s][:, :], w_raw[s][:, :], ACT.Copy).then_inc(hi_done, 1)

                split_hi(base + 2, (base + 2) % SLOTS, base + 2 < SLOTS)
                gates(0)
                split_hi(base + 3, (base + 3) % SLOTS)
                step(1)
                with act.Fori(2, NCH - 1) as c:
                    step(c)
                step(NCH - 1)
                ht_high(NCH - 1)
                if base + 34 < n_pieces:
                    split_hi(base + 34, (base + 34) % SLOTS)

            def ahead(m):
                if m + 2 < n_pieces:
                    split_hi(m + 2, (m + 2) % SLOTS, m + 2 < SLOTS)

            def chunk_tile(k, j, tt, skipped):
                if tt == 0:
                    act.wait_ge(proj_done, chunk0[k] + j + 1 - skipped)
                else:
                    act.wait_ge(used, first_piece[k] + 2 * j + 2)

            def take(k, j, e, dst, func=ACT.Copy, skipped=0):
                for tt in range(TT):
                    chunk_tile(k, j, tt, skipped)
                    nc.scalar.activation(dst[:, tt, :], bank[2 * (j % 2) + tt][:, :], func).then_inc(act_evac, 1)

            def exp_map(g, i):
                act.wait_ge(max_ready, g + 1)
                pr = A["probs"][:, (g % 2) * 384:(g % 2) * 384 + 384]
                for tt, cols in enumerate((slice(0, P), slice(P, 3 * P))):
                    ins = nc.scalar.activation(pr[:, cols], pr[:, cols], ACT.Exp, bias=negmax[:, g % 2, tt:tt + 1],
                                               accum_out=expsum[:, 0, tt, i:i + 1])
                ins.then_inc(exp_done, 1)

            def take_probs(g):
                act.wait_ge(pt_done, g + 1)
                if g >= 2:
                    act.wait_ge(pv_done, g - 1)
                nc.scalar.activation(A["probs_t"][:, (g % 2) * 384:(g % 2) * 384 + 384], bank[6][:, 0:384], ACT.Copy).then_inc(pt_ready, 1)

            def bt_high(i, src, scale=None):
                for b in range(2):
                    for r in range(2):
                        ins = nc.scalar.activation(bt_hi[:, 2 * b + r, :], psum3(src + b, 2)[:, r, :], ACT.Copy,
                                                   scale=1.0 if scale is None else scale[:, 2 * b + r:2 * b + r + 1])
                ins.then_inc(bt_hi_done, 1)

            def pool_attn(k, i):
                n0, e0, g0 = first_piece[k], evac0[k], map0[k]
                u, q, kk, v = (tok(A[name]) for name in ("u", "q", "k", "v"))
                for p in range(PIECES["pool_attn"]):
                    ahead(n0 + p)
                    if p == 1:
                        take(k, 0, e0, u)
                    if p == 3:
                        take(k, 1, e0 + 2, q)
                        act.wait_ge(act_evac, e0 + 4)
                        nc.scalar.activation(A["sq"], A["q"], ACT.Square).then_inc(hsq_done, 1)
                        act.wait_ge(diff_done, i + 1)
                        for b in range(2):
                            ins = nc.scalar.activation(A["qt"][:, b * 512:(b + 1) * 512], bank[4 + b][:, :], ACT.Copy)
                        ins.then_inc(diff_ready, 1)
                    if p == 5:
                        take(k, 2, e0 + 4, kk)
                        act.wait_ge(act_evac, e0 + 6)
                        act.wait_ge(qk_ready, 2 * i + 1)
                        nc.scalar.activation(A["sq"], A["k"], ACT.Square).then_inc(hsq_done, 1)
                        act.wait_ge(params_in, params_at(k))
                        act.wait_ge(y_done, i + 1)
                        bt_high(2 * i, 6, A["pool_scale"])
                    if p == 7:
                        take(k, 3, e0 + 6, v)
                        turned_qk(2 * i, "qt", 4)
                    if p == 8:
                        turned_qk(2 * i + 1, "kt", 6)
                    if 10 <= p <= 17:
                        take_probs(g0 + p - 10)
                    if 9 <= p <= 16:
                        exp_map(g0 + p - 9, p - 9)
                    if p == 16:
                        act.wait_ge(gate_added, 8 * i + 8)
                        nc.scalar.activation(A["gates"], A["gates"], ACT.Sigmoid).then_inc(gates_ready, 1)
                    if p == 17:
                        act.wait_ge(ot_done, i + 1)
                        bt_high(2 * i + 1, 4)
                    if p == 19:
                        xt_high(turn0[k] + 1)

            def copy_banks(b0, dst, ready):
                for b in range(2):
                    ins = nc.scalar.activation(dst[:, b * 512:(b + 1) * 512], bank[b0 + b][:, :], ACT.Copy)
                ins.then_inc(M[ready], 1)

            def delta_ret(k):
                n0, e0 = first_piece[k], evac0[k]
                gates, e4 = G["gates"], G["e4"]

                def take_channels(i):
                    act.wait_ge(used, n0 + 2 * i + 2)
                    if i == 2:
                        act.wait_ge(M["conv_ready"], 1)
                        act.wait_ge(M["co_turned"], 1)
                    b0 = 2 * (i % 2)
                    for b in range(2):
                        nc.scalar.activation(ct[i % 2][:, 2 * b:2 * b + 2, 3:259], psum3(b0 + b, 2), ACT.Copy)
                    for c in range(4):
                        ins = nc.scalar.activation(co[i % 2][:, c, :], psum3(b0 + c // 2, 2)[:, c % 2, :], ACT.Copy,
                                                   scale=G["conv"][:, (4 * i + c) * 4 + 3:(4 * i + c) * 4 + 4])
                    ins.then_inc(M["ct_ready"], 1)

                def silu_conv(i):
                    act.wait_ge(M["conv_ready"], i + 1)
                    nc.scalar.activation(co[i % 2], co[i % 2], ACT.Silu).then_inc(M["co_ready"], 1)

                def take_tokens(i, dst):
                    act.wait_ge(M["co_turned"], i + 1)
                    copy_banks(4, dst, "tm_ready")

                def square(i, src, need=None):
                    if need:
                        act.wait_ge(M[need[0]], need[1])
                    nc.scalar.activation(G["rg"] if i < 2 else G["rv"], src, ACT.Square).then_inc(hsq_done, 1)

                def take_t1(l):
                    for tt in range(TT):
                        act.wait_ge(M["t1_done"], TT * (l - 1) + tt + 1)
                        nc.scalar.activation(prod1[:, tt].rearrange("p h q -> p (h q)"), bank[4 + tt][:, :], ACT.Copy).then_inc(M["t1_ready"], 1)

                act.wait_ge(params_in, params_at(k))
                nc.scalar.activation(ba_hi[:, :], G["ba"], ACT.Copy).then_inc(M["ba_hi"], 1)
                for p in range(PIECES["delta_ret"]):
                    ahead(n0 + p)
                    if p == 0:
                        act.wait_ge(M["abs_ready"], 1)
                        nc.scalar.activation(gates[:, 24:32], gates[:, 16:24], ACT.Exp, scale=-1.0)
                        nc.scalar.activation(gates[:, 32:36], G["alog_dt"][:, 0:4], ACT.Exp)
                        nc.scalar.activation(gates[:, 48:56], gates[:, 40:48], ACT.Exp, scale=-1.0).then_inc(M["exps_ready"], 1)
                        act.wait_ge(M["exps_ready"], 1)
                        nc.scalar.activation(gates[:, 24:32], gates[:, 24:32], ACT.Ln, bias=1.0).then_inc(M["softplus_ready"], 1)
                    if p == 1:
                        act.wait_ge(M["gcum_copied"], 1)
                        nc.scalar.activation(e4, bank[5][:, 0:32], ACT.Exp).then_inc(M["e4_ready"], 1)
                        take_channels(0)
                    if p == 2:
                        act.wait_ge(M["diff_ready"], 1)
                        nc.scalar.activation(G["decay_oa"], G["decay_oa"], ACT.Exp).then_inc(M["decay_ready"], 1)
                    if p == 3:
                        silu_conv(0)
                        take_channels(1)
                        take_tokens(0, G["k_kd"])
                        square(0, G["k_kd"], ("tm_ready", 1))
                    if p == 5:
                        silu_conv(1)
                        take_channels(2)
                        take_tokens(1, G["q_qd_u"])
                        square(1, G["q_qd_u"], ("tm_ready", 2))
                        act.wait_ge(M["kt_turned"], 1)
                        copy_banks(6, G["kt_rt"], "kt_ready")
                    if p == 6:
                        act.wait_ge(M["kbt_turned"], 1)
                        copy_banks(4, G["kbt_wt"], "kbt_ready")
                        act.wait_ge(M["qt_turned"], 1)
                        copy_banks(6, G["qt_pr"], "qt_ready")
                        silu_conv(2)
                    if p == 7:
                        take_tokens(2, G["v_vb"])
                        take(k, 3, e0, tok(G["gz"]), ACT.Silu, 3)
                    if p == 8:
                        act.wait_ge(M["qdt_turned"], 1)
                        copy_banks(6, G["qdt"], "qdt_ready")
                    if p == 9:
                        act.wait_ge(M["x0_turned"], 1)
                        copy_banks(4, inv.rearrange("p t h q -> p (t h q)"), "x0_ready")
                        take(k, 4, e0 + 2, tok(G["rqk_ob"]), ACT.Copy, 3)
                        take_t1(1)
                    if p == 10:
                        take_t1(2)
                    if p == 11:
                        take(k, 5, e0 + 4, tok(G["rv"]), ACT.Copy, 3)
                        take_t1(3)
                        act.wait_ge(M["rqk_turned"], 1)
                        copy_banks(6, G["kt_rt"], "rqk_ready")
                    if p == 12:
                        take_t1(4)
                    if p == 13:
                        take(k, 6, e0 + 6, tok(G["rg"]), ACT.Silu, 3)
                        take_t1(5)
                        act.wait_ge(M["ro_done"], 1)
                        copy_banks(6, G["rqk_ob"], "ro_ready")
                        act.wait_ge(M["ro_ready"], 1)
                        square(2, G["rqk_ob"])
                        act.wait_ge(M["u_done"], 1)
                        copy_banks(4, G["q_qd_u"], "u_ready")
                        act.wait_ge(M["wt_done"], 1)
                        copy_banks(6, G["kbt_wt"], "wt_ready")
                        act.wait_ge(ot_done, o_turn0[k] + 1)
                        bt_high(bt0[k], 4)
                    if p == 15:
                        for tt in range(TT):
                            act.wait_ge(M["o_done"], 2 * tt + 2)
                            nc.scalar.activation(G["decay_oa"][:, tt * 512:(tt + 1) * 512], bank[6 + tt][:, :], ACT.Copy).then_inc(M["oa_ready"], 1)
                        square(3, G["decay_oa"], ("oa_ready", TT))
                        act.wait_ge(ot_done, o_turn0[k] + 2)
                        bt_high(bt0[k] + 1, 4)

            def dil_diff(k):
                n0, e0, g0, c0 = first_piece[k], evac0[k], map0[k], turned0[k]
                order = ("dq", "dk", "dv", "cq", "ck", "cv")
                act.wait_ge(lam_sums, 1)
                nc.scalar.activation(B["lam"][:, 2:4], B["lam"][:, 0:2], ACT.Exp).then_inc(lam_exp, 1)
                for p in range(PIECES["dil_diff"]):
                    ahead(n0 + p)
                    if p % 2 and p < 12:
                        take(k, p // 2, e0 + p - 1, tok(B[order[p // 2]]))
                    if p == 3:
                        turned_qk(c0, "dqt", 4, B)
                    if p == 5:
                        turned_qk(c0 + 1, "dkt", 6, B)
                    if 7 <= p <= 10:
                        take_probs(g0 + 2 * (p - 7))
                        take_probs(g0 + 2 * (p - 7) + 1)
                    if 6 <= p <= 9:
                        exp_map(g0 + 2 * (p - 6), 2 * (p - 6))
                        exp_map(g0 + 2 * (p - 6) + 1, 2 * (p - 6) + 1)
                    if p == 10:
                        turned_qk(c0 + 2, "cqt", 4, B)
                    if p == 11:
                        act.wait_ge(diff_squared, 1)
                        nc.scalar.activation(B["sq"], B["diff"], ACT.Square).then_inc(hsq_done, 1)
                        turned_qk(c0 + 3, "ckt", 4, B)
                        act.wait_ge(ot_done, o_turn0[k] + 1)
                        bt_high(bt0[k], 6)
                    if p == 12:
                        exp_map(g0 + 8, 0)
                        exp_map(g0 + 9, 1)
                    if p == 13:
                        take_probs(g0 + 8)
                        take_probs(g0 + 9)
                        exp_map(g0 + 10, 2)
                        exp_map(g0 + 11, 3)
                        take_probs(g0 + 10)
                        take_probs(g0 + 11)
                        act.wait_ge(ot_done, o_turn0[k] + 2)
                        bt_high(bt0[k] + 1, 4)

            def turned_qk(c, name, b0, bufs=A):
                act.wait_ge(qkt_done, c + 1)
                for b in range(2):
                    ins = nc.scalar.activation(bufs[name][:, b * 512:(b + 1) * 512], bank[b0 + b][:, :], ACT.Copy)
                ins.then_inc(qkt_ready, 1)

            for m in range(2):
                split_hi(m, m, True)
            seen = {"pool_attn": 0}
            f = 0
            for k, kind in enumerate(program):
                norm(k)
                xt_high(turn0[k])
                if kind == "ffn":
                    ffn(f, first_piece[k])
                    f += 1
                if kind == "pool_attn":
                    pool_attn(k, seen[kind])
                    seen[kind] += 1
                if kind == "dil_diff":
                    dil_diff(k)
                if kind == "delta_ret":
                    delta_ret(k)
            norm(norms - 1)

        @block.vector
        def _(dve):
            steps = [0]

            def link(ins):
                steps[0] += 1
                ins.then_inc(dve_step, 1)
                dve.wait_ge(dve_step, steps[0])

            def split_lo(m, s):
                dve.wait_ge(hi_done, m + 1)
                nc.vector.tensor_tensor(w_lo[s][:, :], w_raw[s][:, :], w_hi[s][:, :].bitcast(F32),
                                        ALU.subtract).then_inc(lo_done, 1)

            def norm(k):
                for tt in range(TT):
                    dve.wait_ge(ss_done, TT * k + tt + 1)
                    nc.vector.tensor_scalar(stat[:, 1, tt:tt + 1], stat[:, 0, tt:tt + 1], 1.0 / D, EPS, ALU.mult, ALU.add).then_inc(mean_ready, 1)
                    dve.wait_ge(rstd_ready, TT * k + tt + 1)
                    dve.wait_ge(gain_in, 16 * (k + 1))
                    nc.vector.scalar_tensor_tensor(out=xn[:, tt, :], in0=x[:, tt, :], scalar=stat[:, 2, tt:tt + 1],
                                                   in1=gain[:, :], op0=ALU.mult, op1=ALU.mult).then_inc(xn_ready, 1)

            def xt_low(k):
                for tt in range(TT):
                    for g in range(2):
                        b = 4 + 2 * tt + g
                        dve.wait_ge(xt_hi_done, 4 * k + 2 * tt + g + 1)
                        v = slice(4 * g, 4 * g + 4), slice(tt * P, (tt + 1) * P)
                        nc.vector.tensor_tensor(xt_lo[:, v[0], v[1]], bank[b][:, :].rearrange("p (k q) -> p k q", k=4),
                                                xt_hi[:, v[0], v[1]].bitcast(F32), ALU.subtract).then_inc(xt_lo_done, 1)

            def ffn(f, n0):
                base = n0

                def hidden(c):
                    for tt in range(TT):
                        dve.wait_ge(gate_ready, c * TT + (TT * NCH * f + tt + 1))
                        nc.vector.tensor_tensor(hid[:, tt, :], bank[4 + tt][:, CH:2 * CH], gate[:, tt, :],
                                                ALU.mult).then_inc(hid_ready, 1)

                def ht_low(c):
                    dve.wait_ge(ht_hi_done, c + (NCH * f + 1))
                    nc.vector.tensor_tensor(ht_lo[:, :, :], bank[6][:, :].rearrange("p (k q) -> p k q", k=2),
                                            ht_hi[:, :, :].bitcast(F32), ALU.subtract).then_inc(ht_lo_done, 1)

                def ahead(j, c):
                    m = c * SLOTS + (base - 1 + j)
                    if not isinstance(c, int) or m < n_pieces:
                        split_lo(m, (base + 2 + j) % SLOTS)

                def step(c):
                    ht_low(c - 1)
                    ahead(2, c)
                    ahead(3, c)
                    hidden(c)
                    ahead(4, c)

                split_lo(base + 2, (base + 2) % SLOTS)
                hidden(0)
                split_lo(base + 3, (base + 3) % SLOTS)
                step(1)
                with dve.Fori(2, NCH - 1) as c:
                    step(c)
                step(NCH - 1)
                ht_low(NCH - 1)
                if base + 34 < n_pieces:
                    split_lo(base + 34, (base + 34) % SLOTS)

            def add_to_x(k, o, scale):
                for tt in range(TT):
                    if tt == 0:
                        dve.wait_ge(out_done, o + 1)
                    else:
                        dve.wait_ge(used, first_piece[k] + PIECES[program[k]])
                    for h in range(2):
                        xs = x[:, tt, h * 512:(h + 1) * 512]
                        ins = nc.vector.scalar_tensor_tensor(out=xs, in0=bank[2 * tt + h][:, :], scalar=scale, in1=xs,
                                                             op0=ALU.mult, op1=ALU.add)
                    ins.then_inc(x_ready, 1)

            def ahead(m):
                if m + 2 < n_pieces:
                    split_lo(m + 2, (m + 2) % SLOTS)

            def delta_ret(k):
                n0, e0, h0 = first_piece[k], evac0[k], head_norm0[k]
                gates = G["gates"]
                per_head = lambda v: v.rearrange("p (n w) -> p n w", w=P)
                th = lambda v: v.unsqueeze(2).broadcast_to([P, 8, P])
                beta, e4, gc = gates[:, 56:64], G["e4"], G["gc"]
                eg, edec = e4[:, 0:8], e4[:, 8:16]
                conv = G["conv"]
                tab = G["rope"].rearrange("p (c t d) -> p c t d", c=2, t=TT)
                ret = G["ret"].rearrange("p (h q) -> p h q", h=4)

                def convolve(i):
                    dve.wait_ge(M["ct_ready"], i + 1)
                    for j in range(3):
                        for c in range(4):
                            w = (4 * i + c) * 4 + j
                            ins = nc.vector.scalar_tensor_tensor(out=co[i % 2][:, c, :], in0=ct[i % 2][:, c, j:j + SEQ],
                                                                 scalar=conv[:, w:w + 1], in1=co[i % 2][:, c, :],
                                                                 op0=ALU.mult, op1=ALU.add)
                        if j < 2:
                            link(ins)
                    ins.then_inc(M["conv_ready"], 1)

                def scaled(out, x, by, ready):
                    nc.vector.tensor_tensor(per_head(out), per_head(x), th(by), ALU.mult).then_inc(M[ready], 1)

                def update(l):
                    for tt in range(TT):
                        dve.wait_ge(M["y_done"], TT * (l - 1) + tt + 1)
                        if l < 5:
                            a = inv[:, tt].rearrange("p h q -> p (h q)")
                            nc.vector.tensor_tensor(a, a, bank[6 + tt][:, :], ALU.subtract)
                        a = inv_t[:, tt].rearrange("p h q -> p (h q)")
                        nc.vector.tensor_tensor(a, a, bank[4 + tt][:, :], ALU.subtract).then_inc(M["x_updated"], 1)

                def decay_scores(h):
                    dve.wait_ge(M["rs_done"], h + 1)
                    pr = retention_probs(h)
                    nc.vector.scalar_tensor_tensor(out=pr[:, 0:SEQ], in0=bank[6 + h % 2][:, 0:SEQ], scalar=0.125,
                                                   in1=ret[:, h, :], op0=ALU.mult, op1=ALU.mult)
                    nc.vector.scalar_tensor_tensor(out=pr[:, SEQ:384], in0=bank[6 + h % 2][:, SEQ:384], scalar=0.125,
                                                   in1=ret[:, h, 0:P], op0=ALU.mult, op1=ALU.mult).then_inc(M["rs_ready"], 1)

                def new_values(n):
                    tt, rows = n // 2, slice(64 * (n % 2), 64 * (n % 2) + 64)
                    dve.wait_ge(M["vw_done"], n)
                    nc.vector.tensor_tensor(v_new[rows].rearrange("p h e -> p (h e)"), tok(G["q_qd_u"])[rows, tt, :],
                                            bank[4][rows, :], ALU.subtract).then_inc(M["vn_ready"], 1)

                def next_state(n):
                    dve.wait_ge(M["ds_done"], n + 1)
                    if n == 0:
                        nc.vector.tensor_copy(state.rearrange("p h e -> p (h e)"), bank[5][:, :]).then_inc(M["s_ready"], 1)
                        return
                    el = e4[:, 16 + 8 * (n % 2) + 4 * (n // 2):]
                    for h in range(4):
                        ins = nc.vector.scalar_tensor_tensor(out=state[:, h, :], in0=state[:, h, :], scalar=el[:, h:h + 1],
                                                             in1=psum3(5, 4)[:, h, :], op0=ALU.mult, op1=ALU.add)
                    ins.then_inc(M["s_ready"], 1)

                dve.wait_ge(M["ba_hi"], 1)
                nc.vector.tensor_tensor(ba_lo[:, :], G["ba"], ba_hi[:, :].bitcast(F32), ALU.subtract).then_inc(M["ba_split"], 1)
                for p in range(PIECES["delta_ret"]):
                    ahead(n0 + p)
                    if p == 0:
                        dve.wait_ge(M["ba_done"], 1)
                        ba = bank[4][:, 0:16].rearrange("p (t c) -> p t c", t=TT)
                        g2 = lambda a: gates[:, a:a + 8].rearrange("p (t h) -> p t h", t=TT)
                        dt = G["alog_dt"][:, 4:8].unsqueeze(1).broadcast_to([P, TT, 4])
                        nc.vector.tensor_copy(g2(40), ba[:, :, 0:4])
                        link(nc.vector.tensor_tensor(g2(0), ba[:, :, 4:8], dt, ALU.add))
                        link(nc.vector.tensor_scalar(gates[:, 8:16], gates[:, 0:8], -1.0, None, ALU.mult))
                        nc.vector.tensor_tensor(gates[:, 16:24], gates[:, 0:8], gates[:, 8:16], ALU.max).then_inc(M["abs_ready"], 1)
                        dve.wait_ge(M["softplus_ready"], 1)
                        link(nc.vector.scalar_tensor_tensor(out=gates[:, 8:16], in0=gates[:, 0:8], scalar=0.0,
                                                            in1=gates[:, 24:32], op0=ALU.max, op1=ALU.add))
                        ea = gates[:, 32:36].unsqueeze(1).broadcast_to([P, TT, 4])
                        link(nc.vector.scalar_tensor_tensor(out=g2(0), in0=g2(8), scalar=-1.0, in1=ea, op0=ALU.mult, op1=ALU.mult))
                        link(nc.vector.tensor_scalar(gates[:, 48:56], gates[:, 48:56], 1.0, None, ALU.add))
                        nc.vector.reciprocal(beta, gates[:, 48:56]).then_inc(M["g_ready"], 1)
                        nc.vector.tensor_tensor(per_head(G["decay_oa"]), G["before"].unsqueeze(1).broadcast_to([P, 8, P]),
                                                th(gates[:, 0:8]), ALU.mult).then_inc(M["ug_ready"], 1)
                    if p == 1:
                        dve.wait_ge(M["sums_done"], 1)
                        nc.vector.tensor_copy(gc, bank[5][:, 0:8]).then_inc(M["gcum_copied"], 1)
                    if p == 2:
                        dve.wait_ge(M["diff_done"], 1)
                        dve.wait_ge(M["gcum_copied"], 1)
                        for i in range(8):
                            ins = nc.vector.scalar_tensor_tensor(out=per_head(G["decay_oa"])[:, i, :], in0=psum3(6 + i // 4, 4)[:, i % 4, :],
                                                                 scalar=gc[:, i:i + 1], in1=G["below"], op0=ALU.subtract, op1=ALU.add)
                        ins.then_inc(M["diff_ready"], 1)
                        convolve(0)
                    if p == 4:
                        head_norm(h0, G["rg"], 8, P, 1.0, EPS, per_head(G["k_kd"]))
                        scaled(G["kb_kbe"], G["k_kd"], beta, "kb_ready")
                        convolve(1)
                    if p == 6:
                        head_norm(h0 + 1, G["rg"], 8, P, float(P), P * EPS, per_head(G["q_qd_u"]))
                        nc.vector.tensor_copy(hstat[:, 0, 0:1], hstat[:, 1, 0:1]).then_inc(M["normed"], 1)
                        convolve(2)
                        dve.wait_ge(M["kbt_turned"], 1)
                        dve.wait_ge(M["kb_ready"], 1)
                        dve.wait_ge(M["e4_ready"], 1)
                        scaled(G["kb_kbe"], G["kb_kbe"], eg, "kbe_ready")
                        dve.wait_ge(M["kt_turned"], 1)
                        scaled(G["k_kd"], G["k_kd"], edec, "kd_ready")
                        dve.wait_ge(M["qt_turned"], 1)
                        scaled(G["q_qd_u"], G["q_qd_u"], eg, "qd_ready")
                    if p == 7:
                        dve.wait_ge(M["at_done"], 1)
                        dve.wait_ge(M["decay_ready"], 1)
                        for tt in range(TT):
                            ins = nc.vector.tensor_tensor(at_m[:, tt].rearrange("p h q -> p (h q)"), bank[6 + tt][:, :],
                                                          G["decay_oa"][:, tt * 512:(tt + 1) * 512], ALU.mult)
                        ins.then_inc(M["at_ready"], 1)
                        dve.wait_ge(M["at_ready"], 1)
                        flat = lambda v: v.rearrange("p t h q -> p (t h) q")
                        each = lambda v: v.unsqueeze(1).broadcast_to([P, 8, P])
                        dve.wait_ge(M["conv_ready"], 3)
                        dve.wait_ge(M["co_turned"], 3)
                        link(nc.vector.tensor_tensor(flat(inv_t), flat(at_m), each(G["level"][:, 0:P]), ALU.mult))
                        nc.vector.tensor_tensor(flat(inv_t), each(ident[:, :]), flat(inv_t), ALU.subtract).then_inc(M["xt0_ready"], 1)
                    if p == 8:
                        dve.wait_ge(M["tm_ready"], 3)
                        scaled(G["v_vb"], G["v_vb"], beta, "vb_ready")
                        dve.wait_ge(M["qk_done"], 1)
                        for tt in range(TT):
                            ins = nc.vector.tensor_tensor(qk_m[:, tt].rearrange("p h q -> p (h q)"), bank[4 + tt][:, :],
                                                          G["decay_oa"][:, tt * 512:(tt + 1) * 512], ALU.mult)
                        ins.then_inc(M["qk_masked"], 1)
                        dve.wait_ge(act_evac, e0 + 2)
                        gz = per_head(G["gz"])
                        nc.vector.tensor_tensor(gz, gz, each(G["gdn_norm"]), ALU.mult).then_inc(M["gz_ready"], 1)
                    if p == 10:
                        update(1)
                        dve.wait_ge(act_evac, e0 + 4)
                        rope(heads(G["rqk_ob"]), heads(G["rg"]), tab[:, 0], tab[:, 1], 64).then_inc(qk_ready, 1)
                    if p == 11:
                        update(2)
                    if p == 12:
                        update(3)
                        decay_scores(0)
                        decay_scores(1)
                    if p == 13:
                        update(4)
                        decay_scores(2)
                        decay_scores(3)
                        update(5)
                        head_norm(h0 + 2, G["rv"], 8, P, 1.0 / P, EPS, per_head(G["rqk_ob"]))
                        dve.wait_ge(act_evac, e0 + 8)
                        nc.vector.tensor_tensor(G["rqk_ob"], G["rqk_ob"], G["rg"], ALU.mult).then_inc(M["half_normed"], 1)
                        bt_low(bt0[k], 4)
                    if p == 14:
                        next_state(0)
                        for n in range(1, 4):
                            new_values(n)
                            if n < 3:
                                next_state(n)
                    if p == 15:
                        head_norm(h0 + 3, G["rv"], 8, P, 1.0 / P, EPS, per_head(G["decay_oa"]))
                        dve.wait_ge(M["gz_ready"], 1)
                        nc.vector.tensor_tensor(G["decay_oa"], G["decay_oa"], G["gz"], ALU.mult).then_inc(M["half_normed"], 1)
                        bt_low(bt0[k] + 1, 4)
                add_to_x(k, out0[k], 1.0)

            def dil_diff(k):
                n0, e0, g0, r0, rp = first_piece[k], evac0[k], map0[k], round0[k], rope0[k]
                tab = B["rope"].rearrange("p (c t d) -> p c t d", c=2, t=TT)
                tab_wide = B["rope_wide"].rearrange("p (c t d) -> p c t d", c=2, t=TT)
                lam = B["lam"]
                d4 = heads(B["diff"], P)
                x4 = xn[:, :, 0:512].rearrange("p t (r n w) -> p t r n w", r=2, n=2)

                def rotate(name, j, tables, w):
                    dve.wait_ge(act_evac, e0 + 2 * j + 2)
                    rope(heads(B[name], w), heads(B["rot"], w), tables[:, 0], tables[:, 1], w).then_inc(qk_ready, 1)

                def take_pair(h):
                    dve.wait_ge(pv_done, g0 + 2 * h + 2)
                    i = 2 * h
                    link(nc.vector.reciprocal(expsum[:, 1, :, i:i + 2], expsum[:, 0, :, i:i + 2]))
                    second = expsum[:, 1, :, i + 1]
                    link(nc.vector.tensor_scalar(second, second, lam[:, 5:6], None, ALU.mult))
                    for tt in range(TT):
                        prod = B["prod"][:, tt * P:(tt + 1) * P]
                        link(nc.vector.tensor_scalar(prod, bank[7][:, tt * 256 + P:tt * 256 + 256],
                                                     expsum[:, 1, tt, i + 1:i + 2], None, ALU.mult))
                        ins = nc.vector.scalar_tensor_tensor(out=d4[:, tt, h], in0=bank[7][:, tt * 256:tt * 256 + P],
                                                             scalar=expsum[:, 1, tt, i:i + 1], in1=prod, op0=ALU.mult, op1=ALU.add)
                    ins.then_inc(o_ready, 1)

                dve.wait_ge(params_in, params_at(k))
                pairs = B["lambdas"].rearrange("p (m w d) -> p m w d", m=2, w=2)
                prods = B["prod"][:, 0:128].rearrange("p (m d) -> p m d", m=2)
                link(nc.vector.tensor_tensor(prods, pairs[:, :, 0], pairs[:, :, 1], ALU.mult))
                nc.vector.tensor_reduce(lam[:, 0:2], prods, AX_X, ALU.add).then_inc(lam_sums, 1)
                link(nc.vector.tensor_scalar(B["diff_norm"], B["diff_norm"], 1.0 - LAMBDA_INIT, None, ALU.mult))
                dve.wait_ge(lam_exp, 1)
                link(nc.vector.tensor_tensor(lam[:, 4:5], lam[:, 3:4], lam[:, 2:3], ALU.subtract))
                link(nc.vector.tensor_scalar(lam[:, 5:6], lam[:, 4:5], -LAMBDA_INIT, None, ALU.add))
                for p in range(PIECES["dil_diff"]):
                    ahead(n0 + p)
                    if p == 2:
                        rotate("dq", 0, tab, 64)
                    if p == 4:
                        rotate("dk", 1, tab, 64)
                    if 8 <= p <= 11:
                        take_pair(p - 8)
                    if 6 <= p <= 9:
                        soft(g0 + 2 * (p - 6), 0.125, B["mask"])
                        soft(g0 + 2 * (p - 6) + 1, 0.125, B["mask"])
                    if p == 8:
                        rotate("cq", 3, tab_wide, P)
                    if p == 10:
                        rotate("ck", 4, tab_wide, P)
                    if p == 11:
                        dve.wait_ge(o_ready, r0 + 4)
                        nc.vector.tensor_copy(lam[:, 6:7], lam[:, 5:6]).then_inc(diff_squared, 1)
                        head_norm(head_norm0[k], B["sq"], 8, P, 1.0 / P, EPS, B["diff"].rearrange("p (n w) -> p n w", w=P))
                        gb = B["diff_norm"].unsqueeze(1).broadcast_to([P, 4, P])
                        for tt in range(TT):
                            ins = nc.vector.tensor_tensor(xn[:, tt, 512:D].rearrange("p (h w) -> p h w", w=P), d4[:, tt], gb, ALU.mult)
                        ins.then_inc(diff_normed, 1)
                        bt_low(bt0[k], 6)
                    if p == 12:
                        soft(g0 + 8, DIL_SCALE, B["mask_dil"])
                        soft(g0 + 9, DIL_SCALE, B["mask_dil"])
                    if p == 13:
                        soft(g0 + 10, DIL_SCALE, B["mask_dil"])
                        soft(g0 + 11, DIL_SCALE, B["mask_dil"])
                        take_round(r0 + 4, g0 + 9, 0, 2, x4[:, :, 0])
                        take_round(r0 + 5, g0 + 11, 2, 2, x4[:, :, 1])
                        bt_low(bt0[k] + 1, 4)
                add_to_x(k, out0[k], 1.0)

            def rope_gains(k, i):
                dve.wait_ge(params_in, params_at(k))
                tab = A["rope"].rearrange("p (c t d) -> p c t d", c=2, t=TT)
                out = A["rope_g"].rearrange("p (w c t d) -> p w c t d", w=2, c=2, t=TT)
                for w in range(2):
                    g = A["qk_norm"][:, 64 * w:64 * w + 64]
                    b = lambda lo, hi: g[:, lo:hi].unsqueeze(1).broadcast_to([P, TT, hi - lo])
                    nc.vector.tensor_tensor(out[:, w, 0], tab[:, 0], b(0, 64), ALU.mult)
                    nc.vector.tensor_tensor(out[:, w, 1, :, 0:32], tab[:, 1, :, 0:32], b(32, 64), ALU.mult)
                    link(nc.vector.tensor_tensor(out[:, w, 1, :, 32:64], tab[:, 1, :, 32:64], b(0, 32), ALU.mult))

            def head_norm(c, sq, n, w, scale, eps, x3):
                dve.wait_ge(hsq_done, c + 1)
                link(nc.vector.tensor_reduce(hstat[:, 0, 0:n], sq.rearrange("p (n w) -> p n w", w=w), AX_X, ALU.add))
                nc.vector.tensor_scalar(hstat[:, 1, 0:n], hstat[:, 0, 0:n], scale, eps, ALU.mult, ALU.add).then_inc(hmean_ready, 1)
                dve.wait_ge(hrstd_ready, c + 1)
                link(nc.vector.tensor_tensor(x3, x3, hstat[:, 2, 0:n].unsqueeze(2).broadcast_to([P, n, w]), ALU.mult))

            def rope(x, rot, cos, sin, w):
                h, n = w // 2, x.shape[2]
                b = lambda v: v.unsqueeze(2).broadcast_to([P, TT, n, v.shape[2]])
                nc.vector.tensor_tensor(rot[:, :, :, 0:h], x[:, :, :, h:w], b(sin[:, :, 0:h]), ALU.mult)
                link(nc.vector.tensor_tensor(rot[:, :, :, h:w], x[:, :, :, 0:h], b(sin[:, :, h:w]), ALU.mult))
                link(nc.vector.tensor_tensor(x, x, b(cos), ALU.mult))
                return nc.vector.tensor_tensor(x, x, rot, ALU.add)

            def soft(g, scale, mask):
                pr = A["probs"][:, (g % 2) * 384:(g % 2) * 384 + 384]
                dve.wait_ge(s_done, g + 1)
                if g >= 2:
                    dve.wait_ge(pt_done, g - 1)
                nc.vector.scalar_tensor_tensor(out=pr, in0=bank[4 + g % 2][:, 0:384], scalar=scale, in1=mask,
                                               op0=ALU.mult, op1=ALU.add).then_inc(s_masked, 1)
                dve.wait_ge(s_masked, g + 1)
                nc.vector.tensor_reduce(negmax[:, g % 2, 0:1], pr[:, 0:P], AX_X, ALU.max, negate=True)
                nc.vector.tensor_reduce(negmax[:, g % 2, 1:2], pr[:, P:3 * P], AX_X, ALU.max, negate=True).then_inc(max_ready, 1)

            def take_round(r, last_map, i0, n, out):
                dve.wait_ge(pv_done, last_map + 1)
                link(nc.vector.reciprocal(expsum[:, 1, :, i0:i0 + n], expsum[:, 0, :, i0:i0 + n]))
                w = 512 // (TT * n)
                nc.vector.tensor_tensor(out, bank[7][:, :].rearrange("p (t n w) -> p t n w", t=TT, n=n),
                                        expsum[:, 1, :, i0:i0 + n].unsqueeze(3).broadcast_to([P, TT, n, w]),
                                        ALU.mult).then_inc(o_ready, 1)

            def bt_low(c, src, scale=None):
                dve.wait_ge(bt_hi_done, c + 1)
                for b in range(2):
                    for r in range(2):
                        q, hi = 2 * b + r, bt_hi[:, 2 * b + r, :].bitcast(F32)
                        if scale is None:
                            ins = nc.vector.tensor_tensor(bt_lo[:, q, :], psum3(src + b, 2)[:, r, :], hi, ALU.subtract)
                        else:
                            ins = nc.vector.scalar_tensor_tensor(out=bt_lo[:, q, :], in0=psum3(src + b, 2)[:, r, :],
                                                                 scalar=scale[:, q:q + 1], in1=hi, op0=ALU.mult, op1=ALU.subtract)
                ins.then_inc(bt_lo_done, 1)

            def product_tile(k, o, tt, last_piece):
                if tt == 0:
                    dve.wait_ge(out_done, o + 1)
                else:
                    dve.wait_ge(used, last_piece + 1)

            def pool_attn(k, i):
                n0, g0, r0, c0, o0 = first_piece[k], map0[k], round0[k], head_norm0[k], out0[k]
                rg = A["rope_g"].rearrange("p (w c t d) -> p w c t d", w=2, c=2, t=TT)
                gates = tok(A["gates"])
                o4 = A["u"].rearrange("p (t r n w) -> p t r n w", t=TT, r=2, n=4)

                def rotate(which, name):
                    head_norm(c0 + which, A["sq"], 16, 64, 1.0 / 64, EPS, A[name].rearrange("p (n w) -> p n w", w=64))
                    rope(heads(A[name]), heads(A["rot"]), rg[:, which, 0], rg[:, which, 1], 64).then_inc(qk_ready, 1)

                for p in range(PIECES["pool_attn"]):
                    ahead(n0 + p)
                    if p == 0:
                        rope_gains(k, i)
                    if p == 4:
                        rotate(0, "q")
                    if p == 6:
                        bt_low(2 * i, 6, A["pool_scale"])
                        rotate(1, "k")
                    if p == 15:
                        take_round(r0, g0 + 3, 0, 4, o4[:, :, 0])
                    if 9 <= p <= 16:
                        soft(g0 + p - 9, 0.125, A["mask"])
                    if p in (9, 11, 13, 15):
                        j = (p - 1) // 2
                        for tt in range(TT):
                            if tt == 0:
                                dve.wait_ge(proj_done, chunk0[k] + j + 1)
                            else:
                                dve.wait_ge(used, n0 + 2 * j + 2)
                            gs = gates[:, tt, (j - 4) * 512:(j - 3) * 512]
                            nc.vector.tensor_tensor(gs, bank[2 * (j % 2) + tt][:, :], gs, ALU.add).then_inc(gate_added, 1)
                    if p == 17:
                        take_round(r0 + 1, g0 + 7, 4, 4, o4[:, :, 1])
                        dve.wait_ge(gates_ready, i + 1)
                        for tt in range(TT):
                            product_tile(k, o0, tt, n0 + 17)
                            for h in range(2):
                                ins = nc.vector.tensor_tensor(xn[:, tt, h * 512:(h + 1) * 512], bank[2 * tt + h][:, :],
                                                              gates[:, tt, h * 512:(h + 1) * 512], ALU.mult)
                            ins.then_inc(branch_ready, 1)
                        bt_low(2 * i + 1, 4)
                    if p == 19:
                        for tt in range(TT):
                            product_tile(k, o0 + 1, tt, n0 + 19)
                            g1 = gates[:, tt, D:2 * D]
                            nc.vector.tensor_tensor(g1[:, 0:512], bank[2 * tt][:, :], g1[:, 0:512], ALU.mult)
                            link(nc.vector.tensor_tensor(g1[:, 512:D], bank[2 * tt + 1][:, :], g1[:, 512:D], ALU.mult))
                            nc.vector.tensor_tensor(xn[:, tt, :], xn[:, tt, :], g1, ALU.add).then_inc(xn_ready, 1)
                        xt_low(turn0[k] + 1)
                add_to_x(k, o0 + 2, 1.0)

            for m in range(2):
                split_lo(m, m)
            seen = {"pool_attn": 0}
            f = 0
            for k, kind in enumerate(program):
                norm(k)
                xt_low(turn0[k])
                if kind == "ffn":
                    ffn(f, first_piece[k])
                    f += 1
                    add_to_x(k, out0[k], 0.5)
                if kind == "pool_attn":
                    pool_attn(k, seen[kind])
                    seen[kind] += 1
                if kind == "dil_diff":
                    dil_diff(k)
                if kind == "delta_ret":
                    delta_ret(k)
            norm(norms - 1)

        @block.tensor
        def _(pe):
            def three(out, a_hi, a_lo, b_hi, b_lo, start, stop):
                nc.tensor.matmul(out, a_hi, b_hi, start=start, stop=False)
                nc.tensor.matmul(out, a_hi, b_lo, start=False, stop=False)
                return nc.tensor.matmul(out, a_lo, b_hi, start=False, stop=stop)

            def transpose_x(k):
                for tt in range(TT):
                    pe.wait_ge(xn_ready, TT * k + tt + 1)
                    for g in range(2):
                        for q in range(4):
                            c = (4 * g + q) * P
                            ins = nc.tensor.transpose(bank[4 + 2 * tt + g][:, q * P:(q + 1) * P], xn[:, tt, c:c + P], ident[:, :])
                        ins.then_inc(xt_done, 1)

            def ffn(f, k, n0):
                base = n0

                def up(c):
                    for half in range(2):
                        s = (base + half + (0 if isinstance(c, int) and c == 0 else 2)) % SLOTS
                        m = (base + half) if isinstance(c, int) and c == 0 else c * SLOTS + (base + 2 - SLOTS + half)
                        pe.wait_ge(lo_done, m + 1)
                        for tt in range(TT):
                            if half == 0 and not (isinstance(c, int) and c == 0):
                                pe.wait_ge(hid_ready, c * TT + (TT * NCH * f + tt + 1 - TT))
                            if isinstance(c, int) and c == 0:
                                pe.wait_ge(xt_lo_done, 4 * turn0[k] + 2 * tt + half + 1)
                            for q in range(4):
                                kt = 4 * half + q
                                a = slice(tt * P, (tt + 1) * P)
                                ins = three(bank[4 + tt][:, :], xt_hi[:, kt, a], xt_lo[:, kt, a],
                                            up_view(w_hi[s], q), up_view(w_lo[s], q), kt == 0, kt == KT - 1)
                            if half == 1 and tt == 0:
                                ins.then_inc(up_done, 1)
                        ins.then_inc(used, 1)

                def down(c, m, s):
                    pe.wait_ge(lo_done, m + 1)
                    pe.wait_ge(ht_lo_done, c + (NCH * f + 1))
                    first = isinstance(c, int) and c == 0
                    final = isinstance(c, int) and c == NCH - 1
                    for tt in range(TT):
                        a = slice(tt * P, (tt + 1) * P)
                        for h in range(2):
                            for q in range(2):
                                ins = three(bank[2 * tt + h][:, :], ht_hi[:, q, a], ht_lo[:, q, a],
                                            down_view(w_hi[s], q, h), down_view(w_lo[s], q, h),
                                            first and q == 0, final and q == 1)
                        if final and tt == 0:
                            ins.then_inc(out_done, 1)
                    ins.then_inc(used, 1)

                def turn(c):
                    pe.wait_ge(hid_ready, c * TT + (TT * NCH * f + TT))
                    for q in range(2):
                        for tt in range(TT):
                            ins = nc.tensor.transpose(bank[6][:, q * SEQ + tt * P:q * SEQ + (tt + 1) * P],
                                                      hid[:, tt, q * P:(q + 1) * P], ident[:, :])
                    ins.then_inc(ht_done, 1)

                def step(c):
                    up(c)
                    down(c - 1, c * SLOTS + (base + 1), (base + 4) % SLOTS)
                    turn(c)

                up(0)
                turn(0)
                step(1)
                with pe.Fori(2, NCH - 1) as c:
                    step(c)
                step(NCH - 1)
                down(NCH - 1, base + 3 * NCH - 1, (base + 3 * NCH - 1) % SLOTS)

            def chunk_piece(k, n, j, half, hook=None):
                s = n % SLOTS
                pe.wait_ge(lo_done, n + 1)
                for tt in range(TT):
                    if j == 0:
                        pe.wait_ge(xt_lo_done, 4 * turn0[k] + 2 * tt + half + 1)
                    a = slice(tt * P, (tt + 1) * P)
                    for q in range(4):
                        kt = 4 * half + q
                        ins = three(bank[2 * (j % 2) + tt][:, :], xt_hi[:, kt, a], xt_lo[:, kt, a],
                                    up_view(w_hi[s], q), up_view(w_lo[s], q), kt == 0, kt == KT - 1)
                    if half == 1 and tt == 0:
                        ins.then_inc(proj_done, 1)
                    if tt == TT - 1:
                        ins.then_inc(used, 1)
                    if hook:
                        hook(tt)

            def product(n, pieces, operand, before=None, ready=None, after=None, between=None):
                for i in range(pieces):
                    s = (n + i) % SLOTS
                    pe.wait_ge(lo_done, n + i + 1)
                    for tt in range(TT):
                        if i == 0 and before:
                            before(tt)
                        if ready:
                            ready(i, tt)
                        a = slice(tt * P, (tt + 1) * P)
                        for h in range(2):
                            for q in range(2):
                                hi, lo = operand(i, q)
                                ins = three(bank[2 * tt + h][:, :], hi[:, a], lo[:, a],
                                            down_view(w_hi[s], q, h), down_view(w_lo[s], q, h),
                                            i == 0 and q == 0, i == pieces - 1 and q == 1)
                            last_one = tt == TT - 1 and h == 1
                            if last_one:
                                ins.then_inc(used, 1)
                            if h == 1 and i == pieces - 1 and tt == 0:
                                ins.then_inc(out_done, 1)
                            if between:
                                between(i, tt, h)
                    if after:
                        after(i)

            def in_bt(i, q):
                return bt_hi[:, 2 * (i % 2) + q, :], bt_lo[:, 2 * (i % 2) + q, :]

            def in_xt(i, q):
                return xt_hi[:, 2 * i + q, :], xt_lo[:, 2 * i + q, :]

            def turn_heads(src, b0):
                for c in range(4):
                    for tt in range(TT):
                        at = (c % 2) * SEQ + tt * P
                        ins = nc.tensor.transpose(bank[b0 + c // 2][:, at:at + P], src[:, tt, c * P:(c + 1) * P], ident[:, :])
                return ins

            def scores(g, operands):
                if g >= 2:
                    pe.wait_ge(s_masked, g - 1)
                for (lhs, rhs), (lo, hi) in zip(operands, ((0, P), (P, 3 * P))):
                    ins = nc.tensor.matmul(bank[4 + g % 2][:, lo:hi], lhs, rhs, start=True, stop=True)
                ins.then_inc(s_done, 1)

            def turn_probs(g):
                pe.wait_ge(exp_done, g + 1)
                if g >= 1:
                    pe.wait_ge(pt_ready, g)
                for c in range(3):
                    ins = nc.tensor.transpose(bank[6][:, c * P:(c + 1) * P],
                                              A["probs"][:, (g % 2) * 384 + c * P:(g % 2) * 384 + (c + 1) * P], ident[:, :])
                ins.then_inc(pt_done, 1)

            def values(g, j, n, vs, rounds_before):
                pe.wait_ge(pt_ready, g + 1)
                if j == 0 and rounds_before:
                    pe.wait_ge(o_ready, rounds_before)
                w = 512 // (TT * n)
                pt = A["probs_t"][:, (g % 2) * 384:(g % 2) * 384 + 384]
                nc.tensor.matmul(bank[7][:, j * w:(j + 1) * w], pt[:, 0:P], vs[0], start=True, stop=True)
                out = bank[7][:, 256 + j * w:256 + (j + 1) * w]
                nc.tensor.matmul(out, pt[:, P:2 * P], vs[0], start=True, stop=False)
                nc.tensor.matmul(out, pt[:, 2 * P:3 * P], vs[1], start=False, stop=True).then_inc(pv_done, 1)

            def pool_attn(k, i):
                n0, e0, g0, r0 = first_piece[k], evac0[k], map0[k], round0[k]
                u, v = tok(A["u"]), tok(A["v"])
                means = A["pool_mean"].rearrange("p (g q) -> p g q", g=4)
                mapped = lambda name: A[name].rearrange("p (c q) -> p c q", c=4)
                qt, kt, pw = mapped("qt"), mapped("kt"), A["pool_w"].rearrange("p (g d) -> p g d", g=4)

                def attend(h, what):
                    c, off = h // 2, 64 * (h % 2)
                    if what == "scores":
                        scores(g0 + h, causal_map(g0 + h, qt[:, c], kt[:, c], off, 64))
                    elif what == "turn":
                        turn_probs(g0 + h)
                    else:
                        values(g0 + h, h % 4, 4, [v[:, tt, h * 64:(h + 1) * 64] for tt in range(TT)], r0 + h // 4)

                for p in range(16):
                    j = p // 2
                    if p % 2 == 0 and j >= 2:
                        if j < 6:
                            pe.wait_ge(act_evac, e0 + 2 * (j - 2) + 2)
                        else:
                            pe.wait_ge(gate_added, 8 * i + 2 * (j - 6) + 2)
                    chunk_piece(k, n0 + p, j, p % 2)
                    if p == 3:
                        pe.wait_ge(params_in, params_at(k))
                        pe.wait_ge(act_evac, e0 + 2)
                        for g in range(4):
                            at = (g % 2) * SEQ
                            us = [u[:, tt, g * P:(g + 1) * P] for tt in range(TT)]
                            nc.tensor.matmul(bank[4 + g // 2][:, at:at + SEQ], us[0], means[:, g, 0:SEQ], start=True, stop=False)
                            ins = nc.tensor.matmul(bank[4 + g // 2][:, at + P:at + SEQ], us[1], means[:, g, SEQ:3 * P], start=False, stop=True)
                        ins.then_inc(diff_done, 1)
                    if p == 5:
                        pe.wait_ge(diff_ready, i + 1)
                        for g in range(4):
                            at = (g % 2) * SEQ
                            ins = nc.tensor.matmul(bank[6 + g // 2][:, at:at + SEQ], pw[:, g, :], qt[:, g, :], start=True, stop=True)
                        ins.then_inc(y_done, 1)
                    if p == 7:
                        pe.wait_ge(qk_ready, 2 * i + 1)
                        turn_heads(tok(A["q"]), 4).then_inc(qkt_done, 1)
                    if p == 8:
                        pe.wait_ge(bt_lo_done, 2 * i + 1)
                        pe.wait_ge(qk_ready, 2 * i + 2)
                        turn_heads(tok(A["k"]), 6).then_inc(qkt_done, 1)
                    if p == 9:
                        pe.wait_ge(qkt_ready, 2 * i + 2)
                    if p >= 10:
                        attend(p - 10, "turn")
                    if p >= 9:
                        attend(p - 9, "scores")
                    if p >= 11:
                        attend(p - 11, "values")

                def gates_out(tt):
                    pe.wait_ge(gate_added, 8 * i + 6 + 2 * tt)
                    if tt == 0:
                        pe.wait_ge(bt_lo_done, 2 * i + 1)

                def with_maps(i2):
                    attend(6 + i2, "turn")
                    if i2 == 0:
                        attend(7, "scores")
                    attend(5 + i2, "values")

                product(n0 + 16, 2, in_bt, gates_out, None, with_maps)
                attend(7, "values")
                pe.wait_ge(o_ready, r0 + 2)
                turn_heads(tok(A["u"]), 4).then_inc(ot_done, 1)

                def pooled_out(tt):
                    pe.wait_ge(branch_ready, TT * i + tt + 1)
                    pe.wait_ge(bt_lo_done, 2 * i + 2)

                product(n0 + 18, 2, in_bt, pooled_out)
                transpose_x(turn0[k] + 1)
                product(n0 + 20, 4, in_xt, None,
                        lambda i2, tt: pe.wait_ge(xt_lo_done, 4 * (turn0[k] + 1) + 2 * tt + i2 // 2 + 1))

            def delta_ret(k):
                n0, e0 = first_piece[k], evac0[k]
                mapped = lambda name: G[name].rearrange("p (c q) -> p c q", c=4)
                kt, qt, kbt, qdt, wt, rt = (mapped(name) for name in ("kt_rt", "qt_pr", "kbt_wt", "qdt", "kbt_wt", "kt_rt"))
                vb, kbe, kd, uu = (mats(G[name]) for name in ("v_vb", "kb_kbe", "k_kd", "q_qd_u"))
                rv = mats(G["rv"])
                mm = nc.tensor.matmul

                def channels_piece(i, half):
                    n = n0 + 2 * i + half
                    s, b0 = n % SLOTS, 2 * (i % 2)
                    pe.wait_ge(lo_done, n + 1)
                    for c in range(4):
                        out = psum3(b0 + c // 2, 2)[:, c % 2, :]
                        for q in range(4):
                            kt_ = 4 * half + q
                            cols = slice(q * 512 + c * P, q * 512 + (c + 1) * P)
                            args = dict(skip_group_check=True)
                            mm(out, w_hi[s][:, cols], xt_hi[:, kt_, :], start=kt_ == 0 and c % 2 == 0, stop=False, **args)
                            mm(out, w_hi[s][:, cols], xt_lo[:, kt_, :], start=False, stop=False, **args)
                            ins = mm(out, w_lo[s][:, cols], xt_hi[:, kt_, :], start=False, stop=kt_ == KT - 1, **args)
                    ins.then_inc(used, 1)

                def turn_channels(i):
                    pe.wait_ge(M["co_ready"], i + 1)
                    for tt in range(TT):
                        for c in range(4):
                            ins = nc.tensor.transpose(bank[4 + tt][:, c * P:(c + 1) * P], co[i % 2][:, c, tt * P:(tt + 1) * P], ident[:, :])
                    ins.then_inc(M["co_turned"], 1)

                def per_tile(b0, lhs, rhs, done):
                    for tt in range(TT):
                        for h in range(4):
                            ins = mm(bank[b0 + tt][:, h * P:(h + 1) * P], lhs(tt, h), rhs(tt, h), start=True, stop=True)
                    ins.then_inc(M[done], 1)

                tile = lambda m: (lambda tt, h: m[:, h, tt * P:(tt + 1) * P])
                mat = lambda m: (lambda tt, h: m[:, tt, h, :])

                def level_a(l):
                    pe.wait_ge(M["level_masked"], l)
                    for tt in range(TT):
                        if l == 1:
                            pe.wait_ge(M["x0_ready"], 1)
                        else:
                            pe.wait_ge(M["x_updated"], TT * (l - 2) + tt + 1)
                        for h in range(4):
                            ins = mm(bank[4 + tt][:, h * P:(h + 1) * P], lev[:, tt, h, :], inv[:, tt, h, :], start=True, stop=True)
                        ins.then_inc(M["t1_done"], 1)

                def level_b(l):
                    for tt in range(TT):
                        pe.wait_ge(M["t1_ready"], TT * (l - 1) + tt + 1)
                        for h in range(4):
                            cols = slice(h * P, (h + 1) * P)
                            if l < 5:
                                mm(bank[6 + tt][:, cols], inv_t[:, tt, h, :], prod1[:, tt, h, :], start=True, stop=True)
                            ins = mm(bank[4 + tt][:, cols], prod1[:, tt, h, :], inv_t[:, tt, h, :], start=True, stop=True)
                        ins.then_inc(M["y_done"], 1)

                def retention_scores(h):
                    c, rows = h // 2, slice(64 * (h % 2), 64 * (h % 2) + 64)
                    b = bank[6 + h % 2]
                    if h >= 2:
                        pe.wait_ge(M["rs_ready"], h - 1)
                    mm(b[:, 0:SEQ], rt[rows, 2 + c, 0:P], rt[rows, c, 0:SEQ], start=True, stop=True)
                    mm(b[:, SEQ:384], rt[rows, 2 + c, P:SEQ], rt[rows, c, P:SEQ], start=True, stop=True).then_inc(M["rs_done"], 1)

                def read_out(n, what):
                    tt, lo = n // 2, 64 * (n % 2)
                    rows = slice(lo, lo + 64)
                    toks = slice(tt * P + lo, tt * P + lo + 64)
                    for h in range(4):
                        out = bank[6 + tt][rows, h * P:(h + 1) * P]
                        if what == "state":
                            ins = mm(out, qdt[:, h, toks], state[:, h, :], start=h == 0, stop=False, skip_group_check=True)
                        else:
                            vals = uu[rows, 0, h, :] if n == 0 else v_new[rows, h, :]
                            ins = mm(out, qk_m[rows, tt, h, rows], vals, start=n == 0 and h == 0, stop=True, skip_group_check=True)
                    return ins

                def old_values(n):
                    tt, lo = n // 2, 64 * (n % 2)
                    toks = slice(tt * P + lo, tt * P + lo + 64)
                    pe.wait_ge(M["s_ready"], n)
                    for h in range(4):
                        ins = mm(bank[4][lo:lo + 64, h * P:(h + 1) * P], wt[:, h, toks], state[:, h, :], start=True, stop=True)
                    ins.then_inc(M["vw_done"], 1)
                    read_out(n, "state")

                def own_values(n):
                    tt, rows = n // 2, slice(64 * (n % 2), 64 * (n % 2) + 64)
                    if n:
                        pe.wait_ge(M["vn_ready"], n)
                    if n < 3:
                        for h in range(4):
                            vals = uu[rows, 0, h, :] if n == 0 else v_new[rows, h, :]
                            ins = mm(bank[5][:, h * P:(h + 1) * P], kd[rows, tt, h, :], vals, start=True, stop=True)
                        ins.then_inc(M["ds_done"], 1)
                    read_out(n, "own").then_inc(M["o_done"], 1)

                pe.wait_ge(M["ba_split"], 1)
                pe.wait_ge(xt_lo_done, 4 * turn0[k] + 4)
                for tt in range(TT):
                    for kt_ in range(KT):
                        a, c = slice(tt * P, (tt + 1) * P), slice(kt_ * 8, kt_ * 8 + 8)
                        ins = three(bank[4][:, tt * 8:tt * 8 + 8], xt_hi[:, kt_, a], xt_lo[:, kt_, a], ba_hi[:, c], ba_lo[:, c],
                                    kt_ == 0, kt_ == KT - 1)
                ins.then_inc(M["ba_done"], 1)

                def hook(p, tt):
                    if p == 6 and tt == 0:
                        pe.wait_ge(M["tm_ready"], 2)
                        pe.wait_ge(M["kb_ready"], 1)
                        turn_heads(tok(G["kb_kbe"]), 4).then_inc(M["kbt_turned"], 1)
                    if p == 6 and tt == 1:
                        pe.wait_ge(M["kt_ready"], 1)
                        pe.wait_ge(M["normed"], 1)
                        turn_heads(tok(G["q_qd_u"]), 6).then_inc(M["qt_turned"], 1)
                    if p == 7 and tt == 0:
                        pe.wait_ge(M["kbt_ready"], 1)
                        turn_channels(2)
                    if p == 7 and tt == 1:
                        pe.wait_ge(M["qt_ready"], 1)
                        per_tile(6, tile(kt), tile(kbt), "at_done")
                    if p == 8 and tt == 0:
                        pe.wait_ge(M["tm_ready"], 3)
                        per_tile(4, tile(kt), tile(qt), "qk_done")
                    if p == 8 and tt == 1:
                        pe.wait_ge(M["at_ready"], 1)
                        pe.wait_ge(M["qd_ready"], 1)
                        turn_heads(tok(G["q_qd_u"]), 6).then_inc(M["qdt_turned"], 1)
                    if p == 9 and tt == 0:
                        pe.wait_ge(M["qk_masked"], 1)
                        pe.wait_ge(M["xt0_ready"], 1)
                        for t2 in range(TT):
                            for h in range(4):
                                ins = nc.tensor.transpose(bank[4 + t2][:, h * P:(h + 1) * P], inv_t[:, t2, h, :], ident[:, :])
                        ins.then_inc(M["x0_turned"], 1)
                    if p == 9 and tt == 1:
                        pe.wait_ge(M["qdt_ready"], 1)
                        level_a(1)
                    if p >= 10:
                        if tt == 0:
                            if p == 12:
                                pe.wait_ge(M["rqk_ready"], 1)
                            if p == 13:
                                pe.wait_ge(M["rs_ready"], 2)
                            level_b(p - 9)
                        else:
                            if p == 13:
                                level_a(5)
                                retention_scores(2)
                                retention_scores(3)
                            else:
                                level_a(p - 8)
                            if p == 11:
                                pe.wait_ge(qk_ready, rope0[k] + 1)
                                pe.wait_ge(M["x_updated"], 4)
                                turn_heads(tok(G["rqk_ob"]), 6).then_inc(M["rqk_turned"], 1)
                            if p == 12:
                                pe.wait_ge(M["x_updated"], 6)
                                pe.wait_ge(M["rqk_ready"], 1)
                                retention_scores(0)
                                retention_scores(1)

                for p in range(14):
                    if p < 6:
                        if p == 4:
                            pe.wait_ge(M["ct_ready"], 1)
                        channels_piece(p // 2, p % 2)
                    else:
                        if p % 2 == 0:
                            if p < 10:
                                pe.wait_ge(M["ct_ready"], p // 2 - 1)
                            else:
                                pe.wait_ge(act_evac, e0 + 2 * (p // 2 - 5) + 2)
                        chunk_piece(k, n0 + p, p // 2, p % 2, lambda tt, p=p: hook(p, tt)) if p != 13 else chunk_piece(
                            k, n0 + p, p // 2, 1, lambda tt: hook(13, tt))
                    if p == 0:
                        pe.wait_ge(M["g_ready"], 1)
                        g = G["gates"][:, 0:8]
                        consts = (G["before"], G["after"], G["sub"][:, 0:P], G["sub"][:, P:2 * P])
                        for i, m in enumerate(consts):
                            ins = mm(bank[5][:, 8 * i:8 * i + 8], m, g, start=True, stop=True)
                        ins.then_inc(M["sums_done"], 1)
                    if p == 1:
                        pe.wait_ge(M["ug_ready"], 1)
                        for tt in range(TT):
                            ins = mm(bank[6 + tt][:, :], G["ones"], G["decay_oa"][:, tt * 512:(tt + 1) * 512], start=True, stop=True)
                        ins.then_inc(M["diff_done"], 1)
                    if p == 3:
                        pe.wait_ge(M["e4_ready"], 1)
                        turn_channels(0)
                    if p == 5:
                        pe.wait_ge(M["tm_ready"], 1)
                        turn_channels(1)
                        pe.wait_ge(M["diff_ready"], 1)
                        pe.wait_ge(M["kb_ready"], 1)
                        turn_heads(tok(G["k_kd"]), 6).then_inc(M["kt_turned"], 1)
                level_b(5)
                pe.wait_ge(M["rs_ready"], 4)
                pe.wait_ge(act_evac, e0 + 6)
                for h in range(4):
                    pr, cols = retention_probs(h), slice(h * P, (h + 1) * P)
                    mm(bank[6][:, cols], pr[:, 0:P], rv[:, 0, h, :], start=True, stop=True)
                    mm(bank[7][:, cols], pr[:, P:2 * P], rv[:, 0, h, :], start=True, stop=False)
                    ins = mm(bank[7][:, cols], pr[:, 2 * P:3 * P], rv[:, 1, h, :], start=False, stop=True)
                ins.then_inc(M["ro_done"], 1)
                pe.wait_ge(M["x_updated"], 10)
                pe.wait_ge(M["vb_ready"], 1)
                pe.wait_ge(M["kbe_ready"], 1)
                per_tile(4, mat(inv_t), mat(vb), "u_done")
                pe.wait_ge(M["ro_ready"], 1)
                for h in range(4):
                    for tt in range(TT):
                        ins = mm(psum3(6 + h // 2, 2)[:, h % 2, tt * P:(tt + 1) * P], kbe[:, tt, h, :], inv_t[:, tt, h, :], start=True, stop=True)
                ins.then_inc(M["wt_done"], 1)
                pe.wait_ge(M["u_ready"], 1)
                pe.wait_ge(M["half_normed"], 1)
                turn_heads(tok(G["rqk_ob"]), 4).then_inc(ot_done, 1)

                def before(tt):
                    pe.wait_ge(act_evac, e0 + (6 if tt == 0 else 8))

                def ready(i, tt):
                    if tt == 0 and i in (0, 2):
                        pe.wait_ge(bt_lo_done, bt0[k] + 1 + i // 2)

                def between(i, tt, h):
                    stage = i * 4 + tt * 2 + h
                    if stage == 0:
                        pe.wait_ge(M["wt_ready"], 1)
                        pe.wait_ge(M["kd_ready"], 1)
                        own_values(0)
                    elif stage < 7:
                        (old_values if stage % 2 else own_values)((stage + 1) // 2)
                    elif stage == 7:
                        pe.wait_ge(M["half_normed"], 2)
                        turn_heads(tok(G["decay_oa"]), 4).then_inc(ot_done, 1)

                product(n0 + 14, 4, in_bt, before, ready, None, between)

            def dil_diff(k):
                n0, e0, g0, r0, c0, rp = first_piece[k], evac0[k], map0[k], round0[k], turned0[k], rope0[k]
                mapped = lambda name: B[name].rearrange("p (c q) -> p c q", c=4)
                dv, cv = tok(B["dv"]), tok(B["cv"])

                def diff_scores(m):
                    scores(g0 + m, causal_map(g0 + m, mapped("dqt")[:, m // 2], mapped("dkt")[:, m // 2], 64 * (m % 2), 64))

                def diff_values(m):
                    values(g0 + m, m % 2, 2, [dv[:, tt, (m // 2) * P:(m // 2 + 1) * P] for tt in range(TT)], r0 + m // 2)

                def dil_scores(m):
                    scores(g0 + 8 + m, causal_map(g0 + 8 + m, mapped("cqt")[:, m], mapped("ckt")[:, m], 0, P))

                def dil_values(m):
                    values(g0 + 8 + m, m % 2, 2, [cv[:, tt, m * P:(m + 1) * P] for tt in range(TT)], r0 + 4 + m // 2)

                for p in range(12):
                    j = p // 2
                    if p % 2 == 0 and j >= 2:
                        pe.wait_ge(act_evac, e0 + 2 * (j - 2) + 2)
                    chunk_piece(k, n0 + p, j, p % 2)
                    if p == 3:
                        pe.wait_ge(qk_ready, rp + 1)
                        turn_heads(tok(B["dq"]), 4).then_inc(qkt_done, 1)
                    if p == 5:
                        pe.wait_ge(qk_ready, rp + 2)
                        turn_heads(tok(B["dk"]), 6).then_inc(qkt_done, 1)
                    if p == 6:
                        pe.wait_ge(qkt_ready, c0 + 2)
                    if p == 10:
                        pe.wait_ge(s_masked, g0 + 8)
                        pe.wait_ge(qk_ready, rp + 3)
                        turn_heads(tok(B["cq"]), 4).then_inc(qkt_done, 1)
                    if 7 <= p <= 10:
                        turn_probs(g0 + 2 * (p - 7))
                        turn_probs(g0 + 2 * (p - 7) + 1)
                    if 6 <= p <= 9:
                        diff_scores(2 * (p - 6))
                        diff_scores(2 * (p - 6) + 1)
                    if 7 <= p <= 10:
                        diff_values(2 * (p - 7))
                        diff_values(2 * (p - 7) + 1)
                pe.wait_ge(qkt_ready, c0 + 3)
                pe.wait_ge(qk_ready, rp + 4)
                turn_heads(tok(B["ck"]), 4).then_inc(qkt_done, 1)
                pe.wait_ge(diff_normed, 1)
                turn_heads(xn[:, :, 512:D], 6).then_inc(ot_done, 1)

                def before(tt):
                    pe.wait_ge(act_evac, e0 + 10 + 2 * tt - (0 if tt else 0))

                def ready(i, tt):
                    if tt == 0 and i in (0, 2):
                        pe.wait_ge(bt_lo_done, bt0[k] + 1 + i // 2)

                def after(i):
                    if i == 0:
                        pe.wait_ge(qkt_ready, c0 + 4)
                        dil_scores(0)
                        dil_scores(1)
                    if i == 1:
                        turn_probs(g0 + 8)
                        turn_probs(g0 + 9)
                        dil_scores(2)
                        dil_scores(3)
                        pe.wait_ge(act_evac, e0 + 12)
                        dil_values(0)
                        dil_values(1)
                        turn_probs(g0 + 10)
                        turn_probs(g0 + 11)
                        dil_values(2)
                        dil_values(3)
                        pe.wait_ge(o_ready, r0 + 6)
                        turn_heads(xn[:, :, 0:512], 4).then_inc(ot_done, 1)

                product(n0 + 12, 4, in_bt, before, ready, after)

            pe.wait_ge(id_in, 16)
            seen = {"pool_attn": 0}
            f = 0
            for k, kind in enumerate(program):
                transpose_x(turn0[k])
                if kind == "ffn":
                    ffn(f, k, first_piece[k])
                    f += 1
                if kind == "pool_attn":
                    pool_attn(k, seen[kind])
                    seen[kind] += 1
                if kind == "dil_diff":
                    dil_diff(k)
                if kind == "delta_ret":
                    delta_ret(k)


def up_pieces(w, cols):
    import numpy as np
    w = w[:, cols]
    return w.reshape(-1, 4, P, 512).transpose(0, 2, 1, 3).reshape(-1, P, PIECE)


def down_pieces(w):
    return w.reshape(-1, 2, P, 1024).transpose(0, 2, 1, 3).reshape(-1, P, PIECE)


def ffn_pieces(w_up, w_down):
    import numpy as np
    ups = []
    for c in range(NCH):
        cols = np.r_[c * CH:(c + 1) * CH, DFF + c * CH:DFF + (c + 1) * CH]
        ups.append(up_pieces(w_up, cols))
    downs = down_pieces(w_down)
    order = [ups[0]]
    for c in range(1, NCH):
        order += [ups[c], downs[c - 1:c]]
    return order + [downs[NCH - 1:]]


def first_block_pieces(a, i):
    w = a["w_in"][i]
    u, q, k, v, gl = w[:, :512], w[:, 512:1024], w[:, 1024:1536], w[:, 1536:2048], w[:, 2048:]
    out = [up_pieces(m, slice(None)) for m in (u, q, k, v)]
    out += [up_pieces(gl, slice(c * 512, (c + 1) * 512)) for c in range(4)]
    return out + [down_pieces(a[name][i]) for name in ("w_branch_pool", "w_branch_attn", "w_out")]


def rope_table(width):
    import numpy as np
    half = width // 2
    inv = np.float32(1.0) / np.power(np.float32(10000.0), np.arange(half, dtype=np.float32) * np.float32(2.0 / width))
    ang = (np.arange(SEQ, dtype=np.float32)[:, None] * inv.astype(np.float32)[None, :]).astype(np.float64)
    cos, sin = np.cos(ang), np.sin(ang)
    tab = np.stack([np.concatenate([cos, cos], 1), np.concatenate([-sin, sin], 1)])
    return tab.reshape(2, TT, P, width).transpose(2, 0, 1, 3).reshape(P, -1).astype(np.float32)


def two_tiles(m):
    import numpy as np
    return np.concatenate([m[:P, :P], m[P:, :]], 1)


def pool_means():
    import numpy as np
    out = []
    for w in (2, 4, 8, 16):
        m = np.zeros((SEQ, SEQ), np.float64)
        for q in range(SEQ):
            lo = max(q + 1 - w, 0)
            m[q, lo:q + 1] = 1.0 / (q + 1 - lo)
            m[q, q] -= 1.0
        mt = m.T
        out.append(np.concatenate([mt[:P, :], mt[P:, P:]], 1))
    return np.concatenate(out, 1).astype(np.float32)


def dil_diff_pieces(w, w_out):
    out = [up_pieces(w, slice(c * 512, (c + 1) * 512)) for c in (3, 4, 5, 0, 1, 2)]
    return out + [down_pieces(w_out[512:]), down_pieces(w_out[:512])]


def delta_ret_pieces(w, w_out):
    out = [up_pieces(w, slice(c, c + 512)) for c in (512, 0, 1024, 1536, 2056, 2568, 3080)]
    return out + [down_pieces(w_out[512:]), down_pieces(w_out[:512])]


def delta_ret_constants():
    import numpy as np
    i, j = np.arange(P)[:, None], np.arange(P)[None, :]
    same = i // 64 == j // 64
    f = lambda m: np.asarray(m, np.float32)
    levels = [f((i >> (l + 1) == j >> (l + 1)) & ((i >> l) % 2 == 0) & ((j >> l) % 2 == 1)) for l in range(6)]
    gamma = 1.0 - 2.0 ** (-5.0 - np.arange(4, dtype=np.float64))
    d = np.arange(SEQ)[None, :] - np.arange(P)[:, None]
    ret = [f(np.where(d >= 0, g ** np.maximum(d, 0), 0.0)) for g in gamma]
    return {"g_ones": f(np.ones((P, P))), "g_before": f((i <= j) & same), "g_after": f((i > j) & same),
            "g_sub": np.concatenate([f((i < 64) & (j >= 0)), f((i >= 64) & (j >= 0))], 1),
            "g_below": f(np.where((i <= j) & same, 0.0, NEG)), "g_level": np.concatenate(levels, 1),
            "g_ret": np.concatenate(ret, 1), "g_rope": rope_table(64), "g_zeros": np.zeros((P, 12), np.float32)}


def constants():
    import numpy as np
    q, k = np.arange(SEQ)[:, None], np.arange(SEQ)[None, :]
    causal = two_tiles(np.where(k <= q, 0.0, NEG).astype(np.float32))
    dist = q - k
    count = ((dist >= 0) & (dist <= 128)) + 0.0 + ((dist >= 0) & (dist % 4 == 0)) + ((dist >= 0) & (dist % 16 == 0))
    log_count = two_tiles(np.where(count > 0, np.log(np.maximum(count, 1)), NEG).astype(np.float32))
    return {"b_mask": causal, "b_mask_dil": log_count, "b_rope": rope_table(64), "b_rope_wide": rope_table(128),
            "ident": np.eye(P, dtype=np.float32), "a_pool_mean": pool_means(), "a_mask": causal,
            "a_rope": rope_table(64)}


def kernel(**inputs):
    import numpy as np
    import concourse.bacc as bacc
    from concourse.bass_utils import run_bass_kernel_spmd

    a = {k: np.asarray(v) for k, v in inputs.items()}
    program = PROGRAM
    first = lambda i: [ffn_pieces(a["ffn1_w_gate_up"][i], a["ffn1_w_down"][i]), first_block_pieces(a, i),
                       ffn_pieces(a["ffn2_w_gate_up"][i], a["ffn2_w_down"][i])]
    second = lambda i, mixer: [ffn_pieces(a[f"l{i}_ffn1_w_up_2"], a[f"l{i}_ffn1_w_down_2"]),
                               mixer(a[f"l{i}_w_in_2"], a[f"l{i}_w_out_2"]),
                               ffn_pieces(a[f"l{i}_ffn2_w_up_2"], a[f"l{i}_ffn2_w_down_2"])]
    phases = first(0) + first(1) + second(0, delta_ret_pieces) + second(1, dil_diff_pieces)
    gains = [a[n][i] for i in range(2) for n in ("ffn1_norm", "mix_norm", "ffn2_norm")]
    gains += [a[f"l{i}_{n}_norm_2"] for i in range(2) for n in ("ffn1", "mix", "ffn2")]
    if USE is not None:
        phases, gains = [phases[i] for i in USE], [gains[i] for i in USE]
    weights = np.concatenate([m for phase in phases for m in phase])
    conv = np.concatenate([a["l0_conv_w_2"][:, c:c + 512] for c in (512, 0, 1024)], 1)
    arrays = {"x": a["x"].reshape(SEQ, D), "weights": weights, "gains": np.stack(gains + [a["final_norm_2"]]),
              "g_gdn_norm": a["l0_gdn_norm_2"][None, :],
              "g_conv": conv.reshape(4, 12, P).transpose(2, 1, 0).reshape(P, 48),
              "g_alog_dt": np.concatenate([a["l0_a_log_2"], a["l0_dt_bias_2"]])[None, :],
              "g_ba": a["l0_w_in_2"][:, 2048:2056].reshape(KT, P, 8).transpose(1, 0, 2).reshape(P, KT * 8),
              "b_lambdas": np.concatenate([a["l1_lambda_" + n + "_2"] for n in ("q1", "k1", "q2", "k2")])[None, :],
              "b_diff_norm": a["l1_diff_norm_2"][None, :],
              "a_pool_w": a["pool_w"].transpose(0, 2, 1, 3).reshape(2, P, 512),
              "a_pool_scale": a["pool_scale"].reshape(2, 4, P).transpose(0, 2, 1),
              "a_qk_norm": np.concatenate([a["q_norm"], a["k_norm"]], 1).reshape(2, 1, 128),
              "a_b_gate": a["b_gate"].reshape(2, 1, 2048)}
    arrays.update(constants())
    arrays.update(delta_ret_constants())
    nc = bacc.Bacc("TRN2", target_bir_lowering=False, num_devices=1)
    tensors = {}
    for name in arrays:
        arrays[name] = np.ascontiguousarray(arrays[name])
        tensors[name] = nc.dram_tensor(name + "_dram", arrays[name].shape, mybir.dt.from_np(arrays[name].dtype), kind="ExternalInput").ap()
    tensors["out"] = nc.dram_tensor("out_dram", (SEQ, D), F32, kind="ExternalOutput").ap()
    build(nc, program, tensors)
    r = run_bass_kernel_spmd(nc, [{k + "_dram": v for k, v in arrays.items()}], core_ids=[0])
    return r.results[0]["out_dram"].reshape(1, SEQ, D)
```

```python
from contextlib import ExitStack
import math

import concourse.bass as bass
from concourse import mybir

F32 = mybir.dt.float32
F32R = mybir.dt.float32r
ALU = mybir.AluOpType
ACT = mybir.ActivationFunctionType
AX_X = mybir.AxisListType.X

P = 128
SEQ = 256
TT = SEQ // P
D = 1024
KT = D // P
DFF = 2816
LAMBDA_INIT = 0.8 - 0.6 * math.exp(-0.3)
DIL_SCALE = 128 ** -0.5
MIX_FLOATS = 21760
CH = 256
NCH = DFF // CH
EPS = 1e-6
NEG = -1e30
PIECE = 2048
SLOTS = 3

def starts(program, per_phase):
    out = [0]
    for kind in program:
        out.append(out[-1] + per_phase[kind])
    return out


NORMED = {"ffn": 0, "pool_attn": 0, "delta_ret": 1, "dil_diff": 0}
N_PARAMS = {"ffn": 0, "pool_attn": 8, "delta_ret": 14, "dil_diff": 6}
ROPES = {"ffn": 0, "pool_attn": 2, "delta_ret": 1, "dil_diff": 4}
QK_TURNS = {"ffn": 0, "pool_attn": 2, "delta_ret": 0, "dil_diff": 4}
O_TURNS = {"ffn": 0, "pool_attn": 1, "delta_ret": 2, "dil_diff": 2}
BT_SPLITS = {"ffn": 0, "pool_attn": 2, "delta_ret": 2, "dil_diff": 2}
TURNS = {"ffn": 1, "pool_attn": 2, "delta_ret": 1, "dil_diff": 1}
PRODUCTS = {"ffn": 1, "pool_attn": 3, "delta_ret": 1, "dil_diff": 1}
CHUNKS = {"ffn": 0, "pool_attn": 8, "delta_ret": 4, "dil_diff": 6}
ACT_EVACS = {"ffn": 0, "pool_attn": 8, "delta_ret": 8, "dil_diff": 12}
MAPS = {"ffn": 0, "pool_attn": 8, "delta_ret": 0, "dil_diff": 12}
ROUNDS = {"ffn": 0, "pool_attn": 2, "delta_ret": 0, "dil_diff": 6}
HEAD_NORMS = {"ffn": 0, "pool_attn": 2, "delta_ret": 4, "dil_diff": 1}
PROGRAM = ["ffn", "pool_attn", "ffn"] * 2 + ["ffn", "delta_ret", "ffn", "ffn", "dil_diff", "ffn"]
USE = None
PIECES = {"ffn": 3 * NCH, "pool_attn": 24, "delta_ret": 18, "dil_diff": 16}


def build(nc, program, t):
    n_pieces = sum(PIECES[kind] for kind in program)
    first_piece = starts(program, PIECES)
    turn0 = starts(program, TURNS)
    out0 = starts(program, PRODUCTS)
    chunk0 = starts(program, CHUNKS)
    evac0 = starts(program, ACT_EVACS)
    map0 = starts(program, MAPS)
    round0 = starts(program, ROUNDS)
    head_norm0 = starts(program, HEAD_NORMS)
    rope0 = starts(program, ROPES)
    turned0 = starts(program, QK_TURNS)
    o_turn0 = starts(program, O_TURNS)
    bt0 = starts(program, BT_SPLITS)

    with ExitStack() as ctx:
        def sb(name, shape, dt=F32):
            return ctx.enter_context(nc.sbuf_tensor(name, shape, dt))

        def sem(name):
            return ctx.enter_context(nc.semaphore(name))

        bank = [ctx.enter_context(nc.psum_tensor(f"bank{i}", [P, 512], F32)) for i in range(8)]

        w_raw = [sb(f"w_raw{s}", [P, PIECE]) for s in range(SLOTS)]
        w_hi = [sb(f"w_hi{s}", [P, PIECE], F32R) for s in range(SLOTS)]
        w_lo = [sb(f"w_lo{s}", [P, PIECE], F32R) for s in range(SLOTS)]
        x = sb("x", [P, TT, D])
        xn = sb("xn", [P, TT, D])
        gain = sb("gain", [P, (len(program) + 1) * KT])
        ident = sb("ident", [P, P])
        minus_half = sb("minus_half", [P, 16])
        stat = sb("stat", [P, 3, TT])
        xt_hi = sb("xt_hi", [P, KT, SEQ], F32R)
        xt_lo = sb("xt_lo", [P, KT, SEQ], F32R)
        gate = sb("gate", [P, TT, CH])
        hid = sb("hid", [P, TT, CH])
        ht_hi = sb("ht_hi", [P, 2, SEQ], F32R)
        ht_lo = sb("ht_lo", [P, 2, SEQ], F32R)

        bt_hi = sb("bt_hi", [P, 4, SEQ], F32R)
        bt_lo = sb("bt_lo", [P, 4, SEQ], F32R)
        mix = sb("mix", [P, MIX_FLOATS])
        expsum = sb("expsum", [P, 2, TT, 8])
        negmax = sb("negmax", [P, 2, TT])
        hstat = sb("hstat", [P, 3, 16])

        def carve(sizes):
            parts, at = {}, 0
            for name, size in sizes.items():
                parts[name] = mix[:, at:at + size]
                at += size
            assert at <= MIX_FLOATS, at
            return parts

        landed = [sem(f"weights_landed{s}") for s in range(SLOTS)]
        hi_done = sem("hi_done")
        lo_done = sem("lo_done")
        used = sem("piece_used")
        x_in = [sem(f"x_in{tt}") for tt in range(TT)]
        first_landed = [sem(f"first_piece_landed{q}") for q in range(4)]
        first_hi = sem("first_piece_hi")
        first_lo = sem("first_piece_lo")
        merged_ready = sem("branches_merged")
        id_in = sem("ident_in")
        gain_in = sem("gain_in")
        x_ready = sem("x_ready")
        ss_done = sem("squares_summed")
        xn_ready = sem("xn_ready")
        xt_done = sem("xt_transposed")
        xt_hi_done = sem("xt_hi_done")
        xt_lo_done = sem("xt_lo_done")
        up_done = sem("up_done")
        gate_ready = sem("gate_ready")
        hid_ready = sem("hid_ready")
        ht_done = sem("ht_transposed")
        ht_hi_done = sem("ht_hi_done")
        ht_lo_done = sem("ht_lo_done")
        out_done = sem("out_product_done")
        dve_step = sem("dve_step")
        stored = sem("stored")
        params_in = sem("mixer_params_in")
        proj_done = sem("chunk_tile0_done")
        act_evac = sem("chunk_tile_taken_by_act")
        gate_added = sem("gate_bias_added")
        hsq_done = sem("head_squares_done")
        hmean_ready = sem("head_mean_ready")
        hrstd_ready = sem("head_rstd_ready")
        diff_done = sem("pool_difference_done")
        diff_ready = sem("pool_difference_ready")
        y_done = sem("pool_product_done")
        bt_hi_done = sem("bt_hi_done")
        bt_lo_done = sem("bt_lo_done")
        qk_ready = sem("qk_roped")
        qkt_done = sem("qk_transposed")
        qkt_ready = sem("qk_transpose_ready")
        s_done = sem("scores_done")
        s_masked = sem("scores_masked")
        max_ready = sem("max_ready")
        exp_done = sem("exp_done")
        pt_done = sem("probs_transposed")
        pt_ready = sem("probs_transpose_ready")
        pv_done = sem("pv_done")
        o_ready = sem("attention_round_ready")
        ot_done = sem("attention_transposed")
        gates_ready = sem("gates_ready")
        branch_ready = sem("branch_gated")
        M = {name: sem("m_" + name) for name in (
            "ba_hi", "ba_split", "ba_done", "abs_ready", "exps_ready", "softplus_ready", "g_ready", "ug_ready", "sums_done",
            "gcum_copied", "e4_ready", "diff_done", "diff_ready", "decay_ready", "pads_zero", "ct_ready", "conv_ready",
            "co_ready", "co_turned", "tm_ready", "normed", "kb_ready", "kt_turned", "kt_ready", "kbt_turned", "kbt_ready",
            "qt_turned", "qt_ready", "qd_ready", "qdt_turned", "qdt_ready", "at_done", "at_ready", "qk_done", "qk_masked",
            "xt0_ready", "x0_turned", "x0_ready", "level_masked", "t1_done", "t1_ready", "y_done", "x_updated",
            "vb_ready", "kbe_ready", "kd_ready", "u_done", "u_ready", "wt_done", "wt_ready", "rqk_turned", "rqk_ready",
            "rs_done", "rs_ready", "ro_done", "ro_ready", "oa_ready", "sq_ready", "half_normed", "vw_done", "vn_ready",
            "ds_done", "s_ready", "o_done", "gz_ready")}
        ba_hi = sb("ba_hi", [P, KT * 8], F32R)
        ba_lo = sb("ba_lo", [P, KT * 8], F32R)
        lam_sums = sem("lambda_sums")
        lam_exp = sem("lambda_exponentials")
        diff_squared = sem("diff_ready_to_square")
        diff_normed = sem("diff_normed")
        mean_ready = sem("mean_square_ready")
        rstd_ready = sem("rstd_ready")
        half_ready = sem("minus_half_ready")

        block = ctx.enter_context(nc.Block())
        norms = len(program) + 1
        normed0 = starts(program, NORMED)
        late = [not NORMED[kind] for kind in program] + [False]

        def params_at(k):
            return 16 * sum(N_PARAMS[kind] for kind in program[:k + 1])

        def hidden_parts(c):
            if isinstance(c, int) and c == NCH - 1:
                return bt_hi[:, 0:2, :], bt_lo[:, 0:2, :]
            return ht_hi[:, :, :], ht_lo[:, :, :]

        def up_view(w, k):
            return w[:, k * 512:(k + 1) * 512]

        def down_view(w, k, h):
            return w[:, k * 1024 + h * 512:k * 1024 + (h + 1) * 512]

        def retention_probs(h):
            buf = G["qt_pr"] if h < 2 else G["decay_oa"]
            return buf[:, (h % 2) * 384:(h % 2) * 384 + 384]

        def psum3(b, k):
            return bank[b][:, :].rearrange("p (k q) -> p k q", k=k)

        A = carve(dict(probs=768, probs_t=768, u=1024, q=1024, k=1024, v=1024, sq=1024, rot=1024, qt=1024,
                       kt=1024, gates=4096, pool_w=512, pool_scale=4, qk_norm=128, pool_mean=1536,
                       mask=384, rope=256, rope_g=512))
        B = carve(dict(probs=768, probs_t=768, cq=1024, ck=1024, cv=1024, dq=1024, dk=1024, dv=1024, rot=1024,
                       cqt=1024, ckt=1024, dqt=1024, dkt=1024, diff=1024, sq=1024, prod=256,
                       mask=384, mask_dil=384, rope=256, rope_wide=512, lambdas=256, diff_norm=128, lam=8))
        B_PARAMS = ("mask", "mask_dil", "rope", "rope_wide", "lambdas", "diff_norm")
        G = carve(dict(ct_co=4120, k_kd=1024, q_qd_u=1024, v_vb=1024, kb_kbe=1024, gz=1024, rqk_ob=1024, rv=1024,
                       rg=1024, decay_oa=1024, kt_rt=1024, qt_pr=1024, kbt_wt=1024, qdt=1024,
                       ones=128, before=128, after=128, sub=256, below=128, level=768, ret=1024, rope=256,
                       gdn_norm=128, conv=48, alog_dt=8, ba=64, ab=64, gates=64, e4=32, gc=8))
        G_PARAMS = ("ones", "before", "after", "sub", "below", "level", "ret", "rope", "gdn_norm", "conv", "alog_dt", "ba")
        ct = [G["ct_co"][:, i * 1036:(i + 1) * 1036].rearrange("p (c q) -> p c q", c=4) for i in range(2)]
        co = [G["ct_co"][:, 2072 + i * 1024:2072 + (i + 1) * 1024].rearrange("p (c q) -> p c q", c=4) for i in range(2)]
        mats = lambda v: v.rearrange("p (t h q) -> p t h q", t=TT, h=4)
        inv, inv_t, prod1, lev = (mats(G["ct_co"][:, i * 1024:(i + 1) * 1024]) for i in range(4))
        at_m = mats(xn[:, 0, :])
        qk_m = mats(xn[:, 1, :])
        state = gate[:, :, :].rearrange("p t c -> p (t c)").rearrange("p (h e) -> p h e", h=4)
        v_new = hid[:, :, :].rearrange("p t c -> p (t c)").rearrange("p (h e) -> p h e", h=4)
        A_PARAMS = ("pool_w", "pool_scale", "qk_norm", "pool_mean", "mask", "rope")
        tok = lambda v, d=512: v.rearrange("p (t d) -> p t d", t=TT)
        heads = lambda v, w=64: v.rearrange("p (t h d) -> p t h d", t=TT, d=w)

        def causal_map(g, q_t, k_t, off, width):
            return [(q_t[off:off + width, 0:P], k_t[off:off + width, 0:P]),
                    (q_t[off:off + width, P:SEQ], k_t[off:off + width, 0:SEQ])]

        @block.sync
        def _(sp):
            sp.dma_start(x[:, 0, :], t["x"][0:P, :]).then_inc(x_in[0], 16)
            for q in range(4):
                sp.dma_start(w_raw[0][:, q * 512:(q + 1) * 512], t["weights"][0][:, q * 512:(q + 1) * 512]).then_inc(first_landed[q], 16)
            for tt in range(1, TT):
                sp.dma_start(x[:, tt, :], t["x"][tt * P:(tt + 1) * P, :]).then_inc(x_in[tt], 16)
            for s in range(1, SLOTS):
                sp.dma_start(w_raw[s][:, :], t["weights"][s]).then_inc(landed[s], 16)
            rounds = n_pieces // SLOTS
            with sp.Fori(1, rounds) as i:
                for s in range(SLOTS):
                    sp.wait_ge(lo_done, i * SLOTS + (s + 1 - SLOTS))
                    sp.dma_start(w_raw[s][:, :], t["weights"][i * SLOTS + s]).then_inc(landed[s], 16)
            for m in range(rounds * SLOTS, n_pieces):
                s = m % SLOTS
                sp.wait_ge(lo_done, m + 1 - SLOTS)
                sp.dma_start(w_raw[s][:, :], t["weights"][m]).then_inc(landed[s], 16)
            for tt in range(TT):
                sp.wait_ge(xn_ready, TT * normed0[-1] + tt + 1)
                sp.dma_start(t["out"][tt * P:(tt + 1) * P, :], xn[:, tt, :]).then_inc(stored, 16)
            sp.wait_ge(stored, 16 * TT)

        @block.gpsimd
        def _(pool):
            def rstd(k, tt):
                pool.wait_ge(mean_ready, TT * k + tt + 1)
                nc.gpsimd.tensor_tensor(stat[:, 2, tt:tt + 1], stat[:, 1, tt:tt + 1], minus_half[:, 0:1], ALU.pow).then_inc(rstd_ready, 1)

            pool.dma_start(ident[:, :], t["ident"]).then_inc(id_in, 16)
            pool.dma_start(gain[:, :], t["gains"]).then_inc(gain_in, 16)
            pool.memset(minus_half[:, :], -0.5).then_inc(half_ready, 1)
            pool.wait_ge(half_ready, 1)
            def head_rstd(i, n):
                pool.wait_ge(hmean_ready, i + 1)
                nc.gpsimd.tensor_tensor(hstat[:, 2, 0:n], hstat[:, 1, 0:n], minus_half[:, 0:n], ALU.pow).then_inc(hrstd_ready, 1)

            def load_pool_attn(i):
                for name in A_PARAMS:
                    src = t["a_" + name][i] if name in ("pool_w", "pool_scale", "qk_norm") else t["a_" + name]
                    pool.dma_start(A[name], src.to_broadcast([P, 128]) if name == "qk_norm" else src).then_inc(params_in, 16)
                for tt in range(TT):
                    pool.dma_start(tok(A["gates"])[:, tt, :], t["a_b_gate"][i].to_broadcast([P, 2048])).then_inc(params_in, 16)

            def load_dil_diff():
                for name in B_PARAMS:
                    src = t["b_" + name]
                    pool.dma_start(B[name], src.to_broadcast([P, src.shape[1]]) if src.shape[0] == 1 else src).then_inc(params_in, 16)

            def load_delta_ret():
                for name in G_PARAMS:
                    src = t["g_" + name]
                    pool.dma_start(G[name], src.to_broadcast([P, src.shape[1]]) if src.shape[0] == 1 else src).then_inc(params_in, 16)
                for _ in range(2):
                    pool.dma_start(ct[_][:, :, 0:3], t["g_zeros"].rearrange("p (c q) -> p c q", c=4)).then_inc(params_in, 16)

            def delta_ret(k):
                h0 = head_norm0[k]
                head_rstd(h0, 8)
                head_rstd(h0 + 1, 8)
                for l in range(1, 6):
                    if l == 1:
                        pool.wait_ge(M["x0_ready"], 1)
                    else:
                        pool.wait_ge(M["t1_done"], TT * (l - 1))
                    m = G["level"][:, l * P:(l + 1) * P].unsqueeze(1).broadcast_to([P, 8, P])
                    nc.gpsimd.tensor_tensor(lev.rearrange("p t h q -> p (t h) q"), at_m.rearrange("p t h q -> p (t h) q"),
                                            m, ALU.mult).then_inc(M["level_masked"], 1)
                head_rstd(h0 + 2, 8)
                head_rstd(h0 + 3, 8)

            seen = {"pool_attn": 0, "delta_ret": 0, "dil_diff": 0}

            def load_params(k):
                kind = program[k] if k < len(program) else "ffn"
                if kind == "pool_attn":
                    load_pool_attn(seen[kind])
                if kind == "dil_diff":
                    load_dil_diff()
                if kind == "delta_ret":
                    load_delta_ret()
                if kind != "ffn":
                    seen[kind] += 1

            load_params(0)
            for k in range(norms):
                for tt in range(TT):
                    rstd(k, tt)
                if k == len(program):
                    break
                if k == len(program) - 1:
                    pool.wait_ge(params_in, params_at(k))
                    pool.dma_start(mix[:, 0:D], t["final_gain"].to_broadcast([P, D])).then_inc(params_in, 16)
                if program[k] == "ffn":
                    load_params(k + 1)
                if program[k] == "pool_attn":
                    head_rstd(head_norm0[k], 16)
                    head_rstd(head_norm0[k] + 1, 16)
                if program[k] == "dil_diff":
                    head_rstd(head_norm0[k], 8)
                if program[k] == "delta_ret":
                    delta_ret(k)

        @block.scalar
        def _(act):
            def split_hi(m, s, skip=False):
                if m == 0:
                    for q in range(4):
                        part = slice(q * 512, (q + 1) * 512)
                        act.wait_ge(first_landed[q], 16)
                        nc.scalar.activation(w_hi[0][:, part], w_raw[0][:, part], ACT.Copy).then_inc(
                            hi_done if q == 3 else first_hi, 1)
                    return
                act.wait_ge(landed[s], landed_count(m, s))
                if not skip:
                    act.wait_ge(used, m + (1 - SLOTS))
                nc.scalar.activation(w_hi[s][:, :], w_raw[s][:, :], ACT.Copy).then_inc(hi_done, 1)

            def landed_count(m, s):
                return 16 * (m // SLOTS + (1 if s else 0))

            def squares(k):
                for tt in range(TT):
                    act.wait_ge(x_ready, 4 * (k - 1) + 2 * tt + 2) if k else act.wait_ge(x_in[tt], 16)
                    nc.scalar.activation(xn[:, tt, :], x[:, tt, :], ACT.Square,
                                         accum_out=stat[:, 0, tt:tt + 1]).then_inc(ss_done, 1)

            def xt_high(turn, norm=None, halves=range(4)):
                for j in halves:
                    tt, g = j // 2, j % 2
                    act.wait_ge(xt_done, 4 * turn + j + 1)
                    toks = slice(tt * P, (tt + 1) * P)
                    if norm is None:
                        nc.scalar.activation(xt_hi[:, 4 * g:4 * g + 4, toks], psum3(4 + j, 4), ACT.Copy).then_inc(xt_hi_done, 1)
                        continue
                    for q in range(4):
                        c = norm * KT + 4 * g + q
                        ins = nc.scalar.activation(xt_hi[:, 4 * g + q, toks], psum3(4 + j, 4)[:, q, :], ACT.Copy,
                                                   scale=gain[:, c:c + 1])
                    ins.then_inc(xt_hi_done, 1)

            def ffn(f, k):
                base = first_piece[k]

                def gates(c):
                    for tt in range(TT):
                        if tt == 0:
                            act.wait_ge(up_done, c + (NCH * f + 1))
                        else:
                            act.wait_ge(used, base + 2 if isinstance(c, int) and c == 0 else c * SLOTS + (base + 1))
                        b = bank[tt if isinstance(c, int) and c == 0 else 4 + tt]
                        nc.scalar.activation(gate[:, tt, :], b[:, 0:CH], ACT.Silu, scale=stat[:, 2, tt:tt + 1]).then_inc(gate_ready, 1)

                def ht_high(c):
                    act.wait_ge(ht_done, c + (NCH * f + 1))
                    nc.scalar.activation(hidden_parts(c)[0], bank[6][:, :].rearrange("p (k q) -> p k q", k=2),
                                         ACT.Copy).then_inc(ht_hi_done, 1)

                def step(c, peeled=True):
                    m = base + 2 - SLOTS + c * SLOTS
                    ht_high(c - 1)
                    ahead(m, 2, c)
                    ahead(m, 3, c)
                    gates(c)
                    ahead(m, 4, c)

                def ahead(m, j, c):
                    s = (base + 2 + j) % SLOTS
                    if isinstance(c, int):
                        if m + j < n_pieces:
                            split_hi(m + j, s)
                        return
                    q = (base - 1 + j) // SLOTS
                    act.wait_ge(landed[s], c * 16 + 16 * (q + (1 if s else 0)))
                    act.wait_ge(used, c * SLOTS + (base - 1 + j + 1 - SLOTS))
                    nc.scalar.activation(w_hi[s][:, :], w_raw[s][:, :], ACT.Copy).then_inc(hi_done, 1)

                split_hi(base + 2, (base + 2) % SLOTS, base + 2 < SLOTS)
                act.wait_ge(rstd_ready, TT * (k + 1))
                gates(0)
                split_hi(base + 3, (base + 3) % SLOTS)
                step(1)
                with act.Fori(2, NCH - 1) as c:
                    step(c)
                step(NCH - 1)
                ht_high(NCH - 1)
                if base + 34 < n_pieces:
                    split_hi(base + 34, (base + 34) % SLOTS)

            def ahead(m):
                if m + 2 < n_pieces:
                    split_hi(m + 2, (m + 2) % SLOTS, m + 2 < SLOTS)

            def chunk_tile(k, j, tt, skipped):
                if tt == 0:
                    act.wait_ge(proj_done, chunk0[k] + j + 1 - skipped)
                else:
                    act.wait_ge(used, first_piece[k] + 2 * j + 2)

            def take(k, j, e, dst, func=ACT.Copy, skipped=0):
                if j == 0:
                    act.wait_ge(rstd_ready, TT * (k + 1))
                for tt in range(TT):
                    chunk_tile(k, j, tt, skipped)
                    nc.scalar.activation(dst[:, tt, :], bank[2 * (j % 2) + tt][:, :], func,
                                         scale=stat[:, 2, tt:tt + 1] if late[k] else 1.0).then_inc(act_evac, 1)

            def exp_map(g, i):
                act.wait_ge(max_ready, g + 1)
                pr = A["probs"][:, (g % 2) * 384:(g % 2) * 384 + 384]
                for tt, cols in enumerate((slice(0, P), slice(P, 3 * P))):
                    ins = nc.scalar.activation(pr[:, cols], pr[:, cols], ACT.Exp, bias=negmax[:, g % 2, tt:tt + 1],
                                               accum_out=expsum[:, 0, tt, i:i + 1])
                ins.then_inc(exp_done, 1)

            def take_probs(g):
                act.wait_ge(pt_done, g + 1)
                if g >= 2:
                    act.wait_ge(pv_done, g - 1)
                nc.scalar.activation(A["probs_t"][:, (g % 2) * 384:(g % 2) * 384 + 384], bank[6][:, 0:384], ACT.Copy).then_inc(pt_ready, 1)

            def bt_high(i, src, scale=None):
                for b in range(2):
                    for r in range(2):
                        ins = nc.scalar.activation(bt_hi[:, 2 * b + r, :], psum3(src + b, 2)[:, r, :], ACT.Copy,
                                                   scale=1.0 if scale is None else scale[:, 2 * b + r:2 * b + r + 1])
                ins.then_inc(bt_hi_done, 1)

            def pool_attn(k, i):
                n0, e0, g0 = first_piece[k], evac0[k], map0[k]
                u, q, kk, v = (tok(A[name]) for name in ("u", "q", "k", "v"))
                for p in range(PIECES["pool_attn"]):
                    ahead(n0 + p)
                    if p == 1:
                        take(k, 0, e0, u)
                    if p == 3:
                        take(k, 1, e0 + 2, q)
                        act.wait_ge(act_evac, e0 + 4)
                        nc.scalar.activation(A["sq"], A["q"], ACT.Square).then_inc(hsq_done, 1)
                        act.wait_ge(diff_done, i + 1)
                        for b in range(2):
                            ins = nc.scalar.activation(A["qt"][:, b * 512:(b + 1) * 512], bank[4 + b][:, :], ACT.Copy)
                        ins.then_inc(diff_ready, 1)
                    if p == 5:
                        take(k, 2, e0 + 4, kk)
                        act.wait_ge(act_evac, e0 + 6)
                        act.wait_ge(qk_ready, 2 * i + 1)
                        nc.scalar.activation(A["sq"], A["k"], ACT.Square).then_inc(hsq_done, 1)
                        act.wait_ge(params_in, params_at(k))
                        act.wait_ge(y_done, i + 1)
                        bt_high(2 * i, 6, A["pool_scale"])
                    if p == 7:
                        take(k, 3, e0 + 6, v)
                        turned_qk(2 * i, "qt", 4)
                    if p == 8:
                        turned_qk(2 * i + 1, "kt", 6)
                    if 10 <= p <= 17:
                        take_probs(g0 + p - 10)
                    if 9 <= p <= 16:
                        exp_map(g0 + p - 9, p - 9)
                    if p == 16:
                        act.wait_ge(gate_added, 8 * i + 8)
                        nc.scalar.activation(A["gates"], A["gates"], ACT.Sigmoid).then_inc(gates_ready, 1)
                    if p == 17:
                        act.wait_ge(ot_done, i + 1)
                        bt_high(2 * i + 1, 4)
                    if p == 19:
                        xt_high(turn0[k] + 1)

            def copy_banks(b0, dst, ready):
                for b in range(2):
                    ins = nc.scalar.activation(dst[:, b * 512:(b + 1) * 512], bank[b0 + b][:, :], ACT.Copy)
                ins.then_inc(M[ready], 1)

            def delta_ret(k):
                n0, e0 = first_piece[k], evac0[k]
                gates, e4 = G["gates"], G["e4"]

                def take_channels(i):
                    act.wait_ge(used, n0 + 2 * i + 2)
                    if i == 2:
                        act.wait_ge(M["conv_ready"], 1)
                        act.wait_ge(M["co_turned"], 1)
                    b0 = 2 * (i % 2)
                    for b in range(2):
                        nc.scalar.activation(ct[i % 2][:, 2 * b:2 * b + 2, 3:259], psum3(b0 + b, 2), ACT.Copy)
                    for c in range(4):
                        ins = nc.scalar.activation(co[i % 2][:, c, :], psum3(b0 + c // 2, 2)[:, c % 2, :], ACT.Copy,
                                                   scale=G["conv"][:, (4 * i + c) * 4 + 3:(4 * i + c) * 4 + 4])
                    ins.then_inc(M["ct_ready"], 1)

                def silu_conv(i):
                    act.wait_ge(M["conv_ready"], i + 1)
                    nc.scalar.activation(co[i % 2], co[i % 2], ACT.Silu).then_inc(M["co_ready"], 1)

                def take_tokens(i, dst):
                    act.wait_ge(M["co_turned"], i + 1)
                    copy_banks(4, dst, "tm_ready")

                def square(i, src, need=None):
                    if need:
                        act.wait_ge(M[need[0]], need[1])
                    nc.scalar.activation(G["rg"] if i < 2 else G["rv"], src, ACT.Square).then_inc(hsq_done, 1)

                def take_t1(l):
                    for tt in range(TT):
                        act.wait_ge(M["t1_done"], TT * (l - 1) + tt + 1)
                        nc.scalar.activation(prod1[:, tt].rearrange("p h q -> p (h q)"), bank[4 + tt][:, :], ACT.Copy).then_inc(M["t1_ready"], 1)

                act.wait_ge(params_in, params_at(k))
                nc.scalar.activation(ba_hi[:, :], G["ba"], ACT.Copy).then_inc(M["ba_hi"], 1)
                for p in range(PIECES["delta_ret"]):
                    ahead(n0 + p)
                    if p == 0:
                        act.wait_ge(M["abs_ready"], 1)
                        nc.scalar.activation(gates[:, 24:32], gates[:, 16:24], ACT.Exp, scale=-1.0)
                        nc.scalar.activation(gates[:, 32:36], G["alog_dt"][:, 0:4], ACT.Exp)
                        nc.scalar.activation(gates[:, 48:56], gates[:, 40:48], ACT.Exp, scale=-1.0).then_inc(M["exps_ready"], 1)
                        act.wait_ge(M["exps_ready"], 1)
                        nc.scalar.activation(gates[:, 24:32], gates[:, 24:32], ACT.Ln, bias=1.0).then_inc(M["softplus_ready"], 1)
                    if p == 1:
                        act.wait_ge(M["gcum_copied"], 1)
                        nc.scalar.activation(e4, bank[5][:, 0:32], ACT.Exp).then_inc(M["e4_ready"], 1)
                        take_channels(0)
                    if p == 2:
                        act.wait_ge(M["diff_ready"], 1)
                        nc.scalar.activation(G["decay_oa"], G["decay_oa"], ACT.Exp).then_inc(M["decay_ready"], 1)
                    if p == 3:
                        silu_conv(0)
                        take_channels(1)
                        take_tokens(0, G["k_kd"])
                        square(0, G["k_kd"], ("tm_ready", 1))
                    if p == 5:
                        silu_conv(1)
                        take_channels(2)
                        take_tokens(1, G["q_qd_u"])
                        square(1, G["q_qd_u"], ("tm_ready", 2))
                        act.wait_ge(M["kt_turned"], 1)
                        copy_banks(6, G["kt_rt"], "kt_ready")
                    if p == 6:
                        act.wait_ge(M["kbt_turned"], 1)
                        copy_banks(4, G["kbt_wt"], "kbt_ready")
                        act.wait_ge(M["qt_turned"], 1)
                        copy_banks(6, G["qt_pr"], "qt_ready")
                        silu_conv(2)
                    if p == 7:
                        take_tokens(2, G["v_vb"])
                        take(k, 3, e0, tok(G["gz"]), ACT.Silu, 3)
                    if p == 8:
                        act.wait_ge(M["qdt_turned"], 1)
                        copy_banks(6, G["qdt"], "qdt_ready")
                    if p == 9:
                        act.wait_ge(M["x0_turned"], 1)
                        copy_banks(4, inv.rearrange("p t h q -> p (t h q)"), "x0_ready")
                        take(k, 4, e0 + 2, tok(G["rqk_ob"]), ACT.Copy, 3)
                        take_t1(1)
                    if p == 10:
                        take_t1(2)
                    if p == 11:
                        take(k, 5, e0 + 4, tok(G["rv"]), ACT.Copy, 3)
                        take_t1(3)
                        act.wait_ge(M["rqk_turned"], 1)
                        copy_banks(6, G["kt_rt"], "rqk_ready")
                    if p == 12:
                        take_t1(4)
                    if p == 13:
                        take(k, 6, e0 + 6, tok(G["rg"]), ACT.Silu, 3)
                        take_t1(5)
                        act.wait_ge(M["ro_done"], 1)
                        copy_banks(6, G["rqk_ob"], "ro_ready")
                        act.wait_ge(M["ro_ready"], 1)
                        square(2, G["rqk_ob"])
                        act.wait_ge(M["u_done"], 1)
                        copy_banks(4, G["q_qd_u"], "u_ready")
                        act.wait_ge(M["wt_done"], 1)
                        copy_banks(6, G["kbt_wt"], "wt_ready")
                        act.wait_ge(ot_done, o_turn0[k] + 1)
                        bt_high(bt0[k], 4)
                    if p == 15:
                        for tt in range(TT):
                            act.wait_ge(M["o_done"], 2 * tt + 2)
                            nc.scalar.activation(G["decay_oa"][:, tt * 512:(tt + 1) * 512], bank[6 + tt][:, :], ACT.Copy).then_inc(M["oa_ready"], 1)
                        square(3, G["decay_oa"], ("oa_ready", TT))
                        act.wait_ge(ot_done, o_turn0[k] + 2)
                        bt_high(bt0[k] + 1, 4)

            def dil_diff(k):
                n0, e0, g0, c0 = first_piece[k], evac0[k], map0[k], turned0[k]
                order = ("dq", "dk", "dv", "cq", "ck", "cv")
                act.wait_ge(lam_sums, 1)
                nc.scalar.activation(B["lam"][:, 2:4], B["lam"][:, 0:2], ACT.Exp).then_inc(lam_exp, 1)
                for p in range(PIECES["dil_diff"]):
                    ahead(n0 + p)
                    if p % 2 and p < 12:
                        take(k, p // 2, e0 + p - 1, tok(B[order[p // 2]]))
                    if p == 3:
                        turned_qk(c0, "dqt", 4, B)
                    if p == 5:
                        turned_qk(c0 + 1, "dkt", 6, B)
                    if 7 <= p <= 10:
                        take_probs(g0 + 2 * (p - 7))
                        take_probs(g0 + 2 * (p - 7) + 1)
                    if 6 <= p <= 9:
                        exp_map(g0 + 2 * (p - 6), 2 * (p - 6))
                        exp_map(g0 + 2 * (p - 6) + 1, 2 * (p - 6) + 1)
                    if p == 10:
                        turned_qk(c0 + 2, "cqt", 4, B)
                    if p == 11:
                        act.wait_ge(diff_squared, 1)
                        nc.scalar.activation(B["sq"], B["diff"], ACT.Square).then_inc(hsq_done, 1)
                        turned_qk(c0 + 3, "ckt", 4, B)
                        act.wait_ge(ot_done, o_turn0[k] + 1)
                        bt_high(bt0[k], 6)
                    if p == 12:
                        exp_map(g0 + 8, 0)
                        exp_map(g0 + 9, 1)
                    if p == 13:
                        take_probs(g0 + 8)
                        take_probs(g0 + 9)
                        exp_map(g0 + 10, 2)
                        exp_map(g0 + 11, 3)
                        take_probs(g0 + 10)
                        take_probs(g0 + 11)
                        act.wait_ge(ot_done, o_turn0[k] + 2)
                        bt_high(bt0[k] + 1, 4)

            def turned_qk(c, name, b0, bufs=A):
                act.wait_ge(qkt_done, c + 1)
                for b in range(2):
                    ins = nc.scalar.activation(bufs[name][:, b * 512:(b + 1) * 512], bank[b0 + b][:, :], ACT.Copy)
                ins.then_inc(qkt_ready, 1)

            seen = {"pool_attn": 0}
            f = 0
            for k, kind in enumerate(program):
                if k == 0:
                    act.wait_ge(gain_in, 16)
                    xt_high(0, 0, (0, 1))
                    split_hi(0, 0, True)
                    xt_high(0, 0, (2, 3))
                    split_hi(1, 1, True)
                    squares(0)
                elif late[k]:
                    xt_high(turn0[k], k)
                    squares(k)
                else:
                    squares(k)
                    xt_high(turn0[k], k)
                if kind == "ffn":
                    ffn(f, k)
                    f += 1
                if kind == "pool_attn":
                    pool_attn(k, seen[kind])
                    seen[kind] += 1
                if kind == "dil_diff":
                    dil_diff(k)
                if kind == "delta_ret":
                    delta_ret(k)
            squares(norms - 1)

        @block.vector
        def _(dve):
            steps = [0]

            def link(ins):
                steps[0] += 1
                ins.then_inc(dve_step, 1)
                dve.wait_ge(dve_step, steps[0])

            def split_lo(m, s):
                if isinstance(m, int) and m == 0:
                    for q in range(4):
                        part = slice(q * 512, (q + 1) * 512)
                        dve.wait_ge(hi_done if q == 3 else first_hi, 1 if q == 3 else q + 1)
                        nc.vector.tensor_tensor(w_lo[0][:, part], w_raw[0][:, part], w_hi[0][:, part].bitcast(F32),
                                                ALU.subtract).then_inc(lo_done if q == 3 else first_lo, 1)
                    return
                dve.wait_ge(hi_done, m + 1)
                nc.vector.tensor_tensor(w_lo[s][:, :], w_raw[s][:, :], w_hi[s][:, :].bitcast(F32),
                                        ALU.subtract).then_inc(lo_done, 1)

            def mean_square(k, tt):
                dve.wait_ge(ss_done, TT * k + tt + 1)
                nc.vector.tensor_scalar(stat[:, 1, tt:tt + 1], stat[:, 0, tt:tt + 1], 1.0 / D, EPS, ALU.mult, ALU.add).then_inc(mean_ready, 1)

            def norm(k, tt):
                dve.wait_ge(rstd_ready, TT * k + tt + 1)
                rstd = stat[:, 2, tt:tt + 1]
                if k == norms - 1:
                    dve.wait_ge(params_in, params_at(len(program)) + 16)
                    nc.vector.scalar_tensor_tensor(out=xn[:, tt, :], in0=x[:, tt, :], scalar=rstd, in1=mix[:, 0:D],
                                                   op0=ALU.mult, op1=ALU.mult).then_inc(xn_ready, 1)
                else:
                    nc.vector.tensor_scalar(xn[:, tt, :], x[:, tt, :], rstd, None, ALU.mult).then_inc(xn_ready, 1)

            def xt_low(turn, norm=None, halves=range(4)):
                for j in halves:
                    tt, g = j // 2, j % 2
                    dve.wait_ge(xt_hi_done, 4 * turn + j + 1)
                    toks = slice(tt * P, (tt + 1) * P)
                    if norm is None:
                        nc.vector.tensor_tensor(xt_lo[:, 4 * g:4 * g + 4, toks], psum3(4 + j, 4),
                                                xt_hi[:, 4 * g:4 * g + 4, toks].bitcast(F32), ALU.subtract).then_inc(xt_lo_done, 1)
                        continue
                    for q in range(4):
                        c = norm * KT + 4 * g + q
                        ins = nc.vector.scalar_tensor_tensor(out=xt_lo[:, 4 * g + q, toks], in0=psum3(4 + j, 4)[:, q, :],
                                                             scalar=gain[:, c:c + 1], in1=xt_hi[:, 4 * g + q, toks].bitcast(F32),
                                                             op0=ALU.mult, op1=ALU.subtract)
                    ins.then_inc(xt_lo_done, 1)

            def ffn(f, k):
                base = first_piece[k]

                def hidden(c):
                    for tt in range(TT):
                        dve.wait_ge(gate_ready, c * TT + (TT * NCH * f + tt + 1))
                        b = bank[tt if isinstance(c, int) and c == 0 else 4 + tt]
                        nc.vector.scalar_tensor_tensor(out=hid[:, tt, :], in0=b[:, CH:2 * CH], scalar=stat[:, 2, tt:tt + 1],
                                                       in1=gate[:, tt, :], op0=ALU.mult, op1=ALU.mult).then_inc(hid_ready, 1)

                def ht_low(c):
                    dve.wait_ge(ht_hi_done, c + (NCH * f + 1))
                    nc.vector.tensor_tensor(hidden_parts(c)[1], bank[6][:, :].rearrange("p (k q) -> p k q", k=2),
                                            hidden_parts(c)[0].bitcast(F32), ALU.subtract).then_inc(ht_lo_done, 1)

                def ahead(j, c):
                    m = c * SLOTS + (base - 1 + j)
                    if not isinstance(c, int) or m < n_pieces:
                        split_lo(m, (base + 2 + j) % SLOTS)

                def step(c):
                    ht_low(c - 1)
                    ahead(2, c)
                    ahead(3, c)
                    hidden(c)
                    ahead(4, c)

                split_lo(base + 2, (base + 2) % SLOTS)
                dve.wait_ge(rstd_ready, TT * (k + 1))
                hidden(0)
                split_lo(base + 3, (base + 3) % SLOTS)
                step(1)
                with dve.Fori(2, NCH - 1) as c:
                    step(c)
                step(NCH - 1)
                ht_low(NCH - 1)

            def half_done(o, j, last_piece):
                if j < 3:
                    dve.wait_ge(out_done, 3 * o + j + 1)
                else:
                    dve.wait_ge(used, last_piece + 1)

            def add_to_x(k, o, scale, split=None):
                for j in range(4):
                    half_done(o, j, first_piece[k] + PIECES[program[k]] - 1)
                    xs = x[:, j // 2, (j % 2) * 512:(j % 2 + 1) * 512]
                    nc.vector.scalar_tensor_tensor(out=xs, in0=bank[j][:, :], scalar=scale, in1=xs,
                                                   op0=ALU.mult, op1=ALU.add).then_inc(x_ready, 1)
                    if j == 0 and split is not None and split < n_pieces:
                        split_lo(split, split % SLOTS)
                    if late[k + 1] and j:
                        xt_low(turn0[k + 1], k + 1, (j - 1,))
                    if not late[k + 1] and j == 2:
                        mean_square(k + 1, 0)
                if late[k + 1]:
                    xt_low(turn0[k + 1], k + 1, (3,))
                    for tt in range(TT):
                        mean_square(k + 1, tt)
                else:
                    norm(k + 1, 0)
                    mean_square(k + 1, 1)
                    norm(k + 1, 1)

            def ahead(m):
                if m + 2 < n_pieces:
                    split_lo(m + 2, (m + 2) % SLOTS)

            def delta_ret(k):
                n0, e0, h0 = first_piece[k], evac0[k], head_norm0[k]
                gates = G["gates"]
                per_head = lambda v: v.rearrange("p (n w) -> p n w", w=P)
                th = lambda v: v.unsqueeze(2).broadcast_to([P, 8, P])
                beta, e4, gc = gates[:, 56:64], G["e4"], G["gc"]
                eg, edec = e4[:, 0:8], e4[:, 8:16]
                conv = G["conv"]
                tab = G["rope"].rearrange("p (c t d) -> p c t d", c=2, t=TT)
                ret = G["ret"].rearrange("p (h q) -> p h q", h=4)

                def convolve(i):
                    dve.wait_ge(M["ct_ready"], i + 1)
                    for j in range(3):
                        for c in range(4):
                            w = (4 * i + c) * 4 + j
                            ins = nc.vector.scalar_tensor_tensor(out=co[i % 2][:, c, :], in0=ct[i % 2][:, c, j:j + SEQ],
                                                                 scalar=conv[:, w:w + 1], in1=co[i % 2][:, c, :],
                                                                 op0=ALU.mult, op1=ALU.add)
                        if j < 2:
                            link(ins)
                    ins.then_inc(M["conv_ready"], 1)

                def scaled(out, x, by, ready):
                    nc.vector.tensor_tensor(per_head(out), per_head(x), th(by), ALU.mult).then_inc(M[ready], 1)

                def update(l):
                    for tt in range(TT):
                        dve.wait_ge(M["y_done"], TT * (l - 1) + tt + 1)
                        if l < 5:
                            a = inv[:, tt].rearrange("p h q -> p (h q)")
                            nc.vector.tensor_tensor(a, a, bank[6 + tt][:, :], ALU.subtract)
                        a = inv_t[:, tt].rearrange("p h q -> p (h q)")
                        nc.vector.tensor_tensor(a, a, bank[4 + tt][:, :], ALU.subtract).then_inc(M["x_updated"], 1)

                def decay_scores(h):
                    dve.wait_ge(M["rs_done"], h + 1)
                    pr = retention_probs(h)
                    nc.vector.scalar_tensor_tensor(out=pr[:, 0:SEQ], in0=bank[6 + h % 2][:, 0:SEQ], scalar=0.125,
                                                   in1=ret[:, h, :], op0=ALU.mult, op1=ALU.mult)
                    nc.vector.scalar_tensor_tensor(out=pr[:, SEQ:384], in0=bank[6 + h % 2][:, SEQ:384], scalar=0.125,
                                                   in1=ret[:, h, 0:P], op0=ALU.mult, op1=ALU.mult).then_inc(M["rs_ready"], 1)

                def new_values(n):
                    tt, rows = n // 2, slice(64 * (n % 2), 64 * (n % 2) + 64)
                    dve.wait_ge(M["vw_done"], n)
                    nc.vector.tensor_tensor(v_new[rows].rearrange("p h e -> p (h e)"), tok(G["q_qd_u"])[rows, tt, :],
                                            bank[4][rows, :], ALU.subtract).then_inc(M["vn_ready"], 1)

                def next_state(n):
                    dve.wait_ge(M["ds_done"], n + 1)
                    if n == 0:
                        nc.vector.tensor_copy(state.rearrange("p h e -> p (h e)"), bank[5][:, :]).then_inc(M["s_ready"], 1)
                        return
                    el = e4[:, 16 + 8 * (n % 2) + 4 * (n // 2):]
                    for h in range(4):
                        ins = nc.vector.scalar_tensor_tensor(out=state[:, h, :], in0=state[:, h, :], scalar=el[:, h:h + 1],
                                                             in1=psum3(5, 4)[:, h, :], op0=ALU.mult, op1=ALU.add)
                    ins.then_inc(M["s_ready"], 1)

                dve.wait_ge(M["ba_hi"], 1)
                nc.vector.tensor_tensor(ba_lo[:, :], G["ba"], ba_hi[:, :].bitcast(F32), ALU.subtract).then_inc(M["ba_split"], 1)
                for p in range(PIECES["delta_ret"]):
                    ahead(n0 + p)
                    if p == 0:
                        dve.wait_ge(M["ba_done"], 1)
                        ba = bank[4][:, 0:16].rearrange("p (t c) -> p t c", t=TT)
                        g2 = lambda a: gates[:, a:a + 8].rearrange("p (t h) -> p t h", t=TT)
                        dt = G["alog_dt"][:, 4:8].unsqueeze(1).broadcast_to([P, TT, 4])
                        nc.vector.tensor_copy(g2(40), ba[:, :, 0:4])
                        link(nc.vector.tensor_tensor(g2(0), ba[:, :, 4:8], dt, ALU.add))
                        link(nc.vector.tensor_scalar(gates[:, 8:16], gates[:, 0:8], -1.0, None, ALU.mult))
                        nc.vector.tensor_tensor(gates[:, 16:24], gates[:, 0:8], gates[:, 8:16], ALU.max).then_inc(M["abs_ready"], 1)
                        dve.wait_ge(M["softplus_ready"], 1)
                        link(nc.vector.scalar_tensor_tensor(out=gates[:, 8:16], in0=gates[:, 0:8], scalar=0.0,
                                                            in1=gates[:, 24:32], op0=ALU.max, op1=ALU.add))
                        ea = gates[:, 32:36].unsqueeze(1).broadcast_to([P, TT, 4])
                        link(nc.vector.scalar_tensor_tensor(out=g2(0), in0=g2(8), scalar=-1.0, in1=ea, op0=ALU.mult, op1=ALU.mult))
                        link(nc.vector.tensor_scalar(gates[:, 48:56], gates[:, 48:56], 1.0, None, ALU.add))
                        nc.vector.reciprocal(beta, gates[:, 48:56]).then_inc(M["g_ready"], 1)
                        nc.vector.tensor_tensor(per_head(G["decay_oa"]), G["before"].unsqueeze(1).broadcast_to([P, 8, P]),
                                                th(gates[:, 0:8]), ALU.mult).then_inc(M["ug_ready"], 1)
                    if p == 1:
                        dve.wait_ge(M["sums_done"], 1)
                        nc.vector.tensor_copy(gc, bank[5][:, 0:8]).then_inc(M["gcum_copied"], 1)
                    if p == 2:
                        dve.wait_ge(M["diff_done"], 1)
                        dve.wait_ge(M["gcum_copied"], 1)
                        for i in range(8):
                            ins = nc.vector.scalar_tensor_tensor(out=per_head(G["decay_oa"])[:, i, :], in0=psum3(6 + i // 4, 4)[:, i % 4, :],
                                                                 scalar=gc[:, i:i + 1], in1=G["below"], op0=ALU.subtract, op1=ALU.add)
                        ins.then_inc(M["diff_ready"], 1)
                        convolve(0)
                    if p == 4:
                        head_norm(h0, G["rg"], 8, P, 1.0, EPS, per_head(G["k_kd"]))
                        scaled(G["kb_kbe"], G["k_kd"], beta, "kb_ready")
                        convolve(1)
                    if p == 6:
                        head_norm(h0 + 1, G["rg"], 8, P, float(P), P * EPS, per_head(G["q_qd_u"]))
                        nc.vector.tensor_copy(hstat[:, 0, 0:1], hstat[:, 1, 0:1]).then_inc(M["normed"], 1)
                        convolve(2)
                        dve.wait_ge(M["kbt_turned"], 1)
                        dve.wait_ge(M["kb_ready"], 1)
                        dve.wait_ge(M["e4_ready"], 1)
                        scaled(G["kb_kbe"], G["kb_kbe"], eg, "kbe_ready")
                        dve.wait_ge(M["kt_turned"], 1)
                        scaled(G["k_kd"], G["k_kd"], edec, "kd_ready")
                        dve.wait_ge(M["qt_turned"], 1)
                        scaled(G["q_qd_u"], G["q_qd_u"], eg, "qd_ready")
                    if p == 7:
                        dve.wait_ge(M["at_done"], 1)
                        dve.wait_ge(M["decay_ready"], 1)
                        for tt in range(TT):
                            ins = nc.vector.tensor_tensor(at_m[:, tt].rearrange("p h q -> p (h q)"), bank[6 + tt][:, :],
                                                          G["decay_oa"][:, tt * 512:(tt + 1) * 512], ALU.mult)
                        ins.then_inc(M["at_ready"], 1)
                        dve.wait_ge(M["at_ready"], 1)
                        flat = lambda v: v.rearrange("p t h q -> p (t h) q")
                        each = lambda v: v.unsqueeze(1).broadcast_to([P, 8, P])
                        dve.wait_ge(M["conv_ready"], 3)
                        dve.wait_ge(M["co_turned"], 3)
                        link(nc.vector.tensor_tensor(flat(inv_t), flat(at_m), each(G["level"][:, 0:P]), ALU.mult))
                        nc.vector.tensor_tensor(flat(inv_t), each(ident[:, :]), flat(inv_t), ALU.subtract).then_inc(M["xt0_ready"], 1)
                    if p == 8:
                        dve.wait_ge(M["tm_ready"], 3)
                        scaled(G["v_vb"], G["v_vb"], beta, "vb_ready")
                        dve.wait_ge(M["qk_done"], 1)
                        for tt in range(TT):
                            ins = nc.vector.tensor_tensor(qk_m[:, tt].rearrange("p h q -> p (h q)"), bank[4 + tt][:, :],
                                                          G["decay_oa"][:, tt * 512:(tt + 1) * 512], ALU.mult)
                        ins.then_inc(M["qk_masked"], 1)
                        dve.wait_ge(act_evac, e0 + 2)
                        gz = per_head(G["gz"])
                        nc.vector.tensor_tensor(gz, gz, each(G["gdn_norm"]), ALU.mult).then_inc(M["gz_ready"], 1)
                    if p == 10:
                        update(1)
                        dve.wait_ge(act_evac, e0 + 4)
                        rope(heads(G["rqk_ob"]), heads(G["rg"]), tab[:, 0], tab[:, 1], 64).then_inc(qk_ready, 1)
                    if p == 11:
                        update(2)
                    if p == 12:
                        update(3)
                        decay_scores(0)
                        decay_scores(1)
                    if p == 13:
                        update(4)
                        decay_scores(2)
                        decay_scores(3)
                        update(5)
                        head_norm(h0 + 2, G["rv"], 8, P, 1.0 / P, EPS, per_head(G["rqk_ob"]))
                        dve.wait_ge(act_evac, e0 + 8)
                        nc.vector.tensor_tensor(G["rqk_ob"], G["rqk_ob"], G["rg"], ALU.mult).then_inc(M["half_normed"], 1)
                        bt_low(bt0[k], 4)
                    if p == 14:
                        next_state(0)
                        for n in range(1, 4):
                            new_values(n)
                            if n < 3:
                                next_state(n)
                    if p == 15:
                        head_norm(h0 + 3, G["rv"], 8, P, 1.0 / P, EPS, per_head(G["decay_oa"]))
                        dve.wait_ge(M["gz_ready"], 1)
                        nc.vector.tensor_tensor(G["decay_oa"], G["decay_oa"], G["gz"], ALU.mult).then_inc(M["half_normed"], 1)
                        bt_low(bt0[k] + 1, 4)
                add_to_x(k, out0[k], 1.0)

            def dil_diff(k):
                n0, e0, g0, r0, rp = first_piece[k], evac0[k], map0[k], round0[k], rope0[k]
                tab = B["rope"].rearrange("p (c t d) -> p c t d", c=2, t=TT)
                tab_wide = B["rope_wide"].rearrange("p (c t d) -> p c t d", c=2, t=TT)
                lam = B["lam"]
                d4 = heads(B["diff"], P)
                x4 = xn[:, :, 0:512].rearrange("p t (r n w) -> p t r n w", r=2, n=2)

                def rotate(name, j, tables, w):
                    dve.wait_ge(act_evac, e0 + 2 * j + 2)
                    rope(heads(B[name], w), heads(B["rot"], w), tables[:, 0], tables[:, 1], w).then_inc(qk_ready, 1)

                def take_pair(h):
                    dve.wait_ge(pv_done, g0 + 2 * h + 2)
                    i = 2 * h
                    link(nc.vector.reciprocal(expsum[:, 1, :, i:i + 2], expsum[:, 0, :, i:i + 2]))
                    second = expsum[:, 1, :, i + 1]
                    link(nc.vector.tensor_scalar(second, second, lam[:, 5:6], None, ALU.mult))
                    for tt in range(TT):
                        prod = B["prod"][:, tt * P:(tt + 1) * P]
                        link(nc.vector.tensor_scalar(prod, bank[7][:, tt * 256 + P:tt * 256 + 256],
                                                     expsum[:, 1, tt, i + 1:i + 2], None, ALU.mult))
                        ins = nc.vector.scalar_tensor_tensor(out=d4[:, tt, h], in0=bank[7][:, tt * 256:tt * 256 + P],
                                                             scalar=expsum[:, 1, tt, i:i + 1], in1=prod, op0=ALU.mult, op1=ALU.add)
                    ins.then_inc(o_ready, 1)

                dve.wait_ge(params_in, params_at(k))
                pairs = B["lambdas"].rearrange("p (m w d) -> p m w d", m=2, w=2)
                prods = B["prod"][:, 0:128].rearrange("p (m d) -> p m d", m=2)
                link(nc.vector.tensor_tensor(prods, pairs[:, :, 0], pairs[:, :, 1], ALU.mult))
                nc.vector.tensor_reduce(lam[:, 0:2], prods, AX_X, ALU.add).then_inc(lam_sums, 1)
                link(nc.vector.tensor_scalar(B["diff_norm"], B["diff_norm"], 1.0 - LAMBDA_INIT, None, ALU.mult))
                dve.wait_ge(lam_exp, 1)
                link(nc.vector.tensor_tensor(lam[:, 4:5], lam[:, 3:4], lam[:, 2:3], ALU.subtract))
                link(nc.vector.tensor_scalar(lam[:, 5:6], lam[:, 4:5], -LAMBDA_INIT, None, ALU.add))
                for p in range(PIECES["dil_diff"]):
                    ahead(n0 + p)
                    if p == 2:
                        rotate("dq", 0, tab, 64)
                    if p == 4:
                        rotate("dk", 1, tab, 64)
                    if 8 <= p <= 11:
                        take_pair(p - 8)
                    if 6 <= p <= 9:
                        soft(g0 + 2 * (p - 6), 0.125, B["mask"])
                        soft(g0 + 2 * (p - 6) + 1, 0.125, B["mask"])
                    if p == 8:
                        rotate("cq", 3, tab_wide, P)
                    if p == 10:
                        rotate("ck", 4, tab_wide, P)
                    if p == 11:
                        dve.wait_ge(o_ready, r0 + 4)
                        nc.vector.tensor_copy(lam[:, 6:7], lam[:, 5:6]).then_inc(diff_squared, 1)
                        head_norm(head_norm0[k], B["sq"], 8, P, 1.0 / P, EPS, B["diff"].rearrange("p (n w) -> p n w", w=P))
                        gb = B["diff_norm"].unsqueeze(1).broadcast_to([P, 4, P])
                        for tt in range(TT):
                            ins = nc.vector.tensor_tensor(xn[:, tt, 512:D].rearrange("p (h w) -> p h w", w=P), d4[:, tt], gb, ALU.mult)
                        ins.then_inc(diff_normed, 1)
                        bt_low(bt0[k], 6)
                    if p == 12:
                        soft(g0 + 8, DIL_SCALE, B["mask_dil"])
                        soft(g0 + 9, DIL_SCALE, B["mask_dil"])
                    if p == 13:
                        soft(g0 + 10, DIL_SCALE, B["mask_dil"])
                        soft(g0 + 11, DIL_SCALE, B["mask_dil"])
                        take_round(r0 + 4, g0 + 9, 0, 2, x4[:, :, 0])
                        take_round(r0 + 5, g0 + 11, 2, 2, x4[:, :, 1])
                        bt_low(bt0[k] + 1, 4)
                add_to_x(k, out0[k], 1.0)

            def rope_gains(k, i):
                dve.wait_ge(params_in, params_at(k))
                tab = A["rope"].rearrange("p (c t d) -> p c t d", c=2, t=TT)
                out = A["rope_g"].rearrange("p (w c t d) -> p w c t d", w=2, c=2, t=TT)
                for w in range(2):
                    g = A["qk_norm"][:, 64 * w:64 * w + 64]
                    b = lambda lo, hi: g[:, lo:hi].unsqueeze(1).broadcast_to([P, TT, hi - lo])
                    nc.vector.tensor_tensor(out[:, w, 0], tab[:, 0], b(0, 64), ALU.mult)
                    nc.vector.tensor_tensor(out[:, w, 1, :, 0:32], tab[:, 1, :, 0:32], b(32, 64), ALU.mult)
                    link(nc.vector.tensor_tensor(out[:, w, 1, :, 32:64], tab[:, 1, :, 32:64], b(0, 32), ALU.mult))

            def head_norm(c, sq, n, w, scale, eps, x3):
                dve.wait_ge(hsq_done, c + 1)
                link(nc.vector.tensor_reduce(hstat[:, 0, 0:n], sq.rearrange("p (n w) -> p n w", w=w), AX_X, ALU.add))
                nc.vector.tensor_scalar(hstat[:, 1, 0:n], hstat[:, 0, 0:n], scale, eps, ALU.mult, ALU.add).then_inc(hmean_ready, 1)
                dve.wait_ge(hrstd_ready, c + 1)
                link(nc.vector.tensor_tensor(x3, x3, hstat[:, 2, 0:n].unsqueeze(2).broadcast_to([P, n, w]), ALU.mult))

            def rope(x, rot, cos, sin, w):
                h, n = w // 2, x.shape[2]
                b = lambda v: v.unsqueeze(2).broadcast_to([P, TT, n, v.shape[2]])
                nc.vector.tensor_tensor(rot[:, :, :, 0:h], x[:, :, :, h:w], b(sin[:, :, 0:h]), ALU.mult)
                link(nc.vector.tensor_tensor(rot[:, :, :, h:w], x[:, :, :, 0:h], b(sin[:, :, h:w]), ALU.mult))
                link(nc.vector.tensor_tensor(x, x, b(cos), ALU.mult))
                return nc.vector.tensor_tensor(x, x, rot, ALU.add)

            def soft(g, scale, mask):
                pr = A["probs"][:, (g % 2) * 384:(g % 2) * 384 + 384]
                dve.wait_ge(s_done, g + 1)
                if g >= 2:
                    dve.wait_ge(pt_done, g - 1)
                nc.vector.scalar_tensor_tensor(out=pr, in0=bank[4 + g % 2][:, 0:384], scalar=scale, in1=mask,
                                               op0=ALU.mult, op1=ALU.add).then_inc(s_masked, 1)
                dve.wait_ge(s_masked, g + 1)
                nc.vector.tensor_reduce(negmax[:, g % 2, 0:1], pr[:, 0:P], AX_X, ALU.max, negate=True)
                nc.vector.tensor_reduce(negmax[:, g % 2, 1:2], pr[:, P:3 * P], AX_X, ALU.max, negate=True).then_inc(max_ready, 1)

            def take_round(r, last_map, i0, n, out):
                dve.wait_ge(pv_done, last_map + 1)
                link(nc.vector.reciprocal(expsum[:, 1, :, i0:i0 + n], expsum[:, 0, :, i0:i0 + n]))
                w = 512 // (TT * n)
                nc.vector.tensor_tensor(out, bank[7][:, :].rearrange("p (t n w) -> p t n w", t=TT, n=n),
                                        expsum[:, 1, :, i0:i0 + n].unsqueeze(3).broadcast_to([P, TT, n, w]),
                                        ALU.mult).then_inc(o_ready, 1)

            def bt_low(c, src, scale=None):
                dve.wait_ge(bt_hi_done, c + 1)
                for b in range(2):
                    for r in range(2):
                        q, hi = 2 * b + r, bt_hi[:, 2 * b + r, :].bitcast(F32)
                        if scale is None:
                            ins = nc.vector.tensor_tensor(bt_lo[:, q, :], psum3(src + b, 2)[:, r, :], hi, ALU.subtract)
                        else:
                            ins = nc.vector.scalar_tensor_tensor(out=bt_lo[:, q, :], in0=psum3(src + b, 2)[:, r, :],
                                                                 scalar=scale[:, q:q + 1], in1=hi, op0=ALU.mult, op1=ALU.subtract)
                ins.then_inc(bt_lo_done, 1)

            def pool_attn(k, i):
                n0, g0, r0, c0, o0 = first_piece[k], map0[k], round0[k], head_norm0[k], out0[k]
                rg = A["rope_g"].rearrange("p (w c t d) -> p w c t d", w=2, c=2, t=TT)
                gates = tok(A["gates"])
                o4 = A["u"].rearrange("p (t r n w) -> p t r n w", t=TT, r=2, n=4)

                def rotate(which, name):
                    head_norm(c0 + which, A["sq"], 16, 64, 1.0 / 64, EPS, A[name].rearrange("p (n w) -> p n w", w=64))
                    rope(heads(A[name]), heads(A["rot"]), rg[:, which, 0], rg[:, which, 1], 64).then_inc(qk_ready, 1)

                for p in range(PIECES["pool_attn"]):
                    if p != 19:
                        ahead(n0 + p)
                    if p == 0:
                        rope_gains(k, i)
                        dve.wait_ge(rstd_ready, TT * (k + 1))
                    if p == 4:
                        rotate(0, "q")
                    if p == 6:
                        bt_low(2 * i, 6, A["pool_scale"])
                        rotate(1, "k")
                    if p == 15:
                        take_round(r0, g0 + 3, 0, 4, o4[:, :, 0])
                    if 9 <= p <= 16:
                        soft(g0 + p - 9, 0.125, A["mask"])
                    if p in (9, 11, 13, 15):
                        j = (p - 1) // 2
                        for tt in range(TT):
                            if tt == 0:
                                dve.wait_ge(proj_done, chunk0[k] + j + 1)
                            else:
                                dve.wait_ge(used, n0 + 2 * j + 2)
                            gs = gates[:, tt, (j - 4) * 512:(j - 3) * 512]
                            nc.vector.scalar_tensor_tensor(out=gs, in0=bank[2 * (j % 2) + tt][:, :], scalar=stat[:, 2, tt:tt + 1],
                                                           in1=gs, op0=ALU.mult, op1=ALU.add).then_inc(gate_added, 1)
                    if p == 17:
                        take_round(r0 + 1, g0 + 7, 4, 4, o4[:, :, 1])
                        dve.wait_ge(gates_ready, i + 1)
                        for j in range(4):
                            tt, cols = j // 2, slice((j % 2) * 512, (j % 2 + 1) * 512)
                            half_done(o0, j, n0 + 17)
                            nc.vector.tensor_tensor(xn[:, tt, cols], bank[j][:, :], gates[:, tt, cols], ALU.mult).then_inc(branch_ready, 1)
                        bt_low(2 * i + 1, 4)
                    if p == 19:
                        for j in range(4):
                            tt, cols = j // 2, slice((j % 2) * 512, (j % 2 + 1) * 512)
                            half_done(o0 + 1, j, n0 + 19)
                            g1 = gates[:, tt, D + (j % 2) * 512:D + (j % 2 + 1) * 512]
                            link(nc.vector.tensor_tensor(g1, bank[j][:, :], g1, ALU.mult))
                            nc.vector.tensor_tensor(xn[:, tt, cols], xn[:, tt, cols], g1, ALU.add).then_inc(merged_ready, 1)
                            if j:
                                xt_low(turn0[k] + 1, None, (j - 1,))
                        xt_low(turn0[k] + 1, None, (3,))
                        ahead(n0 + p)
                add_to_x(k, o0 + 2, 1.0)

            seen = {"pool_attn": 0}
            f = 0
            for k, kind in enumerate(program):
                if k == 0:
                    dve.wait_ge(gain_in, 16)
                    xt_low(0, 0, (0, 1))
                    split_lo(0, 0)
                    xt_low(0, 0, (2, 3))
                    split_lo(1, 1)
                    for tt in range(TT):
                        mean_square(0, tt)
                elif not late[k]:
                    xt_low(turn0[k], k)
                if kind == "ffn":
                    ffn(f, k)
                    f += 1
                    add_to_x(k, out0[k], 0.5, first_piece[k] + 34)
                if kind == "pool_attn":
                    pool_attn(k, seen[kind])
                    seen[kind] += 1
                if kind == "dil_diff":
                    dil_diff(k)
                if kind == "delta_ret":
                    delta_ret(k)

        @block.tensor
        def _(pe):
            def three(out, a_hi, a_lo, b_hi, b_lo, start, stop):
                nc.tensor.matmul(out, a_hi, b_hi, start=start, stop=False)
                nc.tensor.matmul(out, a_hi, b_lo, start=False, stop=False)
                return nc.tensor.matmul(out, a_lo, b_hi, start=False, stop=stop)

            def turn(src, j):
                tt, g = j // 2, j % 2
                for q in range(4):
                    c = (4 * g + q) * P
                    ins = nc.tensor.transpose(bank[4 + j][:, q * P:(q + 1) * P], src[:, tt, c:c + P], ident[:, :])
                ins.then_inc(xt_done, 1)

            def turn_x(k, halves):
                for j in halves:
                    if not late[k]:
                        pe.wait_ge(xn_ready, TT * normed0[k] + j // 2 + 1)
                    elif k:
                        pe.wait_ge(x_ready, 4 * (k - 1) + j + 1)
                    else:
                        pe.wait_ge(x_in[j // 2], 16)
                    turn(x if late[k] else xn, j)

            def turn_early(k, j):
                if late[k] and j in (1, 2):
                    turn_x(k, (j - 1,))

            def turn_first(k):
                if k == 0:
                    turn_x(k, (0, 1))
                else:
                    turn_x(k, (2,) if late[k] else range(4))

            def turn_rest(k):
                if k == 0:
                    turn_x(k, (2, 3))
                elif late[k]:
                    turn_x(k, (3,))

            def ffn(f, k, n0):
                base = n0

                def up(c, hook=None):
                    for half in range(2):
                        s = (base + half + (0 if isinstance(c, int) and c == 0 else 2)) % SLOTS
                        m = (base + half) if isinstance(c, int) and c == 0 else c * SLOTS + (base + 2 - SLOTS + half)
                        opening = isinstance(c, int) and c == 0
                        if not isinstance(m, int) or m:
                            pe.wait_ge(lo_done, m + 1)
                        for tt in range(TT):
                            if half == 0 and not (isinstance(c, int) and c <= 1):
                                pe.wait_ge(hid_ready, c * TT + (TT * NCH * f + tt + 1 - TT))
                            if isinstance(c, int) and c == 0:
                                pe.wait_ge(xt_lo_done, 4 * turn0[k] + 2 * tt + half + 1)
                            for q in range(4):
                                if isinstance(m, int) and m == 0 and tt == 0:
                                    pe.wait_ge(lo_done if q == 3 else first_lo, 1 if q == 3 else q + 1)
                                kt = 4 * half + q
                                a = slice(tt * P, (tt + 1) * P)
                                ins = three(bank[tt if opening else 4 + tt][:, :], xt_hi[:, kt, a], xt_lo[:, kt, a],
                                            up_view(w_hi[s], q), up_view(w_lo[s], q), kt == 0, kt == KT - 1)
                            if half == 1 and tt == 0:
                                ins.then_inc(up_done, 1)
                            if opening and half == 0 and tt == 0:
                                turn_rest(k)
                            if tt == 1:
                                ins.then_inc(used, 1)
                        if half == 0 and hook:
                            hook()

                def down(c, m, s, hook=None):
                    pe.wait_ge(lo_done, m + 1)
                    pe.wait_ge(ht_lo_done, c + (NCH * f + 1))
                    first = isinstance(c, int) and c == 0
                    final = isinstance(c, int) and c == NCH - 1
                    for tt in range(TT):
                        a = slice(tt * P, (tt + 1) * P)
                        for h in range(2):
                            for q in range(2):
                                ins = three(bank[2 * tt + h][:, :], hidden_parts(c)[0][:, q, a], hidden_parts(c)[1][:, q, a],
                                            down_view(w_hi[s], q, h), down_view(w_lo[s], q, h),
                                            first and q == 0, final and q == 1)
                            j = 2 * tt + h
                            if final and j < 3:
                                ins.then_inc(out_done, 1)
                            if j == 3:
                                ins.then_inc(used, 1)
                            if final:
                                turn_early(k + 1, j)
                        if tt == 0 and hook:
                            hook()

                def turn_hidden(c):
                    pe.wait_ge(hid_ready, c * TT + (TT * NCH * f + TT))
                    for q in range(2):
                        for tt in range(TT):
                            ins = nc.tensor.transpose(bank[6][:, q * SEQ + tt * P:q * SEQ + (tt + 1) * P],
                                                      hid[:, tt, q * P:(q + 1) * P], ident[:, :])
                    ins.then_inc(ht_done, 1)

                def step(c):
                    up(c)
                    down(c - 1, c * SLOTS + (base + 1), (base + 4) % SLOTS)
                    turn_hidden(c)

                last = NCH - 1
                up(0)
                up(1, lambda: turn_hidden(0))
                down(0, base + 4, (base + 4) % SLOTS)
                turn_hidden(1)
                with pe.Fori(2, last) as c:
                    step(c)
                up(last)
                down(last - 1, base + 3 * last + 1, (base + 3 * last + 1) % SLOTS, lambda: turn_hidden(last))
                down(last, base + 3 * last + 2, (base + 3 * last + 2) % SLOTS)

            def chunk_piece(k, n, j, half, hook=None):
                s = n % SLOTS
                pe.wait_ge(lo_done, n + 1)
                for tt in range(TT):
                    if j == 0:
                        pe.wait_ge(xt_lo_done, 4 * turn0[k] + 2 * tt + half + 1)
                    a = slice(tt * P, (tt + 1) * P)
                    for q in range(4):
                        kt = 4 * half + q
                        ins = three(bank[2 * (j % 2) + tt][:, :], xt_hi[:, kt, a], xt_lo[:, kt, a],
                                    up_view(w_hi[s], q), up_view(w_lo[s], q), kt == 0, kt == KT - 1)
                    if half == 1 and tt == 0:
                        ins.then_inc(proj_done, 1)
                    if tt == TT - 1:
                        ins.then_inc(used, 1)
                    if j == 0 and half == 0 and tt == 0:
                        turn_rest(k)
                    if hook:
                        hook(tt)

            def product(n, pieces, operand, before=None, ready=None, after=None, between=None):
                for i in range(pieces):
                    s = (n + i) % SLOTS
                    pe.wait_ge(lo_done, n + i + 1)
                    for tt in range(TT):
                        if i == 0 and before:
                            before(tt)
                        if ready:
                            ready(i, tt)
                        a = slice(tt * P, (tt + 1) * P)
                        for h in range(2):
                            for q in range(2):
                                hi, lo = operand(i, q)
                                ins = three(bank[2 * tt + h][:, :], hi[:, a], lo[:, a],
                                            down_view(w_hi[s], q, h), down_view(w_lo[s], q, h),
                                            i == 0 and q == 0, i == pieces - 1 and q == 1)
                            j = 2 * tt + h
                            if j == 3:
                                ins.then_inc(used, 1)
                            elif i == pieces - 1:
                                ins.then_inc(out_done, 1)
                            if between:
                                between(i, tt, h)
                    if after:
                        after(i)

            def in_bt(i, q):
                return bt_hi[:, 2 * (i % 2) + q, :], bt_lo[:, 2 * (i % 2) + q, :]

            def in_xt(i, q):
                return xt_hi[:, 2 * i + q, :], xt_lo[:, 2 * i + q, :]

            def turn_heads(src, b0):
                for c in range(4):
                    for tt in range(TT):
                        at = (c % 2) * SEQ + tt * P
                        ins = nc.tensor.transpose(bank[b0 + c // 2][:, at:at + P], src[:, tt, c * P:(c + 1) * P], ident[:, :])
                return ins

            def scores(g, operands):
                if g >= 2:
                    pe.wait_ge(s_masked, g - 1)
                for (lhs, rhs), (lo, hi) in zip(operands, ((0, P), (P, 3 * P))):
                    ins = nc.tensor.matmul(bank[4 + g % 2][:, lo:hi], lhs, rhs, start=True, stop=True)
                ins.then_inc(s_done, 1)

            def turn_probs(g):
                pe.wait_ge(exp_done, g + 1)
                if g >= 1:
                    pe.wait_ge(pt_ready, g)
                for c in range(3):
                    ins = nc.tensor.transpose(bank[6][:, c * P:(c + 1) * P],
                                              A["probs"][:, (g % 2) * 384 + c * P:(g % 2) * 384 + (c + 1) * P], ident[:, :])
                ins.then_inc(pt_done, 1)

            def values(g, j, n, vs, rounds_before):
                pe.wait_ge(pt_ready, g + 1)
                if j == 0 and rounds_before:
                    pe.wait_ge(o_ready, rounds_before)
                w = 512 // (TT * n)
                pt = A["probs_t"][:, (g % 2) * 384:(g % 2) * 384 + 384]
                nc.tensor.matmul(bank[7][:, j * w:(j + 1) * w], pt[:, 0:P], vs[0], start=True, stop=True)
                out = bank[7][:, 256 + j * w:256 + (j + 1) * w]
                nc.tensor.matmul(out, pt[:, P:2 * P], vs[0], start=True, stop=False)
                nc.tensor.matmul(out, pt[:, 2 * P:3 * P], vs[1], start=False, stop=True).then_inc(pv_done, 1)

            def pool_attn(k, i):
                n0, e0, g0, r0 = first_piece[k], evac0[k], map0[k], round0[k]
                u, v = tok(A["u"]), tok(A["v"])
                means = A["pool_mean"].rearrange("p (g q) -> p g q", g=4)
                mapped = lambda name: A[name].rearrange("p (c q) -> p c q", c=4)
                qt, kt, pw = mapped("qt"), mapped("kt"), A["pool_w"].rearrange("p (g d) -> p g d", g=4)

                def attend(h, what):
                    c, off = h // 2, 64 * (h % 2)
                    if what == "scores":
                        scores(g0 + h, causal_map(g0 + h, qt[:, c], kt[:, c], off, 64))
                    elif what == "turn":
                        turn_probs(g0 + h)
                    else:
                        values(g0 + h, h % 4, 4, [v[:, tt, h * 64:(h + 1) * 64] for tt in range(TT)], r0 + h // 4)

                for p in range(16):
                    j = p // 2
                    if p % 2 == 0 and j >= 2:
                        if j < 6:
                            pe.wait_ge(act_evac, e0 + 2 * (j - 2) + 2)
                        else:
                            pe.wait_ge(gate_added, 8 * i + 2 * (j - 6) + 2)
                    chunk_piece(k, n0 + p, j, p % 2)
                    if p == 3:
                        pe.wait_ge(params_in, params_at(k))
                        pe.wait_ge(act_evac, e0 + 2)
                        for g in range(4):
                            at = (g % 2) * SEQ
                            us = [u[:, tt, g * P:(g + 1) * P] for tt in range(TT)]
                            nc.tensor.matmul(bank[4 + g // 2][:, at:at + SEQ], us[0], means[:, g, 0:SEQ], start=True, stop=False)
                            ins = nc.tensor.matmul(bank[4 + g // 2][:, at + P:at + SEQ], us[1], means[:, g, SEQ:3 * P], start=False, stop=True)
                        ins.then_inc(diff_done, 1)
                    if p == 5:
                        pe.wait_ge(diff_ready, i + 1)
                        for g in range(4):
                            at = (g % 2) * SEQ
                            ins = nc.tensor.matmul(bank[6 + g // 2][:, at:at + SEQ], pw[:, g, :], qt[:, g, :], start=True, stop=True)
                        ins.then_inc(y_done, 1)
                    if p == 7:
                        pe.wait_ge(qk_ready, 2 * i + 1)
                        turn_heads(tok(A["q"]), 4).then_inc(qkt_done, 1)
                    if p == 8:
                        pe.wait_ge(bt_lo_done, 2 * i + 1)
                        pe.wait_ge(qk_ready, 2 * i + 2)
                        turn_heads(tok(A["k"]), 6).then_inc(qkt_done, 1)
                    if p == 9:
                        pe.wait_ge(qkt_ready, 2 * i + 2)
                    if p >= 10:
                        attend(p - 10, "turn")
                    if p >= 9:
                        attend(p - 9, "scores")
                    if p >= 11:
                        attend(p - 11, "values")

                def turn_merged(halves):
                    for j in halves:
                        pe.wait_ge(merged_ready, 4 * i + j + 1)
                        turn(xn, j)

                def gates_out(tt):
                    pe.wait_ge(gate_added, 8 * i + 6 + 2 * tt)
                    if tt == 0:
                        pe.wait_ge(bt_lo_done, 2 * i + 1)

                def with_maps(i2):
                    attend(6 + i2, "turn")
                    if i2 == 0:
                        attend(7, "scores")
                    attend(5 + i2, "values")

                product(n0 + 16, 2, in_bt, gates_out, None, with_maps)
                attend(7, "values")
                pe.wait_ge(o_ready, r0 + 2)
                turn_heads(tok(A["u"]), 4).then_inc(ot_done, 1)

                def pooled_out(tt):
                    pe.wait_ge(branch_ready, 4 * i + 2 * tt + 2)
                    pe.wait_ge(bt_lo_done, 2 * i + 2)

                product(n0 + 18, 2, in_bt, pooled_out, None, None,
                        lambda i2, tt, h: turn_merged([2 * tt + h - 1]) if i2 == 1 and tt + h == 1 else None)
                turn_merged([2])

                def late_turns(i2, tt, h):
                    if (i2, tt, h) == (0, 0, 1):
                        turn_merged([3])
                    if i2 == 3:
                        turn_early(k + 1, 2 * tt + h)

                product(n0 + 20, 4, in_xt, None,
                        lambda i2, tt: pe.wait_ge(xt_lo_done, 4 * (turn0[k] + 1) + 2 * tt + i2 // 2 + 1), None, late_turns)

            def delta_ret(k):
                n0, e0 = first_piece[k], evac0[k]
                mapped = lambda name: G[name].rearrange("p (c q) -> p c q", c=4)
                kt, qt, kbt, qdt, wt, rt = (mapped(name) for name in ("kt_rt", "qt_pr", "kbt_wt", "qdt", "kbt_wt", "kt_rt"))
                vb, kbe, kd, uu = (mats(G[name]) for name in ("v_vb", "kb_kbe", "k_kd", "q_qd_u"))
                rv = mats(G["rv"])
                mm = nc.tensor.matmul

                def channels_piece(i, half):
                    n = n0 + 2 * i + half
                    s, b0 = n % SLOTS, 2 * (i % 2)
                    pe.wait_ge(lo_done, n + 1)
                    for c in range(4):
                        out = psum3(b0 + c // 2, 2)[:, c % 2, :]
                        for q in range(4):
                            kt_ = 4 * half + q
                            cols = slice(q * 512 + c * P, q * 512 + (c + 1) * P)
                            args = dict(skip_group_check=True)
                            mm(out, w_hi[s][:, cols], xt_hi[:, kt_, :], start=kt_ == 0 and c % 2 == 0, stop=False, **args)
                            mm(out, w_hi[s][:, cols], xt_lo[:, kt_, :], start=False, stop=False, **args)
                            ins = mm(out, w_lo[s][:, cols], xt_hi[:, kt_, :], start=False, stop=kt_ == KT - 1, **args)
                    ins.then_inc(used, 1)

                def turn_channels(i):
                    pe.wait_ge(M["co_ready"], i + 1)
                    for tt in range(TT):
                        for c in range(4):
                            ins = nc.tensor.transpose(bank[4 + tt][:, c * P:(c + 1) * P], co[i % 2][:, c, tt * P:(tt + 1) * P], ident[:, :])
                    ins.then_inc(M["co_turned"], 1)

                def per_tile(b0, lhs, rhs, done):
                    for tt in range(TT):
                        for h in range(4):
                            ins = mm(bank[b0 + tt][:, h * P:(h + 1) * P], lhs(tt, h), rhs(tt, h), start=True, stop=True)
                    ins.then_inc(M[done], 1)

                tile = lambda m: (lambda tt, h: m[:, h, tt * P:(tt + 1) * P])
                mat = lambda m: (lambda tt, h: m[:, tt, h, :])

                def level_a(l):
                    pe.wait_ge(M["level_masked"], l)
                    for tt in range(TT):
                        if l == 1:
                            pe.wait_ge(M["x0_ready"], 1)
                        else:
                            pe.wait_ge(M["x_updated"], TT * (l - 2) + tt + 1)
                        for h in range(4):
                            ins = mm(bank[4 + tt][:, h * P:(h + 1) * P], lev[:, tt, h, :], inv[:, tt, h, :], start=True, stop=True)
                        ins.then_inc(M["t1_done"], 1)

                def level_b(l):
                    for tt in range(TT):
                        pe.wait_ge(M["t1_ready"], TT * (l - 1) + tt + 1)
                        for h in range(4):
                            cols = slice(h * P, (h + 1) * P)
                            if l < 5:
                                mm(bank[6 + tt][:, cols], inv_t[:, tt, h, :], prod1[:, tt, h, :], start=True, stop=True)
                            ins = mm(bank[4 + tt][:, cols], prod1[:, tt, h, :], inv_t[:, tt, h, :], start=True, stop=True)
                        ins.then_inc(M["y_done"], 1)

                def retention_scores(h):
                    c, rows = h // 2, slice(64 * (h % 2), 64 * (h % 2) + 64)
                    b = bank[6 + h % 2]
                    if h >= 2:
                        pe.wait_ge(M["rs_ready"], h - 1)
                    mm(b[:, 0:SEQ], rt[rows, 2 + c, 0:P], rt[rows, c, 0:SEQ], start=True, stop=True)
                    mm(b[:, SEQ:384], rt[rows, 2 + c, P:SEQ], rt[rows, c, P:SEQ], start=True, stop=True).then_inc(M["rs_done"], 1)

                def read_out(n, what):
                    tt, lo = n // 2, 64 * (n % 2)
                    rows = slice(lo, lo + 64)
                    toks = slice(tt * P + lo, tt * P + lo + 64)
                    for h in range(4):
                        out = bank[6 + tt][rows, h * P:(h + 1) * P]
                        if what == "state":
                            ins = mm(out, qdt[:, h, toks], state[:, h, :], start=h == 0, stop=False, skip_group_check=True)
                        else:
                            vals = uu[rows, 0, h, :] if n == 0 else v_new[rows, h, :]
                            ins = mm(out, qk_m[rows, tt, h, rows], vals, start=n == 0 and h == 0, stop=True, skip_group_check=True)
                    return ins

                def old_values(n):
                    tt, lo = n // 2, 64 * (n % 2)
                    toks = slice(tt * P + lo, tt * P + lo + 64)
                    pe.wait_ge(M["s_ready"], n)
                    for h in range(4):
                        ins = mm(bank[4][lo:lo + 64, h * P:(h + 1) * P], wt[:, h, toks], state[:, h, :], start=True, stop=True)
                    ins.then_inc(M["vw_done"], 1)
                    read_out(n, "state")

                def own_values(n):
                    tt, rows = n // 2, slice(64 * (n % 2), 64 * (n % 2) + 64)
                    if n:
                        pe.wait_ge(M["vn_ready"], n)
                    if n < 3:
                        for h in range(4):
                            vals = uu[rows, 0, h, :] if n == 0 else v_new[rows, h, :]
                            ins = mm(bank[5][:, h * P:(h + 1) * P], kd[rows, tt, h, :], vals, start=True, stop=True)
                        ins.then_inc(M["ds_done"], 1)
                    read_out(n, "own").then_inc(M["o_done"], 1)

                pe.wait_ge(M["ba_split"], 1)
                pe.wait_ge(xt_lo_done, 4 * turn0[k] + 4)
                for tt in range(TT):
                    for kt_ in range(KT):
                        a, c = slice(tt * P, (tt + 1) * P), slice(kt_ * 8, kt_ * 8 + 8)
                        ins = three(bank[4][:, tt * 8:tt * 8 + 8], xt_hi[:, kt_, a], xt_lo[:, kt_, a], ba_hi[:, c], ba_lo[:, c],
                                    kt_ == 0, kt_ == KT - 1)
                ins.then_inc(M["ba_done"], 1)

                def hook(p, tt):
                    if p == 6 and tt == 0:
                        pe.wait_ge(M["tm_ready"], 2)
                        pe.wait_ge(M["kb_ready"], 1)
                        turn_heads(tok(G["kb_kbe"]), 4).then_inc(M["kbt_turned"], 1)
                    if p == 6 and tt == 1:
                        pe.wait_ge(M["kt_ready"], 1)
                        pe.wait_ge(M["normed"], 1)
                        turn_heads(tok(G["q_qd_u"]), 6).then_inc(M["qt_turned"], 1)
                    if p == 7 and tt == 0:
                        pe.wait_ge(M["kbt_ready"], 1)
                        turn_channels(2)
                    if p == 7 and tt == 1:
                        pe.wait_ge(M["qt_ready"], 1)
                        per_tile(6, tile(kt), tile(kbt), "at_done")
                    if p == 8 and tt == 0:
                        pe.wait_ge(M["tm_ready"], 3)
                        per_tile(4, tile(kt), tile(qt), "qk_done")
                    if p == 8 and tt == 1:
                        pe.wait_ge(M["at_ready"], 1)
                        pe.wait_ge(M["qd_ready"], 1)
                        turn_heads(tok(G["q_qd_u"]), 6).then_inc(M["qdt_turned"], 1)
                    if p == 9 and tt == 0:
                        pe.wait_ge(M["qk_masked"], 1)
                        pe.wait_ge(M["xt0_ready"], 1)
                        for t2 in range(TT):
                            for h in range(4):
                                ins = nc.tensor.transpose(bank[4 + t2][:, h * P:(h + 1) * P], inv_t[:, t2, h, :], ident[:, :])
                        ins.then_inc(M["x0_turned"], 1)
                    if p == 9 and tt == 1:
                        pe.wait_ge(M["qdt_ready"], 1)
                        level_a(1)
                    if p >= 10:
                        if tt == 0:
                            if p == 12:
                                pe.wait_ge(M["rqk_ready"], 1)
                            if p == 13:
                                pe.wait_ge(M["rs_ready"], 2)
                            level_b(p - 9)
                        else:
                            if p == 13:
                                level_a(5)
                                retention_scores(2)
                                retention_scores(3)
                            else:
                                level_a(p - 8)
                            if p == 11:
                                pe.wait_ge(qk_ready, rope0[k] + 1)
                                pe.wait_ge(M["x_updated"], 4)
                                turn_heads(tok(G["rqk_ob"]), 6).then_inc(M["rqk_turned"], 1)
                            if p == 12:
                                pe.wait_ge(M["x_updated"], 6)
                                pe.wait_ge(M["rqk_ready"], 1)
                                retention_scores(0)
                                retention_scores(1)

                for p in range(14):
                    if p < 6:
                        if p == 4:
                            pe.wait_ge(M["ct_ready"], 1)
                        channels_piece(p // 2, p % 2)
                    else:
                        if p % 2 == 0:
                            if p < 10:
                                pe.wait_ge(M["ct_ready"], p // 2 - 1)
                            else:
                                pe.wait_ge(act_evac, e0 + 2 * (p // 2 - 5) + 2)
                        chunk_piece(k, n0 + p, p // 2, p % 2, lambda tt, p=p: hook(p, tt)) if p != 13 else chunk_piece(
                            k, n0 + p, p // 2, 1, lambda tt: hook(13, tt))
                    if p == 0:
                        pe.wait_ge(M["g_ready"], 1)
                        g = G["gates"][:, 0:8]
                        consts = (G["before"], G["after"], G["sub"][:, 0:P], G["sub"][:, P:2 * P])
                        for i, m in enumerate(consts):
                            ins = mm(bank[5][:, 8 * i:8 * i + 8], m, g, start=True, stop=True)
                        ins.then_inc(M["sums_done"], 1)
                    if p == 1:
                        pe.wait_ge(M["ug_ready"], 1)
                        for tt in range(TT):
                            ins = mm(bank[6 + tt][:, :], G["ones"], G["decay_oa"][:, tt * 512:(tt + 1) * 512], start=True, stop=True)
                        ins.then_inc(M["diff_done"], 1)
                    if p == 3:
                        pe.wait_ge(M["e4_ready"], 1)
                        turn_channels(0)
                    if p == 5:
                        pe.wait_ge(M["tm_ready"], 1)
                        turn_channels(1)
                        pe.wait_ge(M["diff_ready"], 1)
                        pe.wait_ge(M["kb_ready"], 1)
                        turn_heads(tok(G["k_kd"]), 6).then_inc(M["kt_turned"], 1)
                level_b(5)
                pe.wait_ge(M["rs_ready"], 4)
                pe.wait_ge(act_evac, e0 + 6)
                for h in range(4):
                    pr, cols = retention_probs(h), slice(h * P, (h + 1) * P)
                    mm(bank[6][:, cols], pr[:, 0:P], rv[:, 0, h, :], start=True, stop=True)
                    mm(bank[7][:, cols], pr[:, P:2 * P], rv[:, 0, h, :], start=True, stop=False)
                    ins = mm(bank[7][:, cols], pr[:, 2 * P:3 * P], rv[:, 1, h, :], start=False, stop=True)
                ins.then_inc(M["ro_done"], 1)
                pe.wait_ge(M["x_updated"], 10)
                pe.wait_ge(M["vb_ready"], 1)
                pe.wait_ge(M["kbe_ready"], 1)
                per_tile(4, mat(inv_t), mat(vb), "u_done")
                pe.wait_ge(M["ro_ready"], 1)
                for h in range(4):
                    for tt in range(TT):
                        ins = mm(psum3(6 + h // 2, 2)[:, h % 2, tt * P:(tt + 1) * P], kbe[:, tt, h, :], inv_t[:, tt, h, :], start=True, stop=True)
                ins.then_inc(M["wt_done"], 1)
                pe.wait_ge(M["u_ready"], 1)
                pe.wait_ge(M["half_normed"], 1)
                turn_heads(tok(G["rqk_ob"]), 4).then_inc(ot_done, 1)

                def before(tt):
                    pe.wait_ge(act_evac, e0 + (6 if tt == 0 else 8))

                def ready(i, tt):
                    if tt == 0 and i in (0, 2):
                        pe.wait_ge(bt_lo_done, bt0[k] + 1 + i // 2)

                def between(i, tt, h):
                    stage = i * 4 + tt * 2 + h
                    if stage == 0:
                        pe.wait_ge(M["wt_ready"], 1)
                        pe.wait_ge(M["kd_ready"], 1)
                        own_values(0)
                    elif stage < 7:
                        (old_values if stage % 2 else own_values)((stage + 1) // 2)
                    elif stage == 7:
                        pe.wait_ge(M["half_normed"], 2)
                        turn_heads(tok(G["decay_oa"]), 4).then_inc(ot_done, 1)
                    if i == 3:
                        turn_early(k + 1, 2 * tt + h)

                product(n0 + 14, 4, in_bt, before, ready, None, between)

            def dil_diff(k):
                n0, e0, g0, r0, c0, rp = first_piece[k], evac0[k], map0[k], round0[k], turned0[k], rope0[k]
                mapped = lambda name: B[name].rearrange("p (c q) -> p c q", c=4)
                dv, cv = tok(B["dv"]), tok(B["cv"])

                def diff_scores(m):
                    scores(g0 + m, causal_map(g0 + m, mapped("dqt")[:, m // 2], mapped("dkt")[:, m // 2], 64 * (m % 2), 64))

                def diff_values(m):
                    values(g0 + m, m % 2, 2, [dv[:, tt, (m // 2) * P:(m // 2 + 1) * P] for tt in range(TT)], r0 + m // 2)

                def dil_scores(m):
                    scores(g0 + 8 + m, causal_map(g0 + 8 + m, mapped("cqt")[:, m], mapped("ckt")[:, m], 0, P))

                def dil_values(m):
                    values(g0 + 8 + m, m % 2, 2, [cv[:, tt, m * P:(m + 1) * P] for tt in range(TT)], r0 + 4 + m // 2)

                for p in range(12):
                    j = p // 2
                    if p % 2 == 0 and j >= 2:
                        pe.wait_ge(act_evac, e0 + 2 * (j - 2) + 2)
                    chunk_piece(k, n0 + p, j, p % 2)
                    if p == 3:
                        pe.wait_ge(qk_ready, rp + 1)
                        turn_heads(tok(B["dq"]), 4).then_inc(qkt_done, 1)
                    if p == 5:
                        pe.wait_ge(qk_ready, rp + 2)
                        turn_heads(tok(B["dk"]), 6).then_inc(qkt_done, 1)
                    if p == 6:
                        pe.wait_ge(qkt_ready, c0 + 2)
                    if p == 10:
                        pe.wait_ge(s_masked, g0 + 8)
                        pe.wait_ge(qk_ready, rp + 3)
                        turn_heads(tok(B["cq"]), 4).then_inc(qkt_done, 1)
                    if 7 <= p <= 10:
                        turn_probs(g0 + 2 * (p - 7))
                        turn_probs(g0 + 2 * (p - 7) + 1)
                    if 6 <= p <= 9:
                        diff_scores(2 * (p - 6))
                        diff_scores(2 * (p - 6) + 1)
                    if 7 <= p <= 10:
                        diff_values(2 * (p - 7))
                        diff_values(2 * (p - 7) + 1)
                pe.wait_ge(qkt_ready, c0 + 3)
                pe.wait_ge(qk_ready, rp + 4)
                turn_heads(tok(B["ck"]), 4).then_inc(qkt_done, 1)
                pe.wait_ge(diff_normed, 1)
                turn_heads(xn[:, :, 512:D], 6).then_inc(ot_done, 1)

                def before(tt):
                    pe.wait_ge(act_evac, e0 + 10 + 2 * tt - (0 if tt else 0))

                def ready(i, tt):
                    if tt == 0 and i in (0, 2):
                        pe.wait_ge(bt_lo_done, bt0[k] + 1 + i // 2)

                def after(i):
                    if i == 0:
                        pe.wait_ge(qkt_ready, c0 + 4)
                        dil_scores(0)
                        dil_scores(1)
                    if i == 1:
                        turn_probs(g0 + 8)
                        turn_probs(g0 + 9)
                        dil_scores(2)
                        dil_scores(3)
                        pe.wait_ge(act_evac, e0 + 12)
                        dil_values(0)
                        dil_values(1)
                        turn_probs(g0 + 10)
                        turn_probs(g0 + 11)
                        dil_values(2)
                        dil_values(3)
                        pe.wait_ge(o_ready, r0 + 6)
                        turn_heads(xn[:, :, 0:512], 4).then_inc(ot_done, 1)

                product(n0 + 12, 4, in_bt, before, ready, after,
                        lambda i, tt, h: turn_early(k + 1, 2 * tt + h) if i == 3 else None)

            pe.wait_ge(id_in, 16)
            seen = {"pool_attn": 0}
            f = 0
            for k, kind in enumerate(program):
                turn_first(k)
                if kind == "ffn":
                    ffn(f, k, first_piece[k])
                    f += 1
                if kind == "pool_attn":
                    pool_attn(k, seen[kind])
                    seen[kind] += 1
                if kind == "dil_diff":
                    dil_diff(k)
                if kind == "delta_ret":
                    delta_ret(k)


def up_pieces(w, cols):
    import numpy as np
    w = w[:, cols]
    return w.reshape(-1, 4, P, 512).transpose(0, 2, 1, 3).reshape(-1, P, PIECE)


def down_pieces(w):
    return w.reshape(-1, 2, P, 1024).transpose(0, 2, 1, 3).reshape(-1, P, PIECE)


def ffn_pieces(w_up, w_down):
    import numpy as np
    ups = []
    for c in range(NCH):
        cols = np.r_[c * CH:(c + 1) * CH, DFF + c * CH:DFF + (c + 1) * CH]
        ups.append(up_pieces(w_up, cols))
    downs = down_pieces(w_down)
    order = [ups[0]]
    for c in range(1, NCH):
        order += [ups[c], downs[c - 1:c]]
    return order + [downs[NCH - 1:]]


def first_block_pieces(a, i):
    w = a["w_in"][i]
    u, q, k, v, gl = w[:, :512], w[:, 512:1024], w[:, 1024:1536], w[:, 1536:2048], w[:, 2048:]
    out = [up_pieces(m, slice(None)) for m in (u, q, k, v)]
    out += [up_pieces(gl, slice(c * 512, (c + 1) * 512)) for c in range(4)]
    return out + [down_pieces(a[name][i]) for name in ("w_branch_pool", "w_branch_attn", "w_out")]


def rope_table(width):
    import numpy as np
    half = width // 2
    inv = np.float32(1.0) / np.power(np.float32(10000.0), np.arange(half, dtype=np.float32) * np.float32(2.0 / width))
    ang = (np.arange(SEQ, dtype=np.float32)[:, None] * inv.astype(np.float32)[None, :]).astype(np.float64)
    cos, sin = np.cos(ang), np.sin(ang)
    tab = np.stack([np.concatenate([cos, cos], 1), np.concatenate([-sin, sin], 1)])
    return tab.reshape(2, TT, P, width).transpose(2, 0, 1, 3).reshape(P, -1).astype(np.float32)


def two_tiles(m):
    import numpy as np
    return np.concatenate([m[:P, :P], m[P:, :]], 1)


def pool_means():
    import numpy as np
    out = []
    for w in (2, 4, 8, 16):
        m = np.zeros((SEQ, SEQ), np.float64)
        for q in range(SEQ):
            lo = max(q + 1 - w, 0)
            m[q, lo:q + 1] = 1.0 / (q + 1 - lo)
            m[q, q] -= 1.0
        mt = m.T
        out.append(np.concatenate([mt[:P, :], mt[P:, P:]], 1))
    return np.concatenate(out, 1).astype(np.float32)


def dil_diff_pieces(w, w_out):
    out = [up_pieces(w, slice(c * 512, (c + 1) * 512)) for c in (3, 4, 5, 0, 1, 2)]
    return out + [down_pieces(w_out[512:]), down_pieces(w_out[:512])]


def delta_ret_pieces(w, w_out):
    out = [up_pieces(w, slice(c, c + 512)) for c in (512, 0, 1024, 1536, 2056, 2568, 3080)]
    return out + [down_pieces(w_out[512:]), down_pieces(w_out[:512])]


def delta_ret_constants():
    import numpy as np
    i, j = np.arange(P)[:, None], np.arange(P)[None, :]
    same = i // 64 == j // 64
    f = lambda m: np.asarray(m, np.float32)
    levels = [f((i >> (l + 1) == j >> (l + 1)) & ((i >> l) % 2 == 0) & ((j >> l) % 2 == 1)) for l in range(6)]
    gamma = 1.0 - 2.0 ** (-5.0 - np.arange(4, dtype=np.float64))
    d = np.arange(SEQ)[None, :] - np.arange(P)[:, None]
    ret = [f(np.where(d >= 0, g ** np.maximum(d, 0), 0.0)) for g in gamma]
    return {"g_ones": f(np.ones((P, P))), "g_before": f((i <= j) & same), "g_after": f((i > j) & same),
            "g_sub": np.concatenate([f((i < 64) & (j >= 0)), f((i >= 64) & (j >= 0))], 1),
            "g_below": f(np.where((i <= j) & same, 0.0, NEG)), "g_level": np.concatenate(levels, 1),
            "g_ret": np.concatenate(ret, 1), "g_rope": rope_table(64), "g_zeros": np.zeros((P, 12), np.float32)}


def constants():
    import numpy as np
    q, k = np.arange(SEQ)[:, None], np.arange(SEQ)[None, :]
    causal = two_tiles(np.where(k <= q, 0.0, NEG).astype(np.float32))
    dist = q - k
    count = ((dist >= 0) & (dist <= 128)) + 0.0 + ((dist >= 0) & (dist % 4 == 0)) + ((dist >= 0) & (dist % 16 == 0))
    log_count = two_tiles(np.where(count > 0, np.log(np.maximum(count, 1)), NEG).astype(np.float32))
    return {"b_mask": causal, "b_mask_dil": log_count, "b_rope": rope_table(64), "b_rope_wide": rope_table(128),
            "ident": np.eye(P, dtype=np.float32), "a_pool_mean": pool_means(), "a_mask": causal,
            "a_rope": rope_table(64)}


def kernel(**inputs):
    import numpy as np
    import concourse.bacc as bacc
    from concourse.bass_utils import run_bass_kernel_spmd

    a = {k: np.asarray(v) for k, v in inputs.items()}
    program = PROGRAM
    first = lambda i: [ffn_pieces(a["ffn1_w_gate_up"][i], a["ffn1_w_down"][i]), first_block_pieces(a, i),
                       ffn_pieces(a["ffn2_w_gate_up"][i], a["ffn2_w_down"][i])]
    second = lambda i, mixer: [ffn_pieces(a[f"l{i}_ffn1_w_up_2"], a[f"l{i}_ffn1_w_down_2"]),
                               mixer(a[f"l{i}_w_in_2"], a[f"l{i}_w_out_2"]),
                               ffn_pieces(a[f"l{i}_ffn2_w_up_2"], a[f"l{i}_ffn2_w_down_2"])]
    phases = first(0) + first(1) + second(0, delta_ret_pieces) + second(1, dil_diff_pieces)
    gains = [a[n][i] for i in range(2) for n in ("ffn1_norm", "mix_norm", "ffn2_norm")]
    gains += [a[f"l{i}_{n}_norm_2"] for i in range(2) for n in ("ffn1", "mix", "ffn2")]
    if USE is not None:
        phases, gains = [phases[i] for i in USE], [gains[i] for i in USE]
    weights = np.concatenate([m for phase in phases for m in phase])
    conv = np.concatenate([a["l0_conv_w_2"][:, c:c + 512] for c in (512, 0, 1024)], 1)
    arrays = {"x": a["x"].reshape(SEQ, D), "weights": weights, "gains": np.stack(gains + [a["final_norm_2"]]).reshape(-1, KT, P).transpose(2, 0, 1).reshape(P, -1),
              "final_gain": a["final_norm_2"][None, :],
              "g_gdn_norm": a["l0_gdn_norm_2"][None, :],
              "g_conv": conv.reshape(4, 12, P).transpose(2, 1, 0).reshape(P, 48),
              "g_alog_dt": np.concatenate([a["l0_a_log_2"], a["l0_dt_bias_2"]])[None, :],
              "g_ba": a["l0_w_in_2"][:, 2048:2056].reshape(KT, P, 8).transpose(1, 0, 2).reshape(P, KT * 8),
              "b_lambdas": np.concatenate([a["l1_lambda_" + n + "_2"] for n in ("q1", "k1", "q2", "k2")])[None, :],
              "b_diff_norm": a["l1_diff_norm_2"][None, :],
              "a_pool_w": a["pool_w"].transpose(0, 2, 1, 3).reshape(2, P, 512),
              "a_pool_scale": a["pool_scale"].reshape(2, 4, P).transpose(0, 2, 1),
              "a_qk_norm": np.concatenate([a["q_norm"], a["k_norm"]], 1).reshape(2, 1, 128),
              "a_b_gate": a["b_gate"].reshape(2, 1, 2048)}
    arrays.update(constants())
    arrays.update(delta_ret_constants())
    nc = bacc.Bacc("TRN2", target_bir_lowering=False, num_devices=1)
    tensors = {}
    for name in arrays:
        arrays[name] = np.ascontiguousarray(arrays[name])
        tensors[name] = nc.dram_tensor(name + "_dram", arrays[name].shape, mybir.dt.from_np(arrays[name].dtype), kind="ExternalInput").ap()
    tensors["out"] = nc.dram_tensor("out_dram", (SEQ, D), F32, kind="ExternalOutput").ap()
    build(nc, program, tensors)
    r = run_bass_kernel_spmd(nc, [{k + "_dram": v for k, v in arrays.items()}], core_ids=[0])
    return r.results[0]["out_dram"].reshape(1, SEQ, D)
```

```python
from contextlib import ExitStack
import math

from concourse import mybir

F32 = mybir.dt.float32
F32R = mybir.dt.float32r
ALU = mybir.AluOpType
ACT = mybir.ActivationFunctionType
AX_X = mybir.AxisListType.X

P = 128
SEQ = 256
TT = SEQ // P
D = 1024
KT = D // P
DFF = 2816
LAMBDA_INIT = 0.8 - 0.6 * math.exp(-0.3)
DIL_SCALE = 128 ** -0.5
MIX_FLOATS = 21760
CH = 256
NCH = DFF // CH
EPS = 1e-6
NEG = -1e30
PIECE = 2048
SLOTS = 3


def starts(program, per_phase):
    out = [0]
    for kind in program:
        out.append(out[-1] + per_phase[kind])
    return out


NORMED = {"ffn": 0, "pool_attn": 0, "delta_ret": 1, "dil_diff": 0}
N_PARAMS = {"ffn": 0, "pool_attn": 8, "delta_ret": 14, "dil_diff": 6}
ROPES = {"ffn": 0, "pool_attn": 2, "delta_ret": 1, "dil_diff": 3}
QK_TURNS = {"ffn": 0, "pool_attn": 2, "delta_ret": 0, "dil_diff": 4}
O_TURNS = {"ffn": 0, "pool_attn": 1, "delta_ret": 4, "dil_diff": 4}
BT_SPLITS = {"ffn": 0, "pool_attn": 3, "delta_ret": 4, "dil_diff": 4}
TURNS = {"ffn": 1, "pool_attn": 2, "delta_ret": 1, "dil_diff": 1}
PRODUCTS = {"ffn": 1, "pool_attn": 3, "delta_ret": 1, "dil_diff": 1}
CHUNKS = {"ffn": 0, "pool_attn": 8, "delta_ret": 4, "dil_diff": 6}
ACT_EVACS = {"ffn": 0, "pool_attn": 8, "delta_ret": 8, "dil_diff": 12}
MAPS = {"ffn": 0, "pool_attn": 8, "delta_ret": 0, "dil_diff": 12}
ROUNDS = {"ffn": 0, "pool_attn": 2, "delta_ret": 0, "dil_diff": 6}
HEAD_NORMS = {"ffn": 0, "pool_attn": 2, "delta_ret": 5, "dil_diff": 4}
PROGRAM = ["ffn", "pool_attn", "ffn"] * 2 + ["ffn", "delta_ret", "ffn", "ffn", "dil_diff", "ffn"]
PIECES = {"ffn": 3 * NCH, "pool_attn": 24, "delta_ret": 18, "dil_diff": 16}


def build(nc, program, t):
    n_pieces = sum(PIECES[kind] for kind in program)
    first_piece = starts(program, PIECES)
    turn0 = starts(program, TURNS)
    out0 = starts(program, PRODUCTS)
    chunk0 = starts(program, CHUNKS)
    evac0 = starts(program, ACT_EVACS)
    map0 = starts(program, MAPS)
    round0 = starts(program, ROUNDS)
    head_norm0 = starts(program, HEAD_NORMS)
    rope0 = starts(program, ROPES)
    turned0 = starts(program, QK_TURNS)
    o_turn0 = starts(program, O_TURNS)
    bt0 = starts(program, BT_SPLITS)

    with ExitStack() as ctx:
        def sb(name, shape, dt=F32):
            return ctx.enter_context(nc.sbuf_tensor(name, shape, dt))

        def sem(name):
            return ctx.enter_context(nc.semaphore(name))

        bank = [ctx.enter_context(nc.psum_tensor(f"bank{i}", [P, 512], F32)) for i in range(8)]

        w_raw = [sb(f"w_raw{s}", [P, PIECE]) for s in range(SLOTS)]
        w_hi = [sb(f"w_hi{s}", [P, PIECE], F32R) for s in range(SLOTS)]
        w_lo = [sb(f"w_lo{s}", [P, PIECE], F32R) for s in range(SLOTS)]
        x = sb("x", [P, TT, D])
        xn = sb("xn", [P, TT, D])
        gain = sb("gain", [P, (len(program) + 1) * KT])
        ident = sb("ident", [P, P])
        minus_half = sb("minus_half", [P, 16])
        stat = sb("stat", [P, 3, TT])
        xt_hi = sb("xt_hi", [P, KT, SEQ], F32R)
        xt_lo = sb("xt_lo", [P, KT, SEQ], F32R)
        gate = sb("gate", [P, TT, CH])
        hid = sb("hid", [P, TT, CH])
        ht_hi = sb("ht_hi", [P, 2, SEQ], F32R)
        ht_lo = sb("ht_lo", [P, 2, SEQ], F32R)

        bt_hi = sb("bt_hi", [P, 4, SEQ], F32R)
        bt_lo = sb("bt_lo", [P, 4, SEQ], F32R)
        mix = sb("mix", [P, MIX_FLOATS])
        expsum = sb("expsum", [P, 2, TT, 8])
        negmax = sb("negmax", [P, 2, TT])
        hstat = sb("hstat", [P, 3, 16])

        def carve(sizes):
            parts, at = {}, 0
            for name, size in sizes.items():
                parts[name] = mix[:, at:at + size]
                at += size
            assert at <= MIX_FLOATS, at
            return parts

        landed = [sem(f"weights_landed{s}") for s in range(SLOTS)]
        hi_done = sem("hi_done")
        lo_done = sem("lo_done")
        used = sem("piece_used")
        x_in = [sem(f"x_in{i}") for i in range(3)]
        first_landed = [sem(f"first_piece_landed{q}") for q in range(4)]
        first_hi = sem("first_piece_hi")
        table_loaded = sem("act_table_loaded")
        cq_steps = sem("cq_rotation_steps")
        cq_ready = sem("cq_rotated")
        first_lo = sem("first_piece_lo")
        merged_ready = sem("branches_merged")
        id_in = sem("ident_in")
        gain_in = sem("gain_in")
        x_ready = sem("x_ready")
        ss_done = sem("squares_summed")
        xn_ready = sem("xn_ready")
        xt_done = sem("xt_transposed")
        xt_hi_done = sem("xt_hi_done")
        xt_lo_done = sem("xt_lo_done")
        up_done = sem("up_done")
        gate_ready = sem("gate_ready")
        hid_ready = sem("hid_ready")
        ht_done = sem("ht_transposed")
        ht_hi_done = sem("ht_hi_done")
        ht_lo_done = sem("ht_lo_done")
        out_done = sem("out_product_done")
        dve_step = sem("dve_step")
        stored = sem("stored")
        params_in = sem("mixer_params_in")
        proj_done = sem("chunk_tile0_done")
        act_evac = sem("chunk_tile_taken_by_act")
        gate_added = sem("gate_bias_added")
        hsq_done = sem("head_squares_done")
        hmean_ready = sem("head_mean_ready")
        hrstd_ready = sem("head_rstd_ready")
        diff_done = sem("pool_difference_done")
        diff_ready = sem("pool_difference_ready")
        y_done = sem("pool_product_done")
        bt_hi_done = sem("bt_hi_done")
        bt_lo_done = sem("bt_lo_done")
        qk_ready = sem("qk_roped")
        qkt_done = sem("qk_transposed")
        qkt_ready = sem("qk_transpose_ready")
        s_done = sem("scores_done")
        s_masked = sem("scores_masked")
        max_ready = sem("max_ready")
        exp_done = sem("exp_done")
        pt_done = sem("probs_transposed")
        pt_ready = sem("probs_transpose_ready")
        pv_done = sem("pv_done")
        o_ready = sem("attention_round_ready")
        ot_done = sem("attention_transposed")
        gates_ready = sem("gates_ready")
        branch_ready = sem("branch_gated")
        M = {name: sem("delta_" + name) for name in (
            "ba_hi", "ba_split", "ba_t_done", "ba_t_copied", "ba_done", "abs_ready", "exps_ready", "softplus_ready", "g_ready", "ug_ready", "sums_done",
            "gcum_copied", "e4_ready", "diff_done", "diff_ready", "decay_ready", "ct_ready", "conv_ready",
            "co_ready", "co_turned", "tm_ready", "normed", "kb_ready", "kt_turned", "kt_ready", "kbt_turned", "kbt_ready",
            "qt_turned", "qt_ready", "qd_ready", "qdt_turned", "qdt_ready", "at_done", "at_ready", "qk_done", "qk_masked",
            "xt0_ready", "x0_turned", "x0_ready", "level_masked", "t1_done", "t1_ready", "y_done", "x_updated",
            "vb_ready", "kbe_ready", "kd_ready", "u_done", "u_ready", "wt_done", "wt_ready", "rqk_turned", "rqk_ready",
            "rs_done", "rs_ready", "ro_done", "ro_ready", "half_normed", "vw_done", "vn_ready",
            "ds_done", "s_ready", "o_done", "gz_ready")}
        ba_hi = sb("ba_hi", [P, KT * 8], F32R)
        ba_lo = sb("ba_lo", [P, KT * 8], F32R)
        lam_sums = sem("lambda_sums")
        lam_exp = sem("lambda_exponentials")
        diff_normed = sem("diff_normed")
        mean_ready = sem("mean_square_ready")
        rstd_ready = sem("rstd_ready")
        half_ready = sem("minus_half_ready")

        block = ctx.enter_context(nc.Block())
        norms = len(program) + 1
        normed0 = starts(program, NORMED)
        late = [not NORMED[kind] for kind in program] + [False]

        def params_at(k):
            return 16 * sum(N_PARAMS[kind] for kind in program[:k + 1])

        def steps_of(p, first, shift):
            return [2 * (p - first) + tt + shift for tt in range(TT) if p >= first - 1 and 2 * (p - first) + tt + shift >= 0]

        def hidden_parts(c):
            if isinstance(c, int) and c == NCH - 1:
                return bt_hi[:, 0:2, :], bt_lo[:, 0:2, :]
            return ht_hi[:, :, :], ht_lo[:, :, :]

        beside = (ht_hi[:, :, :], ht_lo[:, :, :])
        first_half = (bt_hi[:, 0:2, :], bt_lo[:, 0:2, :])
        second_half = (bt_hi[:, 2:4, :], bt_lo[:, 2:4, :])

        def up_view(w, k):
            return w[:, k * 512:(k + 1) * 512]

        def down_view(w, k, h):
            return w[:, k * 1024 + h * 512:k * 1024 + (h + 1) * 512]

        def retention_probs(h):
            buf = G["qt_pr"] if h < 2 else G["decay_oa"]
            return buf[:, (h % 2) * 384:(h % 2) * 384 + 384]

        def psum3(b, k):
            return bank[b][:, :].rearrange("p (k q) -> p k q", k=k)

        A = carve(dict(probs=768, probs_t=768, u=1024, q=1024, k=1024, v=1024, sq=1024, rot=1024, qt=1024,
                       kt=1024, gates=4096, pool_w=512, pool_scale=4, qk_norm=128, pool_mean=1536,
                       mask=384, rope=256, rope_g=512))
        B = carve(dict(probs=768, probs_t=768, cq=1024, ck=1024, cv=1024, dq=1024, dk=1024, dv=1024, rot=1024, rot_q=1024,
                       cqt=1024, ckt=1024, dqt=1024, dkt=1024, diff=1024, sq=1024, prod=256,
                       mask=384, mask_dil=384, rope=256, rope_wide=512, lambdas=256, diff_norm=128, lam=8))
        B_PARAMS = ("mask", "mask_dil", "rope", "rope_wide", "lambdas", "diff_norm")
        G = carve(dict(ct_co=4120, k_kd=1024, q_qd_u=1024, v_vb=1024, kb_kbe=1024, gz=1024, rqk_ob=1024, rv=1024,
                       rg=1024, decay_oa=1024, kt_rt=1024, qt_pr=1024, kbt_wt=1024, qdt=1024,
                       ones=128, before=128, after=128, sub=256, below=128, level=768, ret=1024, rope=256,
                       gdn_norm=128, conv=48, alog_dt=8, ba=64, gates=64, e4=32, gc=8))
        G_PARAMS = ("ones", "before", "after", "sub", "below", "level", "ret", "rope", "gdn_norm", "conv", "alog_dt", "ba")
        ct = [G["ct_co"][:, i * 1036:(i + 1) * 1036].rearrange("p (c q) -> p c q", c=4) for i in range(2)]
        co = [G["ct_co"][:, 2072 + i * 1024:2072 + (i + 1) * 1024].rearrange("p (c q) -> p c q", c=4) for i in range(2)]
        mats = lambda v: v.rearrange("p (t h q) -> p t h q", t=TT, h=4)
        inv, inv_t, prod1, lev = (mats(G["ct_co"][:, i * 1024:(i + 1) * 1024]) for i in range(4))
        at_m = mats(xn[:, 0, :])
        qk_m = mats(xn[:, 1, :])
        state = gate[:, :, :].rearrange("p t c -> p (t c)").rearrange("p (h e) -> p h e", h=4)
        v_new = hid[:, :, :].rearrange("p t c -> p (t c)").rearrange("p (h e) -> p h e", h=4)
        A_PARAMS = ("pool_w", "pool_scale", "qk_norm", "pool_mean", "mask", "rope")
        tok = lambda v, d=512: v.rearrange("p (t d) -> p t d", t=TT)
        heads = lambda v, w=64: v.rearrange("p (t h d) -> p t h d", t=TT, d=w)

        def causal_map(q_t, k_t, off, width):
            return [(q_t[off:off + width, 0:P], k_t[off:off + width, 0:P]),
                    (q_t[off:off + width, P:SEQ], k_t[off:off + width, 0:SEQ])]

        @block.sync
        def _(sp):
            for h in range(2):
                sp.dma_start(x[:, 0, h * 512:(h + 1) * 512], t["x"][0:P, h * 512:(h + 1) * 512]).then_inc(x_in[h], 16)
                for q in (2 * h, 2 * h + 1):
                    sp.dma_start(w_raw[0][:, q * 512:(q + 1) * 512], t["weights"][0][:, q * 512:(q + 1) * 512]).then_inc(first_landed[q], 16)
            sp.dma_start(x[:, 1, :], t["x"][P:SEQ, :]).then_inc(x_in[2], 16)
            for s in range(1, SLOTS):
                sp.dma_start(w_raw[s][:, :], t["weights"][s]).then_inc(landed[s], 16)
            rounds = n_pieces // SLOTS
            with sp.Fori(1, rounds) as i:
                for s in range(SLOTS):
                    sp.wait_ge(lo_done, i * SLOTS + (s + 1 - SLOTS))
                    sp.dma_start(w_raw[s][:, :], t["weights"][i * SLOTS + s]).then_inc(landed[s], 16)
            for m in range(rounds * SLOTS, n_pieces):
                s = m % SLOTS
                sp.wait_ge(lo_done, m + 1 - SLOTS)
                sp.dma_start(w_raw[s][:, :], t["weights"][m]).then_inc(landed[s], 16)
            for tt in range(TT):
                sp.wait_ge(xn_ready, TT * normed0[-1] + tt + 1)
                sp.dma_start(t["out"][tt * P:(tt + 1) * P, :], xn[:, tt, :]).then_inc(stored, 16)
            sp.wait_ge(stored, 16 * TT)

        @block.gpsimd
        def _(pool):
            def rstd(k, tt):
                pool.wait_ge(mean_ready, TT * k + tt + 1)
                nc.gpsimd.tensor_tensor(stat[:, 2, tt:tt + 1], stat[:, 1, tt:tt + 1], minus_half[:, 0:1], ALU.pow).then_inc(rstd_ready, 1)

            pool.dma_start(ident[:, :], t["ident"]).then_inc(id_in, 16)
            pool.dma_start(gain[:, :], t["gains"]).then_inc(gain_in, 16)
            pool.memset(minus_half[:, :], -0.5).then_inc(half_ready, 1)
            pool.wait_ge(half_ready, 1)

            def head_rstd(i, n, at=0):
                pool.wait_ge(hmean_ready, i + 1)
                nc.gpsimd.tensor_tensor(hstat[:, 2, at:at + n], hstat[:, 1, at:at + n], minus_half[:, 0:n], ALU.pow).then_inc(hrstd_ready, 1)

            def load_pool_attn(i):
                for name in A_PARAMS:
                    src = t["a_" + name][i] if name in ("pool_w", "pool_scale", "qk_norm") else t["a_" + name]
                    pool.dma_start(A[name], src.to_broadcast([P, 128]) if name == "qk_norm" else src).then_inc(params_in, 16)
                for tt in range(TT):
                    pool.dma_start(tok(A["gates"])[:, tt, :], t["a_b_gate"][i].to_broadcast([P, 2048])).then_inc(params_in, 16)

            def rotate_cq(k):
                pool.wait_ge(act_evac, evac0[k] + 8)
                q, rot = heads(B["cq"], P), heads(B["rot_q"], P)
                tab = B["rope_wide"].rearrange("p (c t d) -> p c t d", c=2, t=TT)
                b = lambda v: v.unsqueeze(2).broadcast_to([P, TT, 4, v.shape[2]])
                nc.gpsimd.tensor_tensor(rot[:, :, :, 0:64], q[:, :, :, 64:P], b(tab[:, 1, :, 0:64]), ALU.mult)
                nc.gpsimd.tensor_tensor(rot[:, :, :, 64:P], q[:, :, :, 0:64], b(tab[:, 1, :, 64:P]), ALU.mult).then_inc(cq_steps, 1)
                pool.wait_ge(cq_steps, 1)
                nc.gpsimd.tensor_tensor(q, q, b(tab[:, 0]), ALU.mult).then_inc(cq_steps, 1)
                pool.wait_ge(cq_steps, 2)
                nc.gpsimd.tensor_tensor(q, q, rot, ALU.add).then_inc(cq_ready, 1)

            def load_dil_diff():
                for name in B_PARAMS:
                    src = t["b_" + name]
                    pool.dma_start(B[name], src.to_broadcast([P, src.shape[1]]) if src.shape[0] == 1 else src).then_inc(params_in, 16)

            def load_delta_ret():
                for name in G_PARAMS:
                    src = t["g_" + name]
                    pool.dma_start(G[name], src.to_broadcast([P, src.shape[1]]) if src.shape[0] == 1 else src).then_inc(params_in, 16)
                for c in ct:
                    pool.dma_start(c[:, :, 0:3], t["g_zeros"].rearrange("p (c q) -> p c q", c=4)).then_inc(params_in, 16)

            def delta_ret(k):
                h0 = head_norm0[k]
                per_head = lambda v: v.rearrange("p (n w) -> p n w", w=P)

                def scaled(name, by, ready):
                    v = per_head(G[name])
                    nc.gpsimd.tensor_tensor(v, v, by.unsqueeze(2).broadcast_to([P, 8, P]), ALU.mult).then_inc(M[ready], 1)

                head_rstd(h0, 8)
                head_rstd(h0 + 1, 8)
                pool.wait_ge(M["kbt_turned"], 1)
                pool.wait_ge(M["e4_ready"], 1)
                scaled("kb_kbe", G["e4"][:, 0:8], "kbe_ready")
                pool.wait_ge(M["kt_turned"], 1)
                scaled("k_kd", G["e4"][:, 8:16], "kd_ready")
                pool.wait_ge(M["tm_ready"], 3)
                scaled("v_vb", G["gates"][:, 56:64], "vb_ready")
                for l in range(1, 6):
                    if l == 1:
                        pool.wait_ge(M["x0_ready"], 1)
                    else:
                        pool.wait_ge(M["t1_done"], TT * (l - 1))
                    m = G["level"][:, l * P:(l + 1) * P].unsqueeze(1).broadcast_to([P, 8, P])
                    nc.gpsimd.tensor_tensor(lev.rearrange("p t h q -> p (t h) q"), at_m.rearrange("p t h q -> p (t h) q"),
                                            m, ALU.mult).then_inc(M["level_masked"], 1)
                head_rstd(h0 + 2, 8)
                pool.wait_ge(act_evac, evac0[k] + 8)
                gz = per_head(G["gz"])
                nc.gpsimd.tensor_tensor(gz, gz, G["gdn_norm"].unsqueeze(1).broadcast_to([P, 8, P]), ALU.mult).then_inc(M["gz_ready"], 1)
                for tt in range(TT):
                    head_rstd(h0 + 3 + tt, 4, 4 * tt)

            seen = {"pool_attn": 0, "delta_ret": 0, "dil_diff": 0}

            def load_params(k):
                kind = program[k] if k < len(program) else "ffn"
                if kind == "pool_attn":
                    load_pool_attn(seen[kind])
                if kind == "dil_diff":
                    load_dil_diff()
                if kind == "delta_ret":
                    load_delta_ret()
                if kind != "ffn":
                    seen[kind] += 1

            load_params(0)
            for k in range(norms):
                for tt in range(TT):
                    rstd(k, tt)
                if k == len(program):
                    break
                if k == len(program) - 1:
                    pool.wait_ge(params_in, params_at(k))
                    pool.dma_start(mix[:, 0:D], t["final_gain"].to_broadcast([P, D])).then_inc(params_in, 16)
                if program[k] == "ffn":
                    load_params(k + 1)
                if program[k] == "pool_attn":
                    head_rstd(head_norm0[k], 16)
                    head_rstd(head_norm0[k] + 1, 16)
                if program[k] == "dil_diff":
                    rotate_cq(k)
                    for h in range(4):
                        head_rstd(head_norm0[k] + h, 2, 2 * h)
                if program[k] == "delta_ret":
                    delta_ret(k)

        @block.scalar
        def _(act):
            def split_hi(m, s, first_in_slot=False):
                if m == 0:
                    for q in range(4):
                        part = slice(q * 512, (q + 1) * 512)
                        act.wait_ge(first_landed[q], 16)
                        nc.scalar.activation(w_hi[0][:, part], w_raw[0][:, part], ACT.Copy).then_inc(
                            hi_done if q == 3 else first_hi, 1)
                    return
                act.wait_ge(landed[s], landed_count(m, s))
                if not first_in_slot:
                    act.wait_ge(used, m + (1 - SLOTS))
                nc.scalar.activation(w_hi[s][:, :], w_raw[s][:, :], ACT.Copy).then_inc(hi_done, 1)

            def landed_count(m, s):
                return 16 * (m // SLOTS + (1 if s else 0))

            def squares(k):
                for tt in range(TT):
                    if k == 0:
                        act.wait_ge(x_in[tt], 16)
                        act.wait_ge(x_in[1 + tt], 16)
                    else:
                        act.wait_ge(x_ready, 4 * (k - 1) + 2 * tt + 2)
                    nc.scalar.activation(xn[:, tt, :], x[:, tt, :], ACT.Square,
                                         accum_out=stat[:, 0, tt:tt + 1]).then_inc(ss_done, 1)

            def xt_high(turn, norm=None, halves=range(4)):
                for j in halves:
                    tt, g = j // 2, j % 2
                    act.wait_ge(xt_done, 4 * turn + j + 1)
                    toks = slice(tt * P, (tt + 1) * P)
                    if norm is None:
                        nc.scalar.activation(xt_hi[:, 4 * g:4 * g + 4, toks], psum3(4 + j, 4), ACT.Copy).then_inc(xt_hi_done, 1)
                        continue
                    for q in range(4):
                        c = norm * KT + 4 * g + q
                        ins = nc.scalar.activation(xt_hi[:, 4 * g + q, toks], psum3(4 + j, 4)[:, q, :], ACT.Copy,
                                                   scale=gain[:, c:c + 1])
                    ins.then_inc(xt_hi_done, 1)

            def ffn(f, k):
                base = first_piece[k]

                def gates(c):
                    for tt in range(TT):
                        if tt == 0:
                            act.wait_ge(up_done, c + (NCH * f + 1))
                        else:
                            act.wait_ge(used, base + 2 if isinstance(c, int) and c == 0 else c * SLOTS + (base + 1))
                        b = bank[tt if isinstance(c, int) and c == 0 else 4 + tt]
                        nc.scalar.activation(gate[:, tt, :], b[:, 0:CH], ACT.Silu, scale=stat[:, 2, tt:tt + 1]).then_inc(gate_ready, 1)

                def ht_high(c):
                    act.wait_ge(ht_done, c + (NCH * f + 1))
                    nc.scalar.activation(hidden_parts(c)[0], bank[6][:, :].rearrange("p (k q) -> p k q", k=2),
                                         ACT.Copy).then_inc(ht_hi_done, 1)

                def step(c):
                    m = base + 2 - SLOTS + c * SLOTS
                    ht_high(c - 1)
                    ahead(m, 2, c)
                    ahead(m, 3, c)
                    gates(c)
                    ahead(m, 4, c)

                def ahead(m, j, c):
                    s = (base + 2 + j) % SLOTS
                    if isinstance(c, int):
                        if m + j < n_pieces:
                            split_hi(m + j, s)
                        return
                    q = (base - 1 + j) // SLOTS
                    act.wait_ge(landed[s], c * 16 + 16 * (q + (1 if s else 0)))
                    act.wait_ge(used, c * SLOTS + (base - 1 + j + 1 - SLOTS))
                    nc.scalar.activation(w_hi[s][:, :], w_raw[s][:, :], ACT.Copy).then_inc(hi_done, 1)

                split_hi(base + 2, (base + 2) % SLOTS, base + 2 < SLOTS)
                act.wait_ge(rstd_ready, TT * (k + 1))
                gates(0)
                split_hi(base + 3, (base + 3) % SLOTS)
                step(1)
                with act.Fori(2, NCH - 1) as c:
                    step(c)
                step(NCH - 1)
                ht_high(NCH - 1)
                if base + 34 < n_pieces:
                    split_hi(base + 34, (base + 34) % SLOTS)

            def ahead(m):
                if m + 2 < n_pieces:
                    split_hi(m + 2, (m + 2) % SLOTS, m + 2 < SLOTS)

            def chunk_tile(k, j, tt, skipped):
                if tt == 0:
                    act.wait_ge(proj_done, chunk0[k] + j + 1 - skipped)
                else:
                    act.wait_ge(used, first_piece[k] + 2 * j + 2)

            def take(k, j, dst, func=ACT.Copy, skipped=0):
                if j == 0:
                    act.wait_ge(rstd_ready, TT * (k + 1))
                for tt in range(TT):
                    chunk_tile(k, j, tt, skipped)
                    nc.scalar.activation(dst[:, tt, :], bank[2 * (j % 2) + tt][:, :], func,
                                         scale=stat[:, 2, tt:tt + 1] if late[k] else 1.0).then_inc(act_evac, 1)

            def exp_map(g, i):
                act.wait_ge(max_ready, g + 1)
                pr = A["probs"][:, (g % 2) * 384:(g % 2) * 384 + 384]
                for tt, cols in enumerate((slice(0, P), slice(P, 3 * P))):
                    ins = nc.scalar.activation(pr[:, cols], pr[:, cols], ACT.Exp, bias=negmax[:, g % 2, tt:tt + 1],
                                               accum_out=expsum[:, 0, tt, i:i + 1])
                ins.then_inc(exp_done, 1)

            def take_probs(g):
                act.wait_ge(pt_done, g + 1)
                if g >= 2:
                    act.wait_ge(pv_done, g - 1)
                nc.scalar.activation(A["probs_t"][:, (g % 2) * 384:(g % 2) * 384 + 384], bank[6][:, 0:384], ACT.Copy).then_inc(pt_ready, 1)

            def pair_high(src, dst):
                nc.scalar.activation(dst[0], psum3(src, 2), ACT.Copy).then_inc(bt_hi_done, 1)

            def bt_high(src, scale=None):
                for b in range(2):
                    for r in range(2):
                        ins = nc.scalar.activation(bt_hi[:, 2 * b + r, :], psum3(src + b, 2)[:, r, :], ACT.Copy,
                                                   scale=1.0 if scale is None else scale[:, 2 * b + r:2 * b + r + 1])
                ins.then_inc(bt_hi_done, 1)

            def pool_attn(k, i):
                n0, e0, g0 = first_piece[k], evac0[k], map0[k]
                u, q, kk, v = (tok(A[name]) for name in ("u", "q", "k", "v"))
                for p in range(PIECES["pool_attn"]):
                    ahead(n0 + p)
                    if p == 1:
                        take(k, 0, u)
                    if p == 3:
                        take(k, 1, q)
                        act.wait_ge(act_evac, e0 + 4)
                        nc.scalar.activation(A["sq"], A["q"], ACT.Square).then_inc(hsq_done, 1)
                        act.wait_ge(diff_done, i + 1)
                        for b in range(2):
                            ins = nc.scalar.activation(A["qt"][:, b * 512:(b + 1) * 512], bank[4 + b][:, :], ACT.Copy)
                        ins.then_inc(diff_ready, 1)
                    if p == 5:
                        take(k, 2, kk)
                        act.wait_ge(act_evac, e0 + 6)
                        act.wait_ge(hmean_ready, head_norm0[k] + 1)
                        nc.scalar.activation(A["sq"], A["k"], ACT.Square).then_inc(hsq_done, 1)
                        act.wait_ge(params_in, params_at(k))
                        act.wait_ge(y_done, i + 1)
                        bt_high(6, A["pool_scale"])
                    if p == 7:
                        take(k, 3, v)
                        turned_qk(2 * i, "qt", 4)
                    if p == 8:
                        turned_qk(2 * i + 1, "kt", 6)
                    for step in steps_of(p, 9, 0):
                        if 2 <= step < 10:
                            take_probs(g0 + step - 2)
                        if step < 8:
                            exp_map(g0 + step, step)
                    if p == 13 or p == 16:
                        act.wait_ge(gate_added, 8 * i + (4 if p == 13 else 8))
                        gs = tok(A["gates"])[:, :, (0 if p == 13 else D):(D if p == 13 else 2 * D)]
                        nc.scalar.activation(gs, gs, ACT.Sigmoid).then_inc(gates_ready, 1)
                    if p == 15:
                        act.wait_ge(ot_done, o_turn0[k] + 1)
                        pair_high(4, beside)
                    if p == 16:
                        act.wait_ge(used, n0 + 17)
                        pair_high(5, first_half)
                    if p == 19:
                        xt_high(turn0[k] + 1)

            def copy_banks(b0, dst, ready):
                for b in range(2):
                    ins = nc.scalar.activation(dst[:, b * 512:(b + 1) * 512], bank[b0 + b][:, :], ACT.Copy)
                ins.then_inc(M[ready], 1)

            def delta_ret(k):
                n0 = first_piece[k]
                gates, e4 = G["gates"], G["e4"]

                def take_channels(i):
                    act.wait_ge(used, n0 + 2 * i + 2)
                    if i == 2:
                        act.wait_ge(M["conv_ready"], 1)
                        act.wait_ge(M["co_turned"], 1)
                    b0 = 2 * (i % 2)
                    for b in range(2):
                        nc.scalar.activation(ct[i % 2][:, 2 * b:2 * b + 2, 3:259], psum3(b0 + b, 2), ACT.Copy)
                    for c in range(4):
                        ins = nc.scalar.activation(co[i % 2][:, c, :], psum3(b0 + c // 2, 2)[:, c % 2, :], ACT.Copy,
                                                   scale=G["conv"][:, (4 * i + c) * 4 + 3:(4 * i + c) * 4 + 4])
                    ins.then_inc(M["ct_ready"], 1)

                def silu_conv(i):
                    act.wait_ge(M["conv_ready"], i + 1)
                    nc.scalar.activation(co[i % 2], co[i % 2], ACT.Silu).then_inc(M["co_ready"], 1)

                def take_tokens(i, dst):
                    act.wait_ge(M["co_turned"], i + 1)
                    copy_banks(4, dst, "tm_ready")

                def square(i, src, need=None):
                    if need:
                        act.wait_ge(M[need[0]], need[1])
                    nc.scalar.activation(G["rg"] if i < 2 else G["rv"], src, ACT.Square).then_inc(hsq_done, 1)

                def take_t1(l):
                    for tt in range(TT):
                        act.wait_ge(M["t1_done"], TT * (l - 1) + tt + 1)
                        nc.scalar.activation(prod1[:, tt].rearrange("p h q -> p (h q)"), bank[4 + tt][:, :], ACT.Copy).then_inc(M["t1_ready"], 1)

                def square_output(tt):
                    act.wait_ge(M["o_done"], 2 * tt + 2)
                    for h in range(4):
                        junk = G["rv"][:, (4 * tt + h) * P:(4 * tt + h + 1) * P]
                        ins = nc.scalar.activation(junk, psum3(6 + tt, 4)[:, h, :], ACT.Square,
                                                   accum_out=hstat[:, 0, 4 * tt + h:4 * tt + h + 1])
                    ins.then_inc(hsq_done, 1)

                act.wait_ge(params_in, params_at(k))
                nc.scalar.activation(ba_hi[:, :], G["ba"], ACT.Copy).then_inc(M["ba_hi"], 1)
                for p in range(PIECES["delta_ret"]):
                    ahead(n0 + p)
                    if p == 0:
                        act.wait_ge(M["abs_ready"], 1)
                        nc.scalar.activation(gates[:, 24:32], gates[:, 16:24], ACT.Exp, scale=-1.0)
                        nc.scalar.activation(gates[:, 32:36], G["alog_dt"][:, 0:4], ACT.Exp)
                        nc.scalar.activation(gates[:, 48:56], gates[:, 40:48], ACT.Exp, scale=-1.0).then_inc(M["exps_ready"], 1)
                        act.wait_ge(M["exps_ready"], 1)
                        nc.scalar.activation(gates[:, 24:32], gates[:, 24:32], ACT.Ln, bias=1.0).then_inc(M["softplus_ready"], 1)
                    if p == 1:
                        act.wait_ge(M["gcum_copied"], 1)
                        nc.scalar.activation(e4, bank[5][:, 0:32], ACT.Exp).then_inc(M["e4_ready"], 1)
                        take_channels(0)
                    if p == 2:
                        act.wait_ge(M["diff_ready"], 1)
                        nc.scalar.activation(G["decay_oa"], G["decay_oa"], ACT.Exp).then_inc(M["decay_ready"], 1)
                    if p == 3:
                        silu_conv(0)
                        take_channels(1)
                        take_tokens(0, G["k_kd"])
                        square(0, G["k_kd"], ("tm_ready", 1))
                    if p == 5:
                        silu_conv(1)
                        take_channels(2)
                        take_tokens(1, G["q_qd_u"])
                        act.wait_ge(hmean_ready, head_norm0[k] + 1)
                        square(1, G["q_qd_u"], ("tm_ready", 2))
                    if p == 6:
                        act.wait_ge(M["kt_turned"], 1)
                        copy_banks(6, G["kt_rt"], "kt_ready")
                        silu_conv(2)
                        act.wait_ge(M["kbt_turned"], 1)
                        copy_banks(4, G["kbt_wt"], "kbt_ready")
                    if p == 7:
                        take_tokens(2, G["v_vb"])
                        act.wait_ge(M["qt_turned"], 1)
                        copy_banks(6, G["qt_pr"], "qt_ready")
                        take(k, 3, tok(G["rqk_ob"]), ACT.Copy, 3)
                    if p == 8:
                        act.wait_ge(M["qdt_turned"], 1)
                        copy_banks(6, G["qdt"], "qdt_ready")
                    if p == 9:
                        act.wait_ge(M["x0_turned"], 1)
                        copy_banks(4, inv.rearrange("p t h q -> p (t h q)"), "x0_ready")
                        take(k, 4, tok(G["rv"]), ACT.Copy, 3)
                        take_t1(1)
                        act.wait_ge(M["rqk_turned"], 1)
                        copy_banks(6, G["kt_rt"], "rqk_ready")
                    if p == 10:
                        take_t1(2)
                    if p == 11:
                        take(k, 5, tok(G["rg"]), ACT.Silu, 3)
                        take_t1(3)
                    if p == 12:
                        take_t1(4)
                        act.wait_ge(M["ro_done"], 1)
                        copy_banks(6, G["rqk_ob"], "ro_ready")
                        act.wait_ge(M["ro_ready"], 1)
                        square(2, G["rqk_ob"])
                    if p == 13:
                        take(k, 6, tok(G["gz"]), ACT.Silu, 3)
                        take_t1(5)
                        for pair, half in enumerate((first_half, second_half)):
                            act.wait_ge(ot_done, o_turn0[k] + 1 + pair)
                            pair_high(2 + pair, half)
                        act.wait_ge(M["u_done"], 1)
                        copy_banks(4, G["q_qd_u"], "u_ready")
                        act.wait_ge(M["wt_done"], 1)
                        copy_banks(6, G["kbt_wt"], "wt_ready")
                    if p == 14:
                        square_output(0)
                    if p == 15:
                        square_output(1)
                        for pair, half in enumerate((beside, first_half)):
                            act.wait_ge(ot_done, o_turn0[k] + 3 + pair)
                            pair_high(4 + pair, half)

            def dil_diff(k):
                n0, g0, c0 = first_piece[k], map0[k], turned0[k]
                order = ("dq", "dk", "dv", "cq", "ck", "cv")
                d4, sq = heads(B["diff"], P), B["sq"].rearrange("p (n w) -> p n w", w=P)
                act.wait_ge(lam_sums, 1)
                nc.scalar.activation(B["lam"][:, 2:4], B["lam"][:, 0:2], ACT.Exp).then_inc(lam_exp, 1)

                def square_head(h):
                    act.wait_ge(o_ready, round0[k] + h + 1)
                    for tt in range(TT):
                        c = 2 * h + tt
                        ins = nc.scalar.activation(sq[:, c, :], d4[:, tt, h], ACT.Square, accum_out=hstat[:, 0, c:c + 1])
                    ins.then_inc(hsq_done, 1)

                for p in range(PIECES["dil_diff"]):
                    ahead(n0 + p)
                    for step in steps_of(p, 6, 1):
                        if 2 <= step < 10:
                            take_probs(g0 + step - 2)
                        if step < 8:
                            exp_map(g0 + step, step)
                        if step in (5, 7, 9):
                            square_head((step - 5) // 2)
                    if p == 10:
                        turned_qk(c0 + 2, "cqt", 4, B)
                        square_head(3)
                    if p == 11:
                        act.wait_ge(ot_done, o_turn0[k] + 1)
                        pair_high(6, first_half)
                        turned_qk(c0 + 3, "ckt", 4, B)
                    if p % 2 and p < 12:
                        take(k, p // 2, tok(B[order[p // 2]]))
                    if p == 3:
                        turned_qk(c0, "dqt", 4, B)
                    if p == 4:
                        turned_qk(c0 + 1, "dkt", 6, B)
                    if p == 11:
                        act.wait_ge(ot_done, o_turn0[k] + 2)
                        pair_high(7, second_half)
                        exp_map(g0 + 8, 0)
                        exp_map(g0 + 9, 1)
                    if p == 12:
                        take_probs(g0 + 8)
                        take_probs(g0 + 9)
                        exp_map(g0 + 10, 2)
                        exp_map(g0 + 11, 3)
                    if p == 13:
                        take_probs(g0 + 10)
                        take_probs(g0 + 11)
                        act.wait_ge(ot_done, o_turn0[k] + 3)
                        pair_high(4, beside)
                    if p == 14:
                        act.wait_ge(ot_done, o_turn0[k] + 4)
                        pair_high(5, first_half)

            def turned_qk(c, name, b0, bufs=A):
                act.wait_ge(qkt_done, c + 1)
                for b in range(2):
                    ins = nc.scalar.activation(bufs[name][:, b * 512:(b + 1) * 512], bank[b0 + b][:, :], ACT.Copy)
                ins.then_inc(qkt_ready, 1)

            seen = {"pool_attn": 0}
            f = 0
            for k, kind in enumerate(program):
                if k == 0:
                    act.wait_ge(half_ready, 1)
                    nc.scalar.activation(hstat[:, 0, :], minus_half[:, :], ACT.Copy).then_inc(table_loaded, 1)
                    act.wait_ge(gain_in, 16)
                    xt_high(0, 0, (0, 1))
                    split_hi(0, 0, True)
                    xt_high(0, 0, (2, 3))
                    split_hi(1, 1, True)
                    squares(0)
                elif late[k]:
                    xt_high(turn0[k], k)
                    squares(k)
                else:
                    squares(k)
                    xt_high(turn0[k], k)
                if kind == "ffn":
                    ffn(f, k)
                    f += 1
                if kind == "pool_attn":
                    pool_attn(k, seen[kind])
                    seen[kind] += 1
                if kind == "dil_diff":
                    dil_diff(k)
                if kind == "delta_ret":
                    delta_ret(k)
            squares(norms - 1)

        @block.vector
        def _(dve):
            steps = [0]

            def link(ins):
                steps[0] += 1
                ins.then_inc(dve_step, 1)
                dve.wait_ge(dve_step, steps[0])

            def split_lo(m, s):
                if isinstance(m, int) and m == 0:
                    for q in range(4):
                        part = slice(q * 512, (q + 1) * 512)
                        dve.wait_ge(hi_done if q == 3 else first_hi, 1 if q == 3 else q + 1)
                        nc.vector.tensor_tensor(w_lo[0][:, part], w_raw[0][:, part], w_hi[0][:, part].bitcast(F32),
                                                ALU.subtract).then_inc(lo_done if q == 3 else first_lo, 1)
                    return
                dve.wait_ge(hi_done, m + 1)
                nc.vector.tensor_tensor(w_lo[s][:, :], w_raw[s][:, :], w_hi[s][:, :].bitcast(F32),
                                        ALU.subtract).then_inc(lo_done, 1)

            def mean_square(k, tt):
                dve.wait_ge(ss_done, TT * k + tt + 1)
                nc.vector.tensor_scalar(stat[:, 1, tt:tt + 1], stat[:, 0, tt:tt + 1], 1.0 / D, EPS, ALU.mult, ALU.add).then_inc(mean_ready, 1)

            def norm(k, tt):
                dve.wait_ge(rstd_ready, TT * k + tt + 1)
                rstd = stat[:, 2, tt:tt + 1]
                if k == norms - 1:
                    dve.wait_ge(params_in, params_at(len(program)) + 16)
                    nc.vector.scalar_tensor_tensor(out=xn[:, tt, :], in0=x[:, tt, :], scalar=rstd, in1=mix[:, 0:D],
                                                   op0=ALU.mult, op1=ALU.mult).then_inc(xn_ready, 1)
                else:
                    nc.vector.tensor_scalar(xn[:, tt, :], x[:, tt, :], rstd, None, ALU.mult).then_inc(xn_ready, 1)

            def xt_low(turn, norm=None, halves=range(4)):
                for j in halves:
                    tt, g = j // 2, j % 2
                    dve.wait_ge(xt_hi_done, 4 * turn + j + 1)
                    toks = slice(tt * P, (tt + 1) * P)
                    if norm is None:
                        nc.vector.tensor_tensor(xt_lo[:, 4 * g:4 * g + 4, toks], psum3(4 + j, 4),
                                                xt_hi[:, 4 * g:4 * g + 4, toks].bitcast(F32), ALU.subtract).then_inc(xt_lo_done, 1)
                        continue
                    for q in range(4):
                        c = norm * KT + 4 * g + q
                        ins = nc.vector.scalar_tensor_tensor(out=xt_lo[:, 4 * g + q, toks], in0=psum3(4 + j, 4)[:, q, :],
                                                             scalar=gain[:, c:c + 1], in1=xt_hi[:, 4 * g + q, toks].bitcast(F32),
                                                             op0=ALU.mult, op1=ALU.subtract)
                    ins.then_inc(xt_lo_done, 1)

            def ffn(f, k):
                base = first_piece[k]

                def hidden(c):
                    for tt in range(TT):
                        dve.wait_ge(gate_ready, c * TT + (TT * NCH * f + tt + 1))
                        b = bank[tt if isinstance(c, int) and c == 0 else 4 + tt]
                        nc.vector.scalar_tensor_tensor(out=hid[:, tt, :], in0=b[:, CH:2 * CH], scalar=stat[:, 2, tt:tt + 1],
                                                       in1=gate[:, tt, :], op0=ALU.mult, op1=ALU.mult).then_inc(hid_ready, 1)

                def ht_low(c):
                    dve.wait_ge(ht_hi_done, c + (NCH * f + 1))
                    nc.vector.tensor_tensor(hidden_parts(c)[1], bank[6][:, :].rearrange("p (k q) -> p k q", k=2),
                                            hidden_parts(c)[0].bitcast(F32), ALU.subtract).then_inc(ht_lo_done, 1)

                def ahead(j, c):
                    m = c * SLOTS + (base - 1 + j)
                    if not isinstance(c, int) or m < n_pieces:
                        split_lo(m, (base + 2 + j) % SLOTS)

                def step(c):
                    ht_low(c - 1)
                    ahead(2, c)
                    ahead(3, c)
                    hidden(c)
                    ahead(4, c)

                split_lo(base + 2, (base + 2) % SLOTS)
                dve.wait_ge(rstd_ready, TT * (k + 1))
                hidden(0)
                split_lo(base + 3, (base + 3) % SLOTS)
                step(1)
                with dve.Fori(2, NCH - 1) as c:
                    step(c)
                step(NCH - 1)
                ht_low(NCH - 1)

            def half_done(o, j, last_piece):
                if j < 3:
                    dve.wait_ge(out_done, 3 * o + j + 1)
                else:
                    dve.wait_ge(used, last_piece + 1)

            def add_to_x(k, o, scale, split):
                for j in range(4):
                    half_done(o, j, first_piece[k] + PIECES[program[k]] - 1)
                    xs = x[:, j // 2, (j % 2) * 512:(j % 2 + 1) * 512]
                    nc.vector.scalar_tensor_tensor(out=xs, in0=bank[j][:, :], scalar=scale, in1=xs,
                                                   op0=ALU.mult, op1=ALU.add).then_inc(x_ready, 1)
                    if j == 0 and not late[k + 1] and split < n_pieces:
                        split_lo(split, split % SLOTS)
                    if late[k + 1] and j:
                        xt_low(turn0[k + 1], k + 1, (j - 1,))
                    if not late[k + 1] and j == 2:
                        mean_square(k + 1, 0)
                if late[k + 1]:
                    if split < n_pieces:
                        split_lo(split, split % SLOTS)
                    xt_low(turn0[k + 1], k + 1, (3,))
                    for tt in range(TT):
                        mean_square(k + 1, tt)
                else:
                    norm(k + 1, 0)
                    mean_square(k + 1, 1)
                    norm(k + 1, 1)

            def ahead(m):
                if m + 2 < n_pieces:
                    split_lo(m + 2, (m + 2) % SLOTS)

            def delta_ret(k):
                n0, e0, h0 = first_piece[k], evac0[k], head_norm0[k]
                gates = G["gates"]
                per_head = lambda v: v.rearrange("p (n w) -> p n w", w=P)
                th = lambda v: v.unsqueeze(2).broadcast_to([P, 8, P])
                beta, e4, gc = gates[:, 56:64], G["e4"], G["gc"]
                eg = e4[:, 0:8]
                conv = G["conv"]
                tab = G["rope"].rearrange("p (c t d) -> p c t d", c=2, t=TT)
                ret = G["ret"].rearrange("p (h q) -> p h q", h=4)

                def convolve(i):
                    dve.wait_ge(M["ct_ready"], i + 1)
                    for j in range(3):
                        for c in range(4):
                            w = (4 * i + c) * 4 + j
                            ins = nc.vector.scalar_tensor_tensor(out=co[i % 2][:, c, :], in0=ct[i % 2][:, c, j:j + SEQ],
                                                                 scalar=conv[:, w:w + 1], in1=co[i % 2][:, c, :],
                                                                 op0=ALU.mult, op1=ALU.add)
                        if j < 2:
                            link(ins)
                    ins.then_inc(M["conv_ready"], 1)

                def scaled(out, x, by, ready):
                    nc.vector.tensor_tensor(per_head(out), per_head(x), th(by), ALU.mult).then_inc(M[ready], 1)

                def update(l):
                    for tt in range(TT):
                        dve.wait_ge(M["y_done"], TT * (l - 1) + tt + 1)
                        if l < 5:
                            a = inv[:, tt].rearrange("p h q -> p (h q)")
                            nc.vector.tensor_tensor(a, a, bank[6 + tt][:, :], ALU.subtract)
                        a = inv_t[:, tt].rearrange("p h q -> p (h q)")
                        nc.vector.tensor_tensor(a, a, bank[4 + tt][:, :], ALU.subtract).then_inc(M["x_updated"], 1)

                def decay_scores(h):
                    dve.wait_ge(M["rs_done"], h + 1)
                    pr = retention_probs(h)
                    nc.vector.scalar_tensor_tensor(out=pr[:, 0:SEQ], in0=bank[6 + h % 2][:, 0:SEQ], scalar=0.125,
                                                   in1=ret[:, h, :], op0=ALU.mult, op1=ALU.mult)
                    nc.vector.scalar_tensor_tensor(out=pr[:, SEQ:384], in0=bank[6 + h % 2][:, SEQ:384], scalar=0.125,
                                                   in1=ret[:, h, 0:P], op0=ALU.mult, op1=ALU.mult).then_inc(M["rs_ready"], 1)

                def new_values(n):
                    tt, rows = n // 2, slice(64 * (n % 2), 64 * (n % 2) + 64)
                    dve.wait_ge(M["vw_done"], n)
                    nc.vector.tensor_tensor(v_new[rows].rearrange("p h e -> p (h e)"), tok(G["q_qd_u"])[rows, tt, :],
                                            bank[4][rows, :], ALU.subtract).then_inc(M["vn_ready"], 1)

                def next_state(n):
                    dve.wait_ge(M["ds_done"], n + 1)
                    if n == 0:
                        nc.vector.tensor_copy(state.rearrange("p h e -> p (h e)"), bank[5][:, :]).then_inc(M["s_ready"], 1)
                        return
                    el = e4[:, 16 + 8 * (n % 2) + 4 * (n // 2):]
                    for h in range(4):
                        ins = nc.vector.scalar_tensor_tensor(out=state[:, h, :], in0=state[:, h, :], scalar=el[:, h:h + 1],
                                                             in1=psum3(5, 4)[:, h, :], op0=ALU.mult, op1=ALU.add)
                    ins.then_inc(M["s_ready"], 1)

                def output_mean(tt):
                    dve.wait_ge(hsq_done, h0 + 4 + tt)
                    cols = slice(4 * tt, 4 * tt + 4)
                    nc.vector.tensor_scalar(hstat[:, 1, cols], hstat[:, 0, cols], 1.0 / P, EPS, ALU.mult, ALU.add).then_inc(hmean_ready, 1)

                def norm_output(tt):
                    dve.wait_ge(hrstd_ready, h0 + 4 + tt)
                    if tt == 0:
                        dve.wait_ge(M["gz_ready"], 1)
                    for h in range(4):
                        at = slice((4 * tt + h) * P, (4 * tt + h + 1) * P)
                        ins = nc.vector.scalar_tensor_tensor(out=G["decay_oa"][:, at], in0=psum3(6 + tt, 4)[:, h, :],
                                                             scalar=hstat[:, 2, 4 * tt + h:4 * tt + h + 1],
                                                             in1=G["gz"][:, at], op0=ALU.mult, op1=ALU.mult)
                    ins.then_inc(M["half_normed"], 1)

                dve.wait_ge(M["ba_hi"], 1)
                nc.vector.tensor_tensor(ba_lo[:, :], G["ba"], ba_hi[:, :].bitcast(F32), ALU.subtract).then_inc(M["ba_split"], 1)
                dve.wait_ge(M["ba_t_done"], 1)
                nc.vector.tensor_copy(G["kt_rt"][0:8, 0:SEQ], bank[4][0:8, 0:SEQ]).then_inc(M["ba_t_copied"], 1)
                last = PIECES["delta_ret"] - 1
                for p in range(PIECES["delta_ret"]):
                    if p == 4:
                        convolve(1)
                    if p == 6:
                        convolve(2)
                        head_mean(h0 + 1, G["rg"], 8, P, float(P), P * EPS)
                    if p not in (13, 14, last):
                        ahead(n0 + p)
                    if p == 0:
                        dve.wait_ge(M["ba_done"], 1)
                        ba = bank[5][:, 256:272].rearrange("p (t c) -> p t c", t=TT)
                        g2 = lambda a: gates[:, a:a + 8].rearrange("p (t h) -> p t h", t=TT)
                        dt = G["alog_dt"][:, 4:8].unsqueeze(1).broadcast_to([P, TT, 4])
                        nc.vector.tensor_copy(g2(40), ba[:, :, 0:4])
                        link(nc.vector.tensor_tensor(g2(0), ba[:, :, 4:8], dt, ALU.add))
                        link(nc.vector.tensor_scalar(gates[:, 8:16], gates[:, 0:8], -1.0, None, ALU.mult))
                        nc.vector.tensor_tensor(gates[:, 16:24], gates[:, 0:8], gates[:, 8:16], ALU.max).then_inc(M["abs_ready"], 1)
                        dve.wait_ge(M["softplus_ready"], 1)
                        link(nc.vector.scalar_tensor_tensor(out=gates[:, 8:16], in0=gates[:, 0:8], scalar=0.0,
                                                            in1=gates[:, 24:32], op0=ALU.max, op1=ALU.add))
                        ea = gates[:, 32:36].unsqueeze(1).broadcast_to([P, TT, 4])
                        link(nc.vector.scalar_tensor_tensor(out=g2(0), in0=g2(8), scalar=-1.0, in1=ea, op0=ALU.mult, op1=ALU.mult))
                        link(nc.vector.tensor_scalar(gates[:, 48:56], gates[:, 48:56], 1.0, None, ALU.add))
                        nc.vector.reciprocal(beta, gates[:, 48:56]).then_inc(M["g_ready"], 1)
                        nc.vector.tensor_tensor(per_head(G["decay_oa"]), G["before"].unsqueeze(1).broadcast_to([P, 8, P]),
                                                th(gates[:, 0:8]), ALU.mult).then_inc(M["ug_ready"], 1)
                    if p == 1:
                        dve.wait_ge(M["sums_done"], 1)
                        nc.vector.tensor_copy(gc, bank[5][:, 0:8]).then_inc(M["gcum_copied"], 1)
                    if p == 2:
                        dve.wait_ge(M["diff_done"], 1)
                        dve.wait_ge(M["gcum_copied"], 1)
                        for i in range(8):
                            ins = nc.vector.scalar_tensor_tensor(out=per_head(G["decay_oa"])[:, i, :], in0=psum3(6 + i // 4, 4)[:, i % 4, :],
                                                                 scalar=gc[:, i:i + 1], in1=G["below"], op0=ALU.subtract, op1=ALU.add)
                        ins.then_inc(M["diff_ready"], 1)
                        convolve(0)
                    if p == 4:
                        head_norm(h0, G["rg"], 8, P, 1.0, EPS, per_head(G["k_kd"]))
                        scaled(G["kb_kbe"], G["k_kd"], beta, "kb_ready")
                    if p == 6:
                        head_scale(h0 + 1, 8, P, per_head(G["q_qd_u"]))
                        nc.vector.tensor_copy(hstat[:, 0, 0:1], hstat[:, 1, 0:1]).then_inc(M["normed"], 1)
                    if p == 7:
                        dve.wait_ge(M["qt_turned"], 1)
                        dve.wait_ge(M["e4_ready"], 1)
                        scaled(G["q_qd_u"], G["q_qd_u"], eg, "qd_ready")
                        dve.wait_ge(M["at_done"], 1)
                        dve.wait_ge(M["decay_ready"], 1)
                        for tt in range(TT):
                            ins = nc.vector.tensor_tensor(at_m[:, tt].rearrange("p h q -> p (h q)"), bank[6 + tt][:, :],
                                                          G["decay_oa"][:, tt * 512:(tt + 1) * 512], ALU.mult)
                        ins.then_inc(M["at_ready"], 1)
                        dve.wait_ge(M["at_ready"], 1)
                        flat = lambda v: v.rearrange("p t h q -> p (t h) q")
                        each = lambda v: v.unsqueeze(1).broadcast_to([P, 8, P])
                        dve.wait_ge(M["conv_ready"], 3)
                        dve.wait_ge(M["co_turned"], 3)
                        link(nc.vector.tensor_tensor(flat(inv_t), flat(at_m), each(G["level"][:, 0:P]), ALU.mult))
                        nc.vector.tensor_tensor(flat(inv_t), each(ident[:, :]), flat(inv_t), ALU.subtract).then_inc(M["xt0_ready"], 1)
                    if p == 8:
                        dve.wait_ge(M["qk_done"], 1)
                        for tt in range(TT):
                            ins = nc.vector.tensor_tensor(qk_m[:, tt].rearrange("p h q -> p (h q)"), bank[4 + tt][:, :],
                                                          G["decay_oa"][:, tt * 512:(tt + 1) * 512], ALU.mult)
                        ins.then_inc(M["qk_masked"], 1)
                    if p == 8:
                        dve.wait_ge(act_evac, e0 + 2)
                        rope(heads(G["rqk_ob"]), heads(G["rg"]), tab[:, 0], tab[:, 1], 64).then_inc(qk_ready, 1)
                    if p == 10:
                        update(1)
                        decay_scores(0)
                        decay_scores(1)
                    if p == 11:
                        update(2)
                        decay_scores(2)
                        decay_scores(3)
                    if p == 12:
                        update(3)
                    if p == 13:
                        head_mean(h0 + 2, G["rv"], 8, P, 1.0 / P, EPS)
                        update(4)
                        head_scale(h0 + 2, 8, P, per_head(G["rqk_ob"]))
                        dve.wait_ge(act_evac, e0 + 6)
                        nc.vector.tensor_tensor(G["rqk_ob"], G["rqk_ob"], G["rg"], ALU.mult).then_inc(M["half_normed"], 1)
                        update(5)
                        pair_low(bt0[k], 2, first_half)
                        pair_low(bt0[k] + 1, 3, second_half)
                        ahead(n0 + 13)
                    if p == 14:
                        next_state(0)
                        for n in range(1, 4):
                            new_values(n)
                            if n == 2:
                                output_mean(0)
                            if n < 3:
                                next_state(n)
                        ahead(n0 + 14)
                        norm_output(0)
                        output_mean(1)
                        norm_output(1)
                        pair_low(bt0[k] + 2, 4, beside)
                        pair_low(bt0[k] + 3, 5, first_half)
                add_to_x(k, out0[k], 1.0, n0 + last + 2)

            def dil_diff(k):
                n0, e0, g0, rp = first_piece[k], evac0[k], map0[k], rope0[k]
                tab = B["rope"].rearrange("p (c t d) -> p c t d", c=2, t=TT)
                tab_wide = B["rope_wide"].rearrange("p (c t d) -> p c t d", c=2, t=TT)
                lam = B["lam"]
                d4 = heads(B["diff"], P)
                x4 = xn[:, :, 0:512].rearrange("p t (r n w) -> p t r n w", r=2, n=2)

                def rotate(name, j, tables, w):
                    dve.wait_ge(act_evac, e0 + 2 * j + 2)
                    rope(heads(B[name], w), heads(B["rot"], w), tables[:, 0], tables[:, 1], w).then_inc(qk_ready, 1)

                def take_pair(h):
                    dve.wait_ge(pv_done, g0 + 2 * h + 2)
                    i = 2 * h
                    link(nc.vector.reciprocal(expsum[:, 1, :, i:i + 2], expsum[:, 0, :, i:i + 2]))
                    second = expsum[:, 1, :, i + 1]
                    link(nc.vector.tensor_scalar(second, second, lam[:, 5:6], None, ALU.mult))
                    for tt in range(TT):
                        prod = B["prod"][:, tt * P:(tt + 1) * P]
                        link(nc.vector.tensor_scalar(prod, bank[7][:, tt * 256 + P:tt * 256 + 256],
                                                     expsum[:, 1, tt, i + 1:i + 2], None, ALU.mult))
                        ins = nc.vector.scalar_tensor_tensor(out=d4[:, tt, h], in0=bank[7][:, tt * 256:tt * 256 + P],
                                                             scalar=expsum[:, 1, tt, i:i + 1], in1=prod, op0=ALU.mult, op1=ALU.add)
                    ins.then_inc(o_ready, 1)

                dve.wait_ge(params_in, params_at(k))
                pairs = B["lambdas"].rearrange("p (m w d) -> p m w d", m=2, w=2)
                prods = B["prod"][:, 0:128].rearrange("p (m d) -> p m d", m=2)
                link(nc.vector.tensor_tensor(prods, pairs[:, :, 0], pairs[:, :, 1], ALU.mult))
                nc.vector.tensor_reduce(lam[:, 0:2], prods, AX_X, ALU.add).then_inc(lam_sums, 1)
                link(nc.vector.tensor_scalar(B["diff_norm"], B["diff_norm"], 1.0 - LAMBDA_INIT, None, ALU.mult))
                dve.wait_ge(lam_exp, 1)
                link(nc.vector.tensor_tensor(lam[:, 4:5], lam[:, 3:4], lam[:, 2:3], ALU.subtract))
                link(nc.vector.tensor_scalar(lam[:, 5:6], lam[:, 4:5], -LAMBDA_INIT, None, ALU.add))
                def head_mean_square(h):
                    dve.wait_ge(hsq_done, head_norm0[k] + h + 1)
                    nc.vector.tensor_scalar(hstat[:, 1, 2 * h:2 * h + 2], hstat[:, 0, 2 * h:2 * h + 2], 1.0 / P, EPS,
                                            ALU.mult, ALU.add).then_inc(hmean_ready, 1)

                def norm_head(h):
                    dve.wait_ge(hrstd_ready, head_norm0[k] + h + 1)
                    for tt in range(TT):
                        ins = nc.vector.scalar_tensor_tensor(out=xn[:, tt, 512 + h * P:512 + (h + 1) * P], in0=d4[:, tt, h],
                                                             scalar=hstat[:, 2, 2 * h + tt:2 * h + tt + 1], in1=B["diff_norm"],
                                                             op0=ALU.mult, op1=ALU.mult)
                    ins.then_inc(diff_normed, 1)

                last = PIECES["dil_diff"] - 1
                for p in range(last + 1):
                    if p == 13:
                        take_round(g0 + 9, 0, 2, x4[:, :, 0])
                    if p == 14:
                        pair_low(bt0[k] + 3, 5, first_half)
                    if p != last:
                        ahead(n0 + p)
                    if p == 1:
                        rotate("dq", 0, tab, 64)
                    if p == 3:
                        dve.wait_ge(qk_ready, rp + 1)
                        rotate("dk", 1, tab, 64)
                    if p == 10:
                        rotate("ck", 4, tab_wide, P)
                    for step in steps_of(p, 6, 1):
                        if step < 8:
                            soft(g0 + step, 0.125, B["mask"])
                        if step in (4, 6, 8, 10):
                            take_pair((step - 4) // 2)
                        if step in (6, 8, 10):
                            head_mean_square((step - 6) // 2)
                        if step == 9:
                            norm_head(0)
                            norm_head(1)
                    if p == 10:
                        head_mean_square(3)
                        norm_head(2)
                        norm_head(3)
                    if p == 11:
                        pair_low(bt0[k], 6, first_half)
                        pair_low(bt0[k] + 1, 7, second_half)
                        soft(g0 + 8, DIL_SCALE, B["mask_dil"])
                        soft(g0 + 9, DIL_SCALE, B["mask_dil"])
                    if p == 12:
                        soft(g0 + 10, DIL_SCALE, B["mask_dil"])
                        soft(g0 + 11, DIL_SCALE, B["mask_dil"])
                    if p == 13:
                        pair_low(bt0[k] + 2, 4, beside)
                        take_round(g0 + 11, 2, 2, x4[:, :, 1])
                add_to_x(k, out0[k], 1.0, n0 + last + 2)

            def rope_gains(k):
                dve.wait_ge(params_in, params_at(k))
                tab = A["rope"].rearrange("p (c t d) -> p c t d", c=2, t=TT)
                out = A["rope_g"].rearrange("p (w c t d) -> p w c t d", w=2, c=2, t=TT)
                for w in range(2):
                    g = A["qk_norm"][:, 64 * w:64 * w + 64]
                    b = lambda lo, hi: g[:, lo:hi].unsqueeze(1).broadcast_to([P, TT, hi - lo])
                    nc.vector.tensor_tensor(out[:, w, 0], tab[:, 0], b(0, 64), ALU.mult)
                    nc.vector.tensor_tensor(out[:, w, 1, :, 0:32], tab[:, 1, :, 0:32], b(32, 64), ALU.mult)
                    link(nc.vector.tensor_tensor(out[:, w, 1, :, 32:64], tab[:, 1, :, 32:64], b(0, 32), ALU.mult))

            def head_norm(c, sq, n, w, scale, eps, x3):
                head_mean(c, sq, n, w, scale, eps)
                head_scale(c, n, w, x3)

            def head_mean(c, sq, n, w, scale, eps):
                dve.wait_ge(hsq_done, c + 1)
                link(nc.vector.tensor_reduce(hstat[:, 0, 0:n], sq.rearrange("p (n w) -> p n w", w=w), AX_X, ALU.add))
                nc.vector.tensor_scalar(hstat[:, 1, 0:n], hstat[:, 0, 0:n], scale, eps, ALU.mult, ALU.add).then_inc(hmean_ready, 1)

            def head_scale(c, n, w, x3):
                dve.wait_ge(hrstd_ready, c + 1)
                link(nc.vector.tensor_tensor(x3, x3, hstat[:, 2, 0:n].unsqueeze(2).broadcast_to([P, n, w]), ALU.mult))

            def rope(x, rot, cos, sin, w):
                h, n = w // 2, x.shape[2]
                b = lambda v: v.unsqueeze(2).broadcast_to([P, TT, n, v.shape[2]])
                nc.vector.tensor_tensor(rot[:, :, :, 0:h], x[:, :, :, h:w], b(sin[:, :, 0:h]), ALU.mult)
                link(nc.vector.tensor_tensor(rot[:, :, :, h:w], x[:, :, :, 0:h], b(sin[:, :, h:w]), ALU.mult))
                link(nc.vector.tensor_tensor(x, x, b(cos), ALU.mult))
                return nc.vector.tensor_tensor(x, x, rot, ALU.add)

            def soft(g, scale, mask):
                pr = A["probs"][:, (g % 2) * 384:(g % 2) * 384 + 384]
                dve.wait_ge(s_done, g + 1)
                if g >= 2:
                    dve.wait_ge(pt_done, g - 1)
                nc.vector.scalar_tensor_tensor(out=pr, in0=bank[4 + g % 2][:, 0:384], scalar=scale, in1=mask,
                                               op0=ALU.mult, op1=ALU.add).then_inc(s_masked, 1)
                dve.wait_ge(s_masked, g + 1)
                nc.vector.tensor_reduce(negmax[:, g % 2, 0:1], pr[:, 0:P], AX_X, ALU.max, negate=True)
                nc.vector.tensor_reduce(negmax[:, g % 2, 1:2], pr[:, P:3 * P], AX_X, ALU.max, negate=True).then_inc(max_ready, 1)

            def take_round(last_map, i0, n, out):
                dve.wait_ge(pv_done, last_map + 1)
                link(nc.vector.reciprocal(expsum[:, 1, :, i0:i0 + n], expsum[:, 0, :, i0:i0 + n]))
                w = 512 // (TT * n)
                nc.vector.tensor_tensor(out, bank[7][:, :].rearrange("p (t n w) -> p t n w", t=TT, n=n),
                                        expsum[:, 1, :, i0:i0 + n].unsqueeze(3).broadcast_to([P, TT, n, w]),
                                        ALU.mult).then_inc(o_ready, 1)

            def pair_low(c, src, dst):
                dve.wait_ge(bt_hi_done, c + 1)
                nc.vector.tensor_tensor(dst[1], psum3(src, 2), dst[0].bitcast(F32), ALU.subtract).then_inc(bt_lo_done, 1)

            def bt_low(c, src, scale=None):
                dve.wait_ge(bt_hi_done, c + 1)
                for b in range(2):
                    for r in range(2):
                        q, hi = 2 * b + r, bt_hi[:, 2 * b + r, :].bitcast(F32)
                        if scale is None:
                            ins = nc.vector.tensor_tensor(bt_lo[:, q, :], psum3(src + b, 2)[:, r, :], hi, ALU.subtract)
                        else:
                            ins = nc.vector.scalar_tensor_tensor(out=bt_lo[:, q, :], in0=psum3(src + b, 2)[:, r, :],
                                                                 scalar=scale[:, q:q + 1], in1=hi, op0=ALU.mult, op1=ALU.subtract)
                ins.then_inc(bt_lo_done, 1)

            def pool_attn(k, i):
                n0, g0, c0, o0 = first_piece[k], map0[k], head_norm0[k], out0[k]
                rg = A["rope_g"].rearrange("p (w c t d) -> p w c t d", w=2, c=2, t=TT)
                gates = tok(A["gates"])
                o4 = A["u"].rearrange("p (t r n w) -> p t r n w", t=TT, r=2, n=4)

                def mean_of(which):
                    head_mean(c0 + which, A["sq"], 16, 64, 1.0 / 64, EPS)

                def rotate(which, name):
                    head_scale(c0 + which, 16, 64, A[name].rearrange("p (n w) -> p n w", w=64))
                    rope(heads(A[name]), heads(A["rot"]), rg[:, which, 0], rg[:, which, 1], 64).then_inc(qk_ready, 1)

                last = PIECES["pool_attn"] - 1
                for p in range(last + 1):
                    if p not in (19, last):
                        ahead(n0 + p)
                    if p == 0:
                        rope_gains(k)
                        dve.wait_ge(rstd_ready, TT * (k + 1))
                    if p == 3:
                        mean_of(0)
                    if p == 4:
                        rotate(0, "q")
                    if p == 5:
                        mean_of(1)
                    if p == 6:
                        bt_low(bt0[k], 6, A["pool_scale"])
                        rotate(1, "k")
                    for step in steps_of(p, 9, 0):
                        if step < 8:
                            soft(g0 + step, 0.125, A["mask"])
                        if step == 6:
                            take_round(g0 + 3, 0, 4, o4[:, :, 0])
                    if p == 14:
                        take_round(g0 + 7, 4, 4, o4[:, :, 1])
                    if p == 15:
                        pair_low(bt0[k] + 1, 4, beside)
                    if p == 16:
                        pair_low(bt0[k] + 2, 5, first_half)
                    if p in (9, 11, 13, 15):
                        j = (p - 1) // 2
                        for tt in range(TT):
                            if tt == 0:
                                dve.wait_ge(proj_done, chunk0[k] + j + 1)
                            else:
                                dve.wait_ge(used, n0 + 2 * j + 2)
                            gs = gates[:, tt, (j - 4) * 512:(j - 3) * 512]
                            nc.vector.scalar_tensor_tensor(out=gs, in0=bank[2 * (j % 2) + tt][:, :], scalar=stat[:, 2, tt:tt + 1],
                                                           in1=gs, op0=ALU.mult, op1=ALU.add).then_inc(gate_added, 1)
                    if p == 17:
                        dve.wait_ge(gates_ready, 2 * i + 1)
                        for j in range(4):
                            tt, cols = j // 2, slice((j % 2) * 512, (j % 2 + 1) * 512)
                            half_done(o0, j, n0 + 17)
                            nc.vector.tensor_tensor(xn[:, tt, cols], bank[j][:, :], gates[:, tt, cols], ALU.mult).then_inc(branch_ready, 1)
                    if p == 19:
                        dve.wait_ge(gates_ready, 2 * i + 2)
                        for j in range(4):
                            tt, cols = j // 2, slice((j % 2) * 512, (j % 2 + 1) * 512)
                            half_done(o0 + 1, j, n0 + 19)
                            g1 = gates[:, tt, D + (j % 2) * 512:D + (j % 2 + 1) * 512]
                            link(nc.vector.tensor_tensor(g1, bank[j][:, :], g1, ALU.mult))
                            nc.vector.tensor_tensor(xn[:, tt, cols], xn[:, tt, cols], g1, ALU.add).then_inc(merged_ready, 1)
                            if j:
                                xt_low(turn0[k] + 1, None, (j - 1,))
                        xt_low(turn0[k] + 1, None, (3,))
                        ahead(n0 + p)
                add_to_x(k, o0 + 2, 1.0, n0 + last + 2)

            seen = {"pool_attn": 0}
            f = 0
            for k, kind in enumerate(program):
                if k == 0:
                    dve.wait_ge(gain_in, 16)
                    xt_low(0, 0, (0, 1))
                    split_lo(0, 0)
                    xt_low(0, 0, (2, 3))
                    split_lo(1, 1)
                    for tt in range(TT):
                        mean_square(0, tt)
                elif not late[k]:
                    xt_low(turn0[k], k)
                if kind == "ffn":
                    ffn(f, k)
                    f += 1
                    add_to_x(k, out0[k], 0.5, first_piece[k] + 34)
                if kind == "pool_attn":
                    pool_attn(k, seen[kind])
                    seen[kind] += 1
                if kind == "dil_diff":
                    dil_diff(k)
                if kind == "delta_ret":
                    delta_ret(k)

        @block.tensor
        def _(pe):
            def three(out, a_hi, a_lo, b_hi, b_lo, start, stop):
                nc.tensor.matmul(out, a_hi, b_hi, start=start, stop=False)
                nc.tensor.matmul(out, a_hi, b_lo, start=False, stop=False)
                return nc.tensor.matmul(out, a_lo, b_hi, start=False, stop=stop)

            def turn(src, j):
                tt, g = j // 2, j % 2
                for q in range(4):
                    c = (4 * g + q) * P
                    ins = nc.tensor.transpose(bank[4 + j][:, q * P:(q + 1) * P], src[:, tt, c:c + P], ident[:, :])
                ins.then_inc(xt_done, 1)

            def turn_x(k, halves):
                for j in halves:
                    if not late[k]:
                        pe.wait_ge(xn_ready, TT * normed0[k] + j // 2 + 1)
                    elif k:
                        pe.wait_ge(x_ready, 4 * (k - 1) + j + 1)
                    else:
                        pe.wait_ge(x_in[min(j, 2)], 16)
                    turn(x if late[k] else xn, j)

            def turn_early(k, j):
                if late[k] and j in (1, 2):
                    turn_x(k, (j - 1,))

            def turn_first(k):
                if k == 0:
                    turn_x(k, (0, 1))
                else:
                    turn_x(k, (2,) if late[k] else range(4))

            def turn_rest(k):
                if k == 0:
                    turn_x(k, (2, 3))
                elif late[k]:
                    turn_x(k, (3,))

            def ffn(f, k, n0):
                base = n0

                def up(c, hook=None):
                    for half in range(2):
                        s = (base + half + (0 if isinstance(c, int) and c == 0 else 2)) % SLOTS
                        m = (base + half) if isinstance(c, int) and c == 0 else c * SLOTS + (base + 2 - SLOTS + half)
                        opening = isinstance(c, int) and c == 0
                        if not isinstance(m, int) or m:
                            pe.wait_ge(lo_done, m + 1)
                        for tt in range(TT):
                            if half == 0 and not (isinstance(c, int) and c <= 1):
                                pe.wait_ge(hid_ready, c * TT + (TT * NCH * f + tt + 1 - TT))
                            if isinstance(c, int) and c == 0:
                                pe.wait_ge(xt_lo_done, 4 * turn0[k] + 2 * tt + half + 1)
                            for q in range(4):
                                if isinstance(m, int) and m == 0 and tt == 0:
                                    pe.wait_ge(lo_done if q == 3 else first_lo, 1 if q == 3 else q + 1)
                                kt = 4 * half + q
                                a = slice(tt * P, (tt + 1) * P)
                                ins = three(bank[tt if opening else 4 + tt][:, :], xt_hi[:, kt, a], xt_lo[:, kt, a],
                                            up_view(w_hi[s], q), up_view(w_lo[s], q), kt == 0, kt == KT - 1)
                                if opening and half == 0 and tt == 0 and q == (3 if k else 1):
                                    turn_rest(k)
                            if half == 1 and tt == 0:
                                ins.then_inc(up_done, 1)
                            if tt == 1:
                                ins.then_inc(used, 1)
                        if half == 0 and hook:
                            hook()

                def down(c, m, s, hook=None):
                    pe.wait_ge(lo_done, m + 1)
                    pe.wait_ge(ht_lo_done, c + (NCH * f + 1))
                    first = isinstance(c, int) and c == 0
                    final = isinstance(c, int) and c == NCH - 1
                    for tt in range(TT):
                        a = slice(tt * P, (tt + 1) * P)
                        for h in range(2):
                            for q in range(2):
                                ins = three(bank[2 * tt + h][:, :], hidden_parts(c)[0][:, q, a], hidden_parts(c)[1][:, q, a],
                                            down_view(w_hi[s], q, h), down_view(w_lo[s], q, h),
                                            first and q == 0, final and q == 1)
                            j = 2 * tt + h
                            if final and j < 3:
                                ins.then_inc(out_done, 1)
                            if j == 3:
                                ins.then_inc(used, 1)
                            if final:
                                turn_early(k + 1, j)
                        if tt == 0 and hook:
                            hook()

                def turn_hidden(c):
                    pe.wait_ge(hid_ready, c * TT + (TT * NCH * f + TT))
                    for q in range(2):
                        for tt in range(TT):
                            ins = nc.tensor.transpose(bank[6][:, q * SEQ + tt * P:q * SEQ + (tt + 1) * P],
                                                      hid[:, tt, q * P:(q + 1) * P], ident[:, :])
                    ins.then_inc(ht_done, 1)

                def step(c):
                    up(c)
                    down(c - 1, c * SLOTS + (base + 1), (base + 4) % SLOTS)
                    turn_hidden(c)

                last = NCH - 1
                up(0)
                up(1, lambda: turn_hidden(0))
                down(0, base + 4, (base + 4) % SLOTS)
                turn_hidden(1)
                with pe.Fori(2, last) as c:
                    step(c)
                up(last)
                down(last - 1, base + 3 * last + 1, (base + 3 * last + 1) % SLOTS, lambda: turn_hidden(last))
                down(last, base + 3 * last + 2, (base + 3 * last + 2) % SLOTS)

            def chunk_piece(k, n, j, half, hook=None):
                s = n % SLOTS
                pe.wait_ge(lo_done, n + 1)
                for tt in range(TT):
                    if j == 0:
                        pe.wait_ge(xt_lo_done, 4 * turn0[k] + 2 * tt + half + 1)
                    a = slice(tt * P, (tt + 1) * P)
                    for q in range(4):
                        kt = 4 * half + q
                        ins = three(bank[2 * (j % 2) + tt][:, :], xt_hi[:, kt, a], xt_lo[:, kt, a],
                                    up_view(w_hi[s], q), up_view(w_lo[s], q), kt == 0, kt == KT - 1)
                    if half == 1 and tt == 0:
                        ins.then_inc(proj_done, 1)
                    if tt == TT - 1:
                        ins.then_inc(used, 1)
                    if j == 0 and half == 0 and tt == 0:
                        turn_rest(k)
                    if hook:
                        hook(tt)

            def product(n, pieces, operand, before=None, ready=None, after=None, between=None):
                for i in range(pieces):
                    s = (n + i) % SLOTS
                    pe.wait_ge(lo_done, n + i + 1)
                    for tt in range(TT):
                        if i == 0 and before:
                            before(tt)
                        if ready:
                            ready(i, tt)
                        a = slice(tt * P, (tt + 1) * P)
                        for h in range(2):
                            for q in range(2):
                                hi, lo = operand(i, q)
                                ins = three(bank[2 * tt + h][:, :], hi[:, a], lo[:, a],
                                            down_view(w_hi[s], q, h), down_view(w_lo[s], q, h),
                                            i == 0 and q == 0, i == pieces - 1 and q == 1)
                            j = 2 * tt + h
                            if j == 3:
                                ins.then_inc(used, 1)
                            elif i == pieces - 1:
                                ins.then_inc(out_done, 1)
                            if between:
                                between(i, tt, h)
                    if after:
                        after(i)

            def in_heads(i, q):
                hi, lo = (first_half, second_half, beside, first_half)[i]
                return hi[:, q], lo[:, q]

            def heads_ready(k, i, tt):
                if tt == 0:
                    pe.wait_ge(bt_lo_done, bt0[k] + 1 + i)

            def in_bt(i, q):
                return bt_hi[:, 2 * (i % 2) + q, :], bt_lo[:, 2 * (i % 2) + q, :]

            def in_xt(i, q):
                return xt_hi[:, 2 * i + q, :], xt_lo[:, 2 * i + q, :]

            def turn_heads(src, b0):
                for c in range(4):
                    for tt in range(TT):
                        at = (c % 2) * SEQ + tt * P
                        ins = nc.tensor.transpose(bank[b0 + c // 2][:, at:at + P], src[:, tt, c * P:(c + 1) * P], ident[:, :])
                return ins

            def turn_pair(src, c0, b):
                for c in range(2):
                    for tt in range(TT):
                        at = c * SEQ + tt * P
                        ins = nc.tensor.transpose(bank[b][:, at:at + P], src[:, tt, (c0 + c) * P:(c0 + c + 1) * P], ident[:, :])
                ins.then_inc(ot_done, 1)

            def scores(g, operands):
                if g >= 2:
                    pe.wait_ge(s_masked, g - 1)
                for (lhs, rhs), (lo, hi) in zip(operands, ((0, P), (P, 3 * P))):
                    ins = nc.tensor.matmul(bank[4 + g % 2][:, lo:hi], lhs, rhs, start=True, stop=True)
                ins.then_inc(s_done, 1)

            def turn_probs(g):
                pe.wait_ge(exp_done, g + 1)
                if g >= 1:
                    pe.wait_ge(pt_ready, g)
                for c in range(3):
                    ins = nc.tensor.transpose(bank[6][:, c * P:(c + 1) * P],
                                              A["probs"][:, (g % 2) * 384 + c * P:(g % 2) * 384 + (c + 1) * P], ident[:, :])
                ins.then_inc(pt_done, 1)

            def values(g, j, n, vs, rounds_before):
                pe.wait_ge(pt_ready, g + 1)
                if j == 0 and rounds_before:
                    pe.wait_ge(o_ready, rounds_before)
                w = 512 // (TT * n)
                pt = A["probs_t"][:, (g % 2) * 384:(g % 2) * 384 + 384]
                nc.tensor.matmul(bank[7][:, j * w:(j + 1) * w], pt[:, 0:P], vs[0], start=True, stop=True)
                out = bank[7][:, 256 + j * w:256 + (j + 1) * w]
                nc.tensor.matmul(out, pt[:, P:2 * P], vs[0], start=True, stop=False)
                nc.tensor.matmul(out, pt[:, 2 * P:3 * P], vs[1], start=False, stop=True).then_inc(pv_done, 1)

            def pool_attn(k, i):
                n0, e0, g0, r0 = first_piece[k], evac0[k], map0[k], round0[k]
                u, v = tok(A["u"]), tok(A["v"])
                means = A["pool_mean"].rearrange("p (g q) -> p g q", g=4)
                mapped = lambda name: A[name].rearrange("p (c q) -> p c q", c=4)
                qt, kt, pw = mapped("qt"), mapped("kt"), A["pool_w"].rearrange("p (g d) -> p g d", g=4)

                def attend(h, what):
                    c, off = h // 2, 64 * (h % 2)
                    if what == "scores":
                        scores(g0 + h, causal_map(qt[:, c], kt[:, c], off, 64))
                    elif what == "turn":
                        turn_probs(g0 + h)
                    else:
                        values(g0 + h, h % 4, 4, [v[:, tt, h * 64:(h + 1) * 64] for tt in range(TT)], r0 + h // 4)

                def attention_step(p, tt):
                    step = 2 * (p - 9) + tt
                    if step < 0:
                        return
                    if step == 0:
                        pe.wait_ge(qkt_ready, 2 * i + 2)
                    if 2 <= step < 10:
                        attend(step - 2, "turn")
                    if step < 8:
                        attend(step, "scores")
                    if 3 <= step < 11:
                        attend(step - 3, "values")
                    if step == 12:
                        pe.wait_ge(o_ready, r0 + 2)
                        turn_heads(tok(A["u"]), 4).then_inc(ot_done, 1)

                for p in range(16):
                    j = p // 2
                    if p % 2 == 0 and j >= 2:
                        if j < 6:
                            pe.wait_ge(act_evac, e0 + 2 * (j - 2) + 2)
                        else:
                            pe.wait_ge(gate_added, 8 * i + 2 * (j - 6) + 2)
                    chunk_piece(k, n0 + p, j, p % 2, lambda tt, p=p: attention_step(p, tt))
                    if p == 3:
                        pe.wait_ge(params_in, params_at(k))
                        pe.wait_ge(act_evac, e0 + 2)
                        for g in range(4):
                            at = (g % 2) * SEQ
                            us = [u[:, tt, g * P:(g + 1) * P] for tt in range(TT)]
                            nc.tensor.matmul(bank[4 + g // 2][:, at:at + SEQ], us[0], means[:, g, 0:SEQ], start=True, stop=False)
                            ins = nc.tensor.matmul(bank[4 + g // 2][:, at + P:at + SEQ], us[1], means[:, g, SEQ:3 * P], start=False, stop=True)
                        ins.then_inc(diff_done, 1)
                    if p == 5:
                        pe.wait_ge(diff_ready, i + 1)
                        for g in range(4):
                            at = (g % 2) * SEQ
                            ins = nc.tensor.matmul(bank[6 + g // 2][:, at:at + SEQ], pw[:, g, :], qt[:, g, :], start=True, stop=True)
                        ins.then_inc(y_done, 1)
                    if p == 7:
                        pe.wait_ge(qk_ready, 2 * i + 1)
                        turn_heads(tok(A["q"]), 4).then_inc(qkt_done, 1)
                    if p == 8:
                        pe.wait_ge(bt_lo_done, bt0[k] + 1)
                        pe.wait_ge(qk_ready, 2 * i + 2)
                        turn_heads(tok(A["k"]), 6).then_inc(qkt_done, 1)

                def turn_merged(halves):
                    for j in halves:
                        pe.wait_ge(merged_ready, 4 * i + j + 1)
                        turn(xn, j)

                def gates_out(tt):
                    pe.wait_ge(gate_added, 8 * i + 6 + 2 * tt)
                    if tt == 0:
                        pe.wait_ge(bt_lo_done, bt0[k] + 1)

                product(n0 + 16, 2, in_bt, gates_out)

                def in_attention(i2, q):
                    hi, lo = first_half if i2 else beside
                    return hi[:, q], lo[:, q]

                product(n0 + 18, 2, in_attention, lambda tt: pe.wait_ge(branch_ready, 4 * i + 2 * tt + 2),
                        lambda i2, tt: pe.wait_ge(bt_lo_done, bt0[k] + 2 + i2), None,
                        lambda i2, tt, h: turn_merged([2 * tt + h - 1]) if i2 == 1 and tt + h == 1 else None)
                turn_merged([2])

                def late_turns(i2, tt, h):
                    if (i2, tt, h) == (0, 0, 1):
                        turn_merged([3])
                    if i2 == 3:
                        turn_early(k + 1, 2 * tt + h)

                product(n0 + 20, 4, in_xt, None,
                        lambda i2, tt: pe.wait_ge(xt_lo_done, 4 * (turn0[k] + 1) + 2 * tt + i2 // 2 + 1), None, late_turns)

            def delta_ret(k):
                n0, e0 = first_piece[k], evac0[k]
                mapped = lambda name: G[name].rearrange("p (c q) -> p c q", c=4)
                kt, qt, kbt, qdt, wt, rt = (mapped(name) for name in ("kt_rt", "qt_pr", "kbt_wt", "qdt", "kbt_wt", "kt_rt"))
                vb, kbe, kd, uu = (mats(G[name]) for name in ("v_vb", "kb_kbe", "k_kd", "q_qd_u"))
                rv = mats(G["rv"])
                mm = nc.tensor.matmul

                def sum_decays():
                    pe.wait_ge(M["g_ready"], 1)
                    consts = (G["before"], G["after"], G["sub"][:, 0:P], G["sub"][:, P:2 * P])
                    for i, m in enumerate(consts):
                        ins = mm(bank[5][:, 8 * i:8 * i + 8], m, G["gates"][:, 0:8], start=True, stop=True)
                    ins.then_inc(M["sums_done"], 1)

                def channels_piece(i, half):
                    n = n0 + 2 * i + half
                    s, b0 = n % SLOTS, 2 * (i % 2)
                    pe.wait_ge(lo_done, n + 1)
                    if i == 0:
                        pe.wait_ge(xt_lo_done, 4 * turn0[k] + 3 + half)
                    for c in range(4):
                        out = psum3(b0 + c // 2, 2)[:, c % 2, :]
                        for q in range(4):
                            kt_ = 4 * half + q
                            cols = slice(q * 512 + c * P, q * 512 + (c + 1) * P)
                            args = dict(skip_group_check=True)
                            mm(out, w_hi[s][:, cols], xt_hi[:, kt_, :], start=kt_ == 0 and c % 2 == 0, stop=False, **args)
                            mm(out, w_hi[s][:, cols], xt_lo[:, kt_, :], start=False, stop=False, **args)
                            ins = mm(out, w_lo[s][:, cols], xt_hi[:, kt_, :], start=False, stop=kt_ == KT - 1, **args)
                        if (i, half, c) == (0, 0, 1):
                            product_ba()
                        if (i, half, c) == (0, 0, 2):
                            turn_ba()
                        if (i, half, c) == (0, 1, 1):
                            sum_decays()
                        if (i, half, c) == (2, 0, 1):
                            pe.wait_ge(M["e4_ready"], 1)
                            turn_channels(0)
                    ins.then_inc(used, 1)

                def turn_channels(i):
                    pe.wait_ge(M["co_ready"], i + 1)
                    for tt in range(TT):
                        for c in range(4):
                            ins = nc.tensor.transpose(bank[4 + tt][:, c * P:(c + 1) * P], co[i % 2][:, c, tt * P:(tt + 1) * P], ident[:, :])
                    ins.then_inc(M["co_turned"], 1)

                def per_tile(b0, lhs, rhs, done):
                    for tt in range(TT):
                        for h in range(4):
                            ins = mm(bank[b0 + tt][:, h * P:(h + 1) * P], lhs(tt, h), rhs(tt, h), start=True, stop=True)
                    ins.then_inc(M[done], 1)

                tile = lambda m: (lambda tt, h: m[:, h, tt * P:(tt + 1) * P])
                mat = lambda m: (lambda tt, h: m[:, tt, h, :])

                def level_a(l):
                    pe.wait_ge(M["level_masked"], l)
                    for tt in range(TT):
                        if l == 1:
                            pe.wait_ge(M["x0_ready"], 1)
                        else:
                            pe.wait_ge(M["x_updated"], TT * (l - 2) + tt + 1)
                        for h in range(4):
                            ins = mm(bank[4 + tt][:, h * P:(h + 1) * P], lev[:, tt, h, :], inv[:, tt, h, :], start=True, stop=True)
                        ins.then_inc(M["t1_done"], 1)

                def level_b(l):
                    for tt in range(TT):
                        pe.wait_ge(M["t1_ready"], TT * (l - 1) + tt + 1)
                        for h in range(4):
                            cols = slice(h * P, (h + 1) * P)
                            if l < 5:
                                mm(bank[6 + tt][:, cols], inv_t[:, tt, h, :], prod1[:, tt, h, :], start=True, stop=True)
                            ins = mm(bank[4 + tt][:, cols], prod1[:, tt, h, :], inv_t[:, tt, h, :], start=True, stop=True)
                        ins.then_inc(M["y_done"], 1)

                def retention_scores(h):
                    c, rows = h // 2, slice(64 * (h % 2), 64 * (h % 2) + 64)
                    b = bank[6 + h % 2]
                    if h >= 2:
                        pe.wait_ge(M["rs_ready"], h - 1)
                    mm(b[:, 0:SEQ], rt[rows, 2 + c, 0:P], rt[rows, c, 0:SEQ], start=True, stop=True)
                    mm(b[:, SEQ:384], rt[rows, 2 + c, P:SEQ], rt[rows, c, P:SEQ], start=True, stop=True).then_inc(M["rs_done"], 1)

                def read_out(n, what):
                    tt, lo = n // 2, 64 * (n % 2)
                    rows = slice(lo, lo + 64)
                    toks = slice(tt * P + lo, tt * P + lo + 64)
                    for h in range(4):
                        out = bank[6 + tt][rows, h * P:(h + 1) * P]
                        if what == "state":
                            ins = mm(out, qdt[:, h, toks], state[:, h, :], start=h == 0, stop=False, skip_group_check=True)
                        else:
                            vals = uu[rows, 0, h, :] if n == 0 else v_new[rows, h, :]
                            ins = mm(out, qk_m[rows, tt, h, rows], vals, start=n == 0 and h == 0, stop=True, skip_group_check=True)
                    return ins

                def old_values(n):
                    tt, lo = n // 2, 64 * (n % 2)
                    toks = slice(tt * P + lo, tt * P + lo + 64)
                    pe.wait_ge(M["s_ready"], n)
                    for h in range(4):
                        ins = mm(bank[4][lo:lo + 64, h * P:(h + 1) * P], wt[:, h, toks], state[:, h, :], start=True, stop=True)
                    ins.then_inc(M["vw_done"], 1)
                    read_out(n, "state")

                def own_values(n):
                    tt, rows = n // 2, slice(64 * (n % 2), 64 * (n % 2) + 64)
                    if n:
                        pe.wait_ge(M["vn_ready"], n)
                    if n < 3:
                        for h in range(4):
                            vals = uu[rows, 0, h, :] if n == 0 else v_new[rows, h, :]
                            ins = mm(bank[5][:, h * P:(h + 1) * P], kd[rows, tt, h, :], vals, start=True, stop=True)
                        ins.then_inc(M["ds_done"], 1)
                    read_out(n, "own").then_inc(M["o_done"], 1)

                def product_ba():
                    pe.wait_ge(M["ba_split"], 1)
                    pe.wait_ge(xt_lo_done, 4 * turn0[k] + 4)
                    for kt_ in range(KT):
                        c = slice(kt_ * 8, kt_ * 8 + 8)
                        ins = three(bank[4][0:8, 0:SEQ], ba_hi[:, c], ba_lo[:, c], xt_hi[:, kt_, :], xt_lo[:, kt_, :],
                                    kt_ == 0, kt_ == KT - 1)
                    ins.then_inc(M["ba_t_done"], 1)

                def turn_ba():
                    pe.wait_ge(M["ba_t_copied"], 1)
                    for tt in range(TT):
                        ins = nc.tensor.transpose(bank[5][:, 256 + tt * 8:264 + tt * 8], G["kt_rt"][0:8, tt * P:(tt + 1) * P],
                                                  ident[0:8, 0:8])
                    ins.then_inc(M["ba_done"], 1)

                def hook(p, tt):
                    if p == 6 and tt == 0:
                        pe.wait_ge(M["diff_ready"], 1)
                        pe.wait_ge(M["kb_ready"], 1)
                        turn_heads(tok(G["k_kd"]), 6).then_inc(M["kt_turned"], 1)
                    if p == 6 and tt == 1:
                        pe.wait_ge(M["tm_ready"], 2)
                        turn_heads(tok(G["kb_kbe"]), 4).then_inc(M["kbt_turned"], 1)
                    if p == 7 and tt == 0:
                        pe.wait_ge(M["kbt_ready"], 1)
                        turn_channels(2)
                        pe.wait_ge(M["kt_ready"], 1)
                        pe.wait_ge(M["normed"], 1)
                        turn_heads(tok(G["q_qd_u"]), 6).then_inc(M["qt_turned"], 1)
                    if p == 7 and tt == 1:
                        pe.wait_ge(M["qt_ready"], 1)
                        per_tile(6, tile(kt), tile(kbt), "at_done")
                    if p == 8 and tt == 0:
                        pe.wait_ge(M["tm_ready"], 3)
                        per_tile(4, tile(kt), tile(qt), "qk_done")
                    if p == 8 and tt == 1:
                        pe.wait_ge(M["at_ready"], 1)
                        pe.wait_ge(M["qd_ready"], 1)
                        turn_heads(tok(G["q_qd_u"]), 6).then_inc(M["qdt_turned"], 1)
                    if p == 9 and tt == 0:
                        pe.wait_ge(M["qk_masked"], 1)
                        pe.wait_ge(M["xt0_ready"], 1)
                        for t2 in range(TT):
                            for h in range(4):
                                ins = nc.tensor.transpose(bank[4 + t2][:, h * P:(h + 1) * P], inv_t[:, t2, h, :], ident[:, :])
                        ins.then_inc(M["x0_turned"], 1)
                    if p == 9 and tt == 1:
                        pe.wait_ge(M["qdt_ready"], 1)
                        level_a(1)
                        pe.wait_ge(qk_ready, rope0[k] + 1)
                        turn_heads(tok(G["rqk_ob"]), 6).then_inc(M["rqk_turned"], 1)
                    if p >= 10 and tt == 0:
                        if p == 10:
                            pe.wait_ge(M["rqk_ready"], 1)
                        if p in (11, 12):
                            pe.wait_ge(M["rs_ready"], 2 * (p - 10))
                        if p == 13:
                            pe.wait_ge(M["ro_ready"], 1)
                        level_b(p - 9)
                    if p >= 10 and tt == 1:
                        level_a(p - 8)
                        if p == 10:
                            retention_scores(0)
                            retention_scores(1)
                        if p == 11:
                            retention_scores(2)
                            retention_scores(3)
                        if p == 12:
                            pe.wait_ge(act_evac, e0 + 4)
                            for h in range(4):
                                pr, cols = retention_probs(h), slice(h * P, (h + 1) * P)
                                mm(bank[6][:, cols], pr[:, 0:P], rv[:, 0, h, :], start=True, stop=True)
                                mm(bank[7][:, cols], pr[:, P:2 * P], rv[:, 0, h, :], start=True, stop=False)
                                ins = mm(bank[7][:, cols], pr[:, 2 * P:3 * P], rv[:, 1, h, :], start=False, stop=True)
                            ins.then_inc(M["ro_done"], 1)

                for p in range(14):
                    if p < 6:
                        if p == 4:
                            pe.wait_ge(M["ct_ready"], 1)
                        channels_piece(p // 2, p % 2)
                    else:
                        if p % 2 == 0:
                            if p < 10:
                                pe.wait_ge(M["ct_ready"], p // 2 - 1)
                            else:
                                pe.wait_ge(act_evac, e0 + 2 * (p // 2 - 5) + 2)
                        chunk_piece(k, n0 + p, p // 2, p % 2, lambda tt, p=p: hook(p, tt))
                    if p == 1:
                        pe.wait_ge(M["ug_ready"], 1)
                        for tt in range(TT):
                            ins = mm(bank[6 + tt][:, :], G["ones"], G["decay_oa"][:, tt * 512:(tt + 1) * 512], start=True, stop=True)
                        ins.then_inc(M["diff_done"], 1)
                    if p == 5:
                        pe.wait_ge(M["tm_ready"], 1)
                        turn_channels(1)
                level_b(5)
                pe.wait_ge(M["half_normed"], 1)
                turn_pair(tok(G["rqk_ob"]), 0, 2)
                turn_pair(tok(G["rqk_ob"]), 2, 3)
                pe.wait_ge(M["x_updated"], 10)
                pe.wait_ge(M["vb_ready"], 1)
                pe.wait_ge(M["kbe_ready"], 1)
                per_tile(4, mat(inv_t), mat(vb), "u_done")
                for h in range(4):
                    for tt in range(TT):
                        ins = mm(psum3(6 + h // 2, 2)[:, h % 2, tt * P:(tt + 1) * P], kbe[:, tt, h, :], inv_t[:, tt, h, :], start=True, stop=True)
                ins.then_inc(M["wt_done"], 1)

                def before(tt):
                    if tt == 0:
                        pe.wait_ge(act_evac, e0 + 8)
                    else:
                        pe.wait_ge(bt_lo_done, bt0[k] + 2)

                def between(i, tt, h):
                    slot = i * 4 + tt * 2 + h
                    if slot == 0:
                        pe.wait_ge(M["wt_ready"], 1)
                        pe.wait_ge(M["kd_ready"], 1)
                        own_values(0)
                    elif slot < 7:
                        (old_values if slot % 2 else own_values)((slot + 1) // 2)
                    elif slot == 7:
                        pe.wait_ge(M["half_normed"], 3)
                        turn_pair(tok(G["decay_oa"]), 0, 4)
                    elif slot == 8:
                        turn_pair(tok(G["decay_oa"]), 2, 5)
                    if i == 3:
                        turn_early(k + 1, 2 * tt + h)

                product(n0 + 14, 4, in_heads, before, lambda i, tt: heads_ready(k, i, tt), None, between)

            def dil_diff(k):
                n0, e0, g0, r0, c0, rp = first_piece[k], evac0[k], map0[k], round0[k], turned0[k], rope0[k]
                mapped = lambda name: B[name].rearrange("p (c q) -> p c q", c=4)
                dv, cv = tok(B["dv"]), tok(B["cv"])

                def diff_scores(m):
                    scores(g0 + m, causal_map(mapped("dqt")[:, m // 2], mapped("dkt")[:, m // 2], 64 * (m % 2), 64))

                def diff_values(m):
                    values(g0 + m, m % 2, 2, [dv[:, tt, (m // 2) * P:(m // 2 + 1) * P] for tt in range(TT)], r0 + m // 2)

                def dil_scores(m):
                    scores(g0 + 8 + m, causal_map(mapped("cqt")[:, m], mapped("ckt")[:, m], 0, P))

                def dil_values(m):
                    values(g0 + 8 + m, m % 2, 2, [cv[:, tt, m * P:(m + 1) * P] for tt in range(TT)], r0 + 4 + m // 2)

                def with_tile(p, tt):
                    step = 2 * (p - 6) + tt + 1
                    if step == 0:
                        pe.wait_ge(qkt_ready, c0 + 2)
                    if 2 <= step < 10:
                        turn_probs(g0 + step - 2)
                    if 0 <= step < 8:
                        diff_scores(step)
                    if 3 <= step < 11:
                        diff_values(step - 3)
                    if (p, tt) == (11, 0):
                        pe.wait_ge(diff_normed, 2)
                        turn_pair(xn, 4, 6)
                        pe.wait_ge(qkt_ready, c0 + 3)
                        pe.wait_ge(qk_ready, rp + 3)
                        turn_heads(tok(B["ck"]), 4).then_inc(qkt_done, 1)
                    if (p, tt) == (11, 1):
                        pe.wait_ge(diff_normed, 4)
                        turn_pair(xn, 6, 7)
                        pe.wait_ge(qkt_ready, c0 + 4)
                        dil_scores(0)
                        dil_scores(1)

                for p in range(12):
                    j = p // 2
                    if p % 2 == 0 and j >= 2:
                        pe.wait_ge(act_evac, e0 + 2 * (j - 2) + 2)
                    if p == 5:
                        pe.wait_ge(qk_ready, rp + 2)
                        turn_heads(tok(B["dk"]), 6).then_inc(qkt_done, 1)
                    chunk_piece(k, n0 + p, j, p % 2, lambda tt, p=p: with_tile(p, tt))
                    if p == 3:
                        pe.wait_ge(qk_ready, rp + 1)
                        turn_heads(tok(B["dq"]), 4).then_inc(qkt_done, 1)
                    if p == 10:
                        pe.wait_ge(s_masked, g0 + 8)
                        pe.wait_ge(cq_ready, 1)
                        turn_heads(tok(B["cq"]), 4).then_inc(qkt_done, 1)

                def before(tt):
                    pe.wait_ge(act_evac, e0 + 10 + 2 * tt)

                def between(i, tt, h):
                    slot = 4 * i + 2 * tt + h
                    if slot == 1:
                        turn_probs(g0 + 8)
                    if slot == 2:
                        turn_probs(g0 + 9)
                        dil_scores(2)
                    if slot == 3:
                        pe.wait_ge(bt_lo_done, bt0[k] + 2)
                        pe.wait_ge(act_evac, e0 + 12)
                        dil_values(0)
                        dil_scores(3)
                    if slot == 4:
                        turn_probs(g0 + 10)
                        dil_values(1)
                    if slot == 5:
                        turn_probs(g0 + 11)
                    if slot == 6:
                        dil_values(2)
                        pe.wait_ge(o_ready, r0 + 5)
                        turn_pair(xn, 0, 4)
                    if slot == 7:
                        dil_values(3)
                    if slot == 8:
                        pe.wait_ge(o_ready, r0 + 6)
                        turn_pair(xn, 2, 5)
                    if i == 3:
                        turn_early(k + 1, 2 * tt + h)

                product(n0 + 12, 4, in_heads, before, lambda i, tt: heads_ready(k, i, tt), None, between)

            pe.wait_ge(id_in, 16)
            seen = {"pool_attn": 0}
            f = 0
            for k, kind in enumerate(program):
                turn_first(k)
                if kind == "ffn":
                    ffn(f, k, first_piece[k])
                    f += 1
                if kind == "pool_attn":
                    pool_attn(k, seen[kind])
                    seen[kind] += 1
                if kind == "dil_diff":
                    dil_diff(k)
                if kind == "delta_ret":
                    delta_ret(k)


def up_pieces(w, cols):
    import numpy as np
    w = w[:, cols]
    return w.reshape(-1, 4, P, 512).transpose(0, 2, 1, 3).reshape(-1, P, PIECE)


def down_pieces(w):
    return w.reshape(-1, 2, P, 1024).transpose(0, 2, 1, 3).reshape(-1, P, PIECE)


def ffn_pieces(w_up, w_down):
    import numpy as np
    ups = []
    for c in range(NCH):
        cols = np.r_[c * CH:(c + 1) * CH, DFF + c * CH:DFF + (c + 1) * CH]
        ups.append(up_pieces(w_up, cols))
    downs = down_pieces(w_down)
    order = [ups[0]]
    for c in range(1, NCH):
        order += [ups[c], downs[c - 1:c]]
    return order + [downs[NCH - 1:]]


def first_block_pieces(a, i):
    w = a["w_in"][i]
    u, q, k, v, gl = w[:, :512], w[:, 512:1024], w[:, 1024:1536], w[:, 1536:2048], w[:, 2048:]
    out = [up_pieces(m, slice(None)) for m in (u, q, k, v)]
    out += [up_pieces(gl, slice(c * 512, (c + 1) * 512)) for c in range(4)]
    return out + [down_pieces(a[name][i]) for name in ("w_branch_pool", "w_branch_attn", "w_out")]


def rope_table(width):
    import numpy as np
    half = width // 2
    inv = np.float32(1.0) / np.power(np.float32(10000.0), np.arange(half, dtype=np.float32) * np.float32(2.0 / width))
    ang = (np.arange(SEQ, dtype=np.float32)[:, None] * inv.astype(np.float32)[None, :]).astype(np.float64)
    cos, sin = np.cos(ang), np.sin(ang)
    tab = np.stack([np.concatenate([cos, cos], 1), np.concatenate([-sin, sin], 1)])
    return tab.reshape(2, TT, P, width).transpose(2, 0, 1, 3).reshape(P, -1).astype(np.float32)


def two_tiles(m):
    import numpy as np
    return np.concatenate([m[:P, :P], m[P:, :]], 1)


def pool_means():
    import numpy as np
    out = []
    for w in (2, 4, 8, 16):
        m = np.zeros((SEQ, SEQ), np.float64)
        for q in range(SEQ):
            lo = max(q + 1 - w, 0)
            m[q, lo:q + 1] = 1.0 / (q + 1 - lo)
            m[q, q] -= 1.0
        mt = m.T
        out.append(np.concatenate([mt[:P, :], mt[P:, P:]], 1))
    return np.concatenate(out, 1).astype(np.float32)


def dil_diff_pieces(w, w_out):
    out = [up_pieces(w, slice(c * 512, (c + 1) * 512)) for c in (3, 4, 5, 0, 1, 2)]
    return out + [down_pieces(w_out[512:]), down_pieces(w_out[:512])]


def delta_ret_pieces(w, w_out):
    out = [up_pieces(w, slice(c, c + 512)) for c in (512, 0, 1024, 2056, 2568, 3080, 1536)]
    return out + [down_pieces(w_out[512:]), down_pieces(w_out[:512])]


def delta_ret_constants():
    import numpy as np
    i, j = np.arange(P)[:, None], np.arange(P)[None, :]
    same = i // 64 == j // 64
    f = lambda m: np.asarray(m, np.float32)
    levels = [f((i >> (l + 1) == j >> (l + 1)) & ((i >> l) % 2 == 0) & ((j >> l) % 2 == 1)) for l in range(6)]
    gamma = 1.0 - 2.0 ** (-5.0 - np.arange(4, dtype=np.float64))
    d = np.arange(SEQ)[None, :] - np.arange(P)[:, None]
    ret = [f(np.where(d >= 0, g ** np.maximum(d, 0), 0.0)) for g in gamma]
    return {"g_ones": f(np.ones((P, P))), "g_before": f((i <= j) & same), "g_after": f((i > j) & same),
            "g_sub": np.concatenate([f((i < 64) & (j >= 0)), f((i >= 64) & (j >= 0))], 1),
            "g_below": f(np.where((i <= j) & same, 0.0, NEG)), "g_level": np.concatenate(levels, 1),
            "g_ret": np.concatenate(ret, 1), "g_rope": rope_table(64), "g_zeros": np.zeros((P, 12), np.float32)}


def constants():
    import numpy as np
    q, k = np.arange(SEQ)[:, None], np.arange(SEQ)[None, :]
    causal = two_tiles(np.where(k <= q, 0.0, NEG).astype(np.float32))
    dist = q - k
    count = ((dist >= 0) & (dist <= 128)) + 0.0 + ((dist >= 0) & (dist % 4 == 0)) + ((dist >= 0) & (dist % 16 == 0))
    log_count = two_tiles(np.where(count > 0, np.log(np.maximum(count, 1)), NEG).astype(np.float32))
    return {"b_mask": causal, "b_mask_dil": log_count, "b_rope": rope_table(64), "b_rope_wide": rope_table(128),
            "ident": np.eye(P, dtype=np.float32), "a_pool_mean": pool_means(), "a_mask": causal,
            "a_rope": rope_table(64)}


def kernel(**inputs):
    import numpy as np
    import concourse.bacc as bacc
    from concourse.bass_utils import run_bass_kernel_spmd

    a = {k: np.asarray(v) for k, v in inputs.items()}
    first = lambda i: [ffn_pieces(a["ffn1_w_gate_up"][i], a["ffn1_w_down"][i]), first_block_pieces(a, i),
                       ffn_pieces(a["ffn2_w_gate_up"][i], a["ffn2_w_down"][i])]
    second = lambda i, mixer: [ffn_pieces(a[f"l{i}_ffn1_w_up_2"], a[f"l{i}_ffn1_w_down_2"]),
                               mixer(a[f"l{i}_w_in_2"], a[f"l{i}_w_out_2"]),
                               ffn_pieces(a[f"l{i}_ffn2_w_up_2"], a[f"l{i}_ffn2_w_down_2"])]
    phases = first(0) + first(1) + second(0, delta_ret_pieces) + second(1, dil_diff_pieces)
    gains = [a[n][i] for i in range(2) for n in ("ffn1_norm", "mix_norm", "ffn2_norm")]
    gains += [a[f"l{i}_{n}_norm_2"] for i in range(2) for n in ("ffn1", "mix", "ffn2")]
    weights = np.concatenate([m for phase in phases for m in phase])
    conv = np.concatenate([a["l0_conv_w_2"][:, c:c + 512] for c in (512, 0, 1024)], 1)
    arrays = {"x": a["x"].reshape(SEQ, D), "weights": weights, 
              "gains": np.stack(gains + [a["final_norm_2"]]).reshape(-1, KT, P).transpose(2, 0, 1).reshape(P, -1),
              "final_gain": a["final_norm_2"][None, :],
              "g_gdn_norm": a["l0_gdn_norm_2"][None, :],
              "g_conv": conv.reshape(4, 12, P).transpose(2, 1, 0).reshape(P, 48),
              "g_alog_dt": np.concatenate([a["l0_a_log_2"], a["l0_dt_bias_2"]])[None, :],
              "g_ba": a["l0_w_in_2"][:, 2048:2056].reshape(KT, P, 8).transpose(1, 0, 2).reshape(P, KT * 8),
              "b_lambdas": np.concatenate([a["l1_lambda_" + n + "_2"] for n in ("q1", "k1", "q2", "k2")])[None, :],
              "b_diff_norm": a["l1_diff_norm_2"][None, :],
              "a_pool_w": a["pool_w"].transpose(0, 2, 1, 3).reshape(2, P, 512),
              "a_pool_scale": a["pool_scale"].reshape(2, 4, P).transpose(0, 2, 1),
              "a_qk_norm": np.concatenate([a["q_norm"], a["k_norm"]], 1).reshape(2, 1, 128),
              "a_b_gate": a["b_gate"].reshape(2, 1, 2048)}
    arrays.update(constants())
    arrays.update(delta_ret_constants())
    nc = bacc.Bacc("TRN2", target_bir_lowering=False, num_devices=1)
    tensors = {}
    for name in arrays:
        arrays[name] = np.ascontiguousarray(arrays[name])
        tensors[name] = nc.dram_tensor(name + "_dram", arrays[name].shape, mybir.dt.from_np(arrays[name].dtype), kind="ExternalInput").ap()
    tensors["out"] = nc.dram_tensor("out_dram", (SEQ, D), F32, kind="ExternalOutput").ap()
    build(nc, PROGRAM, tensors)
    r = run_bass_kernel_spmd(nc, [{k + "_dram": v for k, v in arrays.items()}], core_ids=[0])
    return r.results[0]["out_dram"].reshape(1, SEQ, D)
```
